# Optimizing a Trainium2 kernel written in Bass

```python
import math
import jax
import jax.numpy as jnp
from jax import lax
import numpy as np
import jax, jax.numpy as jnp

D_MODEL = 1024
BATCH = 1
SEQ = 256
DEPTH = 2

N_MIXERS = 3
D_PLE = 256
NORM_EPS = 1e-6
Q_BLOCK = 128
NEG_INF = -1e30

MLA_HEADS = 16
MLA_Q_RANK = 384
MLA_KV_RANK = 256
MLA_NOPE = 64
MLA_ROPE = 32
MLA_V = 64
ROPE_THETA = 10000.0

DIL_PATTERNS = ((128, 1), (512, 4), (2048, 16))
DIL_GROUPS = len(DIL_PATTERNS)
DIL_HEADS = 16
DIL_HEAD_DIM = 64

REL_BUCKETS = 32
REL_MAX_DIST = 2048

FOX_HEADS = 16
FOX_HEAD_DIM = 64

D_FF = -(-8 * D_MODEL // (3 * 256)) * 256


def rms_norm(x, g):
    xf = x.astype(jnp.float32)
    y = xf * lax.rsqrt(jnp.mean(xf * xf, axis=-1, keepdims=True) + NORM_EPS)
    return (y * g.astype(jnp.float32)).astype(x.dtype)

def apply_rope(x, positions):
    half = x.shape[-1] // 2
    inv = ROPE_THETA ** (-jnp.arange(half, dtype=jnp.float32) / half)
    ang = positions.astype(jnp.float32)[:, :, None, None] * inv
    cos, sin = jnp.cos(ang), jnp.sin(ang)
    xf = x.astype(jnp.float32)
    x1, x2 = xf[..., :half], xf[..., half:]
    return jnp.concatenate([x1 * cos - x2 * sin, x2 * cos + x1 * sin], axis=-1).astype(x.dtype)

def causal_block_attention(q, k, v, scale, log_forget_cumsum=None):
    s_len = q.shape[1]
    outs = []
    for b0 in range(0, s_len, Q_BLOCK):
        b1 = b0 + Q_BLOCK
        qb, kb, vb = q[:, b0:b1], k[:, :b1], v[:, :b1]
        logits = jnp.einsum('bqhd,bkhd->bhqk', qb, kb).astype(jnp.float32) * scale
        if log_forget_cumsum is not None:
            c_q = jnp.transpose(log_forget_cumsum[:, b0:b1], (0, 2, 1))
            c_k = jnp.transpose(log_forget_cumsum[:, :b1], (0, 2, 1))
            logits = logits + (c_q[..., :, None] - c_k[..., None, :])
        q_idx = b0 + jnp.arange(Q_BLOCK)
        k_idx = jnp.arange(b1)
        causal = k_idx[None, :] <= q_idx[:, None]
        logits = jnp.where(causal, logits, NEG_INF)
        probs = jax.nn.softmax(logits, axis=-1).astype(v.dtype)
        outs.append(jnp.einsum('bhqk,bkhd->bqhd', probs, vb))
    return jnp.concatenate(outs, axis=1)

def t5_bucket(dist):
    max_exact = REL_BUCKETS // 2
    n = jnp.maximum(dist.astype(jnp.float32), 1.0)
    large = max_exact + (jnp.log(n / max_exact) / math.log(REL_MAX_DIST / max_exact)
                         * (REL_BUCKETS - max_exact)).astype(jnp.int32)
    large = jnp.minimum(large, REL_BUCKETS - 1)
    return jnp.where(dist < max_exact, dist, large)

def dilated_branch(q, k, v, dilation, span, bias_table):
    b, s_len, h, dh = q.shape
    sub_len = s_len // dilation
    n_blk = -(-sub_len // Q_BLOCK)
    pad_len = n_blk * Q_BLOCK

    def to_blocks(t):
        t = t.reshape(b, sub_len, dilation, h, dh).transpose(0, 2, 1, 3, 4)
        t = t.reshape(b * dilation, sub_len, h, dh)
        t = jnp.pad(t, ((0, 0), (0, pad_len - sub_len), (0, 0), (0, 0)))
        return t.reshape(b * dilation, n_blk, Q_BLOCK, h, dh)

    def with_previous(t):
        prev = jnp.concatenate([jnp.zeros_like(t[:, :1]), t[:, :-1]], axis=1)
        return jnp.concatenate([prev, t], axis=2)

    qs = to_blocks(q)
    kb = with_previous(to_blocks(k))
    vb = with_previous(to_blocks(v))

    logits = jnp.einsum('bnqhd,bnkhd->bnhqk', qs, kb).astype(jnp.float32) * (dh ** -0.5)
    i = jnp.arange(Q_BLOCK)
    j = jnp.arange(2 * Q_BLOCK)
    rel = Q_BLOCK + i[:, None] - j[None, :]
    bucket = t5_bucket(jnp.clip(rel, 0) * dilation)
    bias = jnp.transpose(bias_table[bucket].astype(jnp.float32), (2, 0, 1))
    key_pos = jnp.arange(n_blk)[:, None] * Q_BLOCK - Q_BLOCK + j[None, :]
    valid = ((rel >= 0) & (rel <= span))[None] & (key_pos >= 0)[:, None, :]
    logits = jnp.where(valid[None, :, None], logits + bias[None, None], NEG_INF)
    lse = jax.nn.logsumexp(logits, axis=-1, keepdims=True)
    probs = jnp.exp(logits - lse).astype(v.dtype)
    o = jnp.einsum('bnhqk,bnkhd->bnqhd', probs, vb)

    o = o.reshape(b * dilation, pad_len, h, dh)[:, :sub_len]
    o = o.reshape(b, dilation, sub_len, h, dh).transpose(0, 2, 1, 3, 4).reshape(b, s_len, h, dh)
    lse = jnp.transpose(lse[..., 0], (0, 1, 3, 2)).reshape(b * dilation, pad_len, h)[:, :sub_len]
    lse = lse.reshape(b, dilation, sub_len, h).transpose(0, 2, 1, 3).reshape(b, s_len, h)
    return o, lse

def mla_mixer(h, positions, w_a, q_norm, kv_norm, w_uq, w_ukv, w_o):
    b, s_len, _ = h.shape
    a = h @ w_a
    c_q = rms_norm(a[..., :MLA_Q_RANK], q_norm)
    c_kv = rms_norm(a[..., MLA_Q_RANK:MLA_Q_RANK + MLA_KV_RANK], kv_norm)
    k_rot = apply_rope(a[..., MLA_Q_RANK + MLA_KV_RANK:][:, :, None, :], positions)
    q = (c_q @ w_uq).reshape(b, s_len, MLA_HEADS, MLA_NOPE + MLA_ROPE)
    q = jnp.concatenate([q[..., :MLA_NOPE], apply_rope(q[..., MLA_NOPE:], positions)], axis=-1)
    kv = (c_kv @ w_ukv).reshape(b, s_len, MLA_HEADS, MLA_NOPE + MLA_V)
    k = jnp.concatenate([kv[..., :MLA_NOPE],
                         jnp.broadcast_to(k_rot, (b, s_len, MLA_HEADS, MLA_ROPE))], axis=-1)
    v = kv[..., MLA_NOPE:]
    o = causal_block_attention(q, k, v, (MLA_NOPE + MLA_ROPE) ** -0.5)
    return o.reshape(b, s_len, MLA_HEADS * MLA_V) @ w_o

def dilated_mixer(h, w_qkv, w_o, rel_bias):
    b, s_len, _ = h.shape
    qkv = (h @ w_qkv).reshape(b, s_len, DIL_GROUPS, 3, DIL_HEADS, DIL_HEAD_DIM)
    table = rel_bias.reshape(REL_BUCKETS, DIL_GROUPS, DIL_HEADS)
    outs, lses = [], []
    for g, (window, dilation) in enumerate(DIL_PATTERNS):
        o, lse = dilated_branch(qkv[:, :, g, 0], qkv[:, :, g, 1], qkv[:, :, g, 2],
                                dilation, window // dilation, table[:, g])
        outs.append(o)
        lses.append(lse)
    alpha = jax.nn.softmax(jnp.stack(lses, axis=0), axis=0)
    o = jnp.sum(alpha[..., None] * jnp.stack(outs, axis=0).astype(jnp.float32), axis=0).astype(h.dtype)
    return o.reshape(b, s_len, DIL_HEADS * DIL_HEAD_DIM) @ w_o

def fox_mixer(h, w_qkvf, b_f, w_o):
    b, s_len, _ = h.shape
    inner = FOX_HEADS * FOX_HEAD_DIM
    a = h @ w_qkvf
    qkv = a[..., :3 * inner].reshape(b, s_len, 3, FOX_HEADS, FOX_HEAD_DIM)
    log_f = jax.nn.log_sigmoid((a[..., 3 * inner:] + b_f).astype(jnp.float32))
    cum = jnp.cumsum(log_f, axis=1)
    o = causal_block_attention(qkv[:, :, 0], qkv[:, :, 1], qkv[:, :, 2], FOX_HEAD_DIM ** -0.5, cum)
    return o.reshape(b, s_len, inner) @ w_o

def swiglu(h, w_in, w_out):
    gu = h @ w_in
    return (jax.nn.silu(gu[..., :D_FF]) * gu[..., D_FF:]) @ w_out

def first_inputs(seed: int = 0) -> dict:
    key = jax.random.key(seed)
    ks = jax.random.split(key, 20)
    f32 = jnp.float32
    n_a, n_b, n_c = (len(range(m, DEPTH, N_MIXERS)) for m in range(N_MIXERS))

    def dense(k, shape):
        return jax.random.normal(k, shape, f32) * shape[-2] ** -0.5

    def gain(k, shape):
        return 1.0 + 0.1 * jax.random.normal(k, shape, f32)

    x = jax.random.normal(ks[0], (BATCH, SEQ, D_MODEL), f32)
    p = jax.random.normal(ks[1], (DEPTH, BATCH, SEQ, D_PLE), f32)
    offsets = jax.random.randint(ks[2], (BATCH, 1), 0, 4096, jnp.int32)
    positions = (offsets + jnp.arange(SEQ, dtype=jnp.int32)[None, :]).astype(jnp.int32)
    norm_g = gain(ks[3], (DEPTH, 4, D_MODEL))
    ffn_w_in = dense(ks[4], (DEPTH, D_MODEL, 2 * D_FF))
    ffn_w_out = dense(ks[5], (DEPTH, D_FF, D_MODEL))
    ple_w_proj = dense(ks[6], (DEPTH, D_PLE, D_MODEL))
    ple_w_gate = dense(ks[7], (DEPTH, D_MODEL, D_MODEL))
    rel_bias = 0.5 * jax.random.normal(ks[8], (REL_BUCKETS, DIL_GROUPS * DIL_HEADS), f32)
    mla_w_a = dense(ks[9], (n_a, D_MODEL, MLA_Q_RANK + MLA_KV_RANK + MLA_ROPE))
    mla_q_norm = gain(ks[10], (n_a, MLA_Q_RANK))
    mla_kv_norm = gain(ks[11], (n_a, MLA_KV_RANK))
    mla_w_uq = dense(ks[12], (n_a, MLA_Q_RANK, MLA_HEADS * (MLA_NOPE + MLA_ROPE)))
    mla_w_ukv = dense(ks[13], (n_a, MLA_KV_RANK, MLA_HEADS * (MLA_NOPE + MLA_V)))
    mla_w_o = dense(ks[14], (n_a, MLA_HEADS * MLA_V, D_MODEL))
    dil_w_qkv = dense(ks[15], (n_b, D_MODEL, DIL_GROUPS * 3 * DIL_HEADS * DIL_HEAD_DIM))
    dil_w_o = dense(ks[16], (n_b, DIL_HEADS * DIL_HEAD_DIM, D_MODEL))
    fox_w_qkvf = dense(ks[17], (n_c, D_MODEL, 3 * FOX_HEADS * FOX_HEAD_DIM + FOX_HEADS))
    fox_b_f = jax.random.uniform(ks[18], (n_c, FOX_HEADS), f32, 1.0, 5.0)
    fox_w_o = dense(ks[19], (n_c, FOX_HEADS * FOX_HEAD_DIM, D_MODEL))
    return {'x': x, 'p': p, 'positions': positions, 'norm_g': norm_g,
            'ffn_w_in': ffn_w_in, 'ffn_w_out': ffn_w_out,
            'ple_w_proj': ple_w_proj, 'ple_w_gate': ple_w_gate, 'rel_bias': rel_bias,
            'mla_w_a': mla_w_a, 'mla_q_norm': mla_q_norm, 'mla_kv_norm': mla_kv_norm,
            'mla_w_uq': mla_w_uq, 'mla_w_ukv': mla_w_ukv, 'mla_w_o': mla_w_o,
            'dil_w_qkv': dil_w_qkv, 'dil_w_o': dil_w_o,
            'fox_w_qkvf': fox_w_qkvf, 'fox_b_f': fox_b_f, 'fox_w_o': fox_w_o}

def first_block(x, p, positions, norm_g, ffn_w_in, ffn_w_out, ple_w_proj, ple_w_gate, rel_bias,
              mla_w_a, mla_q_norm, mla_kv_norm, mla_w_uq, mla_w_ukv, mla_w_o,
              dil_w_qkv, dil_w_o, fox_w_qkvf, fox_b_f, fox_w_o):
    h = x
    for i in range(DEPTH):
        mixer, j = i % N_MIXERS, i // N_MIXERS
        g = norm_g[i]
        hn = rms_norm(h, g[0])
        if mixer == 0:
            y = mla_mixer(hn, positions, mla_w_a[j], mla_q_norm[j], mla_kv_norm[j],
                          mla_w_uq[j], mla_w_ukv[j], mla_w_o[j])
        elif mixer == 1:
            y = dilated_mixer(hn, dil_w_qkv[j], dil_w_o[j], rel_bias)
        else:
            y = fox_mixer(hn, fox_w_qkvf[j], fox_b_f[j], fox_w_o[j])
        h = h + rms_norm(y, g[1])
        h = h + rms_norm(swiglu(rms_norm(h, g[2]), ffn_w_in[i], ffn_w_out[i]), g[3])
        h = h + (p[i] @ ple_w_proj[i]) * jax.nn.sigmoid(h @ ple_w_gate[i])
    return h


HEAD_DIM = 64
N_MIX_HEADS = D_MODEL // HEAD_DIM
CONV_WIDTH = D_MODEL // 4
CONV_GROUPS = CONV_WIDTH // HEAD_DIM
RET_HEADS = (N_MIX_HEADS - CONV_GROUPS) // 2
MOBA_HEADS = N_MIX_HEADS - CONV_GROUPS - RET_HEADS
RET_WIDTH = RET_HEADS * HEAD_DIM
MOBA_WIDTH = MOBA_HEADS * HEAD_DIM
IN_COLS = 4 * RET_WIDTH + 3 * MOBA_WIDTH + 3 * CONV_WIDTH
CONV_K = 3
RET_CHUNK = 128
MOBA_BLOCK = 256
MOBA_TOPK = 3
MOBA_Q_CHUNK = 16
REL_MAX_DIST_2 = 128
ROPE_BASE = 10000.0
D_FF_2 = 256 * ((8 * D_MODEL // 3 + 255) // 256)
DN_ALPHA = (2.0 * DEPTH) ** 0.25
DN_BETA = (8.0 * DEPTH) ** -0.25
LN_EPS = 1e-5


F32 = jnp.float32

def layer_norm(x, g, b):
    xf = x.astype(F32)
    mu = jnp.mean(xf, axis=-1, keepdims=True)
    var = jnp.mean(jnp.square(xf - mu), axis=-1, keepdims=True)
    y = (xf - mu) * lax.rsqrt(var + LN_EPS)
    return (y * g.astype(F32) + b.astype(F32)).astype(x.dtype)

def causal_dwconv(x, w):
    K = w.shape[0]
    S = x.shape[1]
    xp = jnp.pad(x, ((0, 0), (K - 1, 0), (0, 0)))
    y = xp[:, 0:S] * w[0]
    for i in range(1, K):
        y = y + xp[:, i:i + S] * w[i]
    return y

def split_heads(t, n_heads):
    B, S, _ = t.shape
    return t.reshape(B, S, n_heads, HEAD_DIM).transpose(0, 2, 1, 3)

def merge_heads(t):
    B, H, S, dh = t.shape
    return t.transpose(0, 2, 1, 3).reshape(B, S, H * dh)

def rotary(t):
    S, dh = t.shape[2], t.shape[3]
    inv = ROPE_BASE ** (-jnp.arange(0, dh, 2, dtype=F32) / dh)
    ang = jnp.arange(S, dtype=F32)[:, None] * inv[None, :]
    cos, sin = jnp.cos(ang), jnp.sin(ang)
    t1, t2 = t[..., : dh // 2], t[..., dh // 2:]
    return jnp.concatenate([t1 * cos - t2 * sin, t1 * sin + t2 * cos], axis=-1)

def retention(q, k, v):
    B, H, S, dh = q.shape
    C = RET_CHUNK
    n = S // C
    log_g = jnp.log(1.0 - 2.0 ** (-5.0 - jnp.arange(H, dtype=F32)))
    idx = jnp.arange(C, dtype=F32)
    diff = idx[:, None] - idx[None, :]
    decay = jnp.where(diff >= 0, jnp.exp(jnp.maximum(diff, 0.0)[None] * log_g[:, None, None]), 0.0)
    xi = jnp.exp((idx + 1.0)[None, :] * log_g[:, None])
    zeta = jnp.exp((C - 1.0 - idx)[None, :] * log_g[:, None])
    g_chunk = jnp.exp(C * log_g)

    def to_chunks(t):
        return t.reshape(B, H, n, C, dh).transpose(2, 0, 1, 3, 4)

    def step(state, qkv):
        qc, kc, vc = qkv
        scores = jnp.einsum('bhcd,bhed->bhce', qc, kc) * decay[None]
        inner = jnp.einsum('bhce,bhev->bhcv', scores, vc)
        cross = jnp.einsum('bhcd,bhdv->bhcv', qc, state) * xi[None, :, :, None]
        state = state * g_chunk[None, :, None, None] + jnp.einsum(
            'bhcd,bhcv->bhdv', kc * zeta[None, :, :, None], vc)
        return state, inner + cross

    state0 = jnp.zeros((B, H, dh, dh), F32)
    _, out = lax.scan(step, state0, (to_chunks(q), to_chunks(k), to_chunks(v)))
    return out.transpose(1, 2, 0, 3, 4).reshape(B, H, S, dh)

def t5_bucket_2(dist):
    n = jnp.maximum(dist, 0)
    max_exact = REL_BUCKETS // 2
    nf = jnp.maximum(n, 1).astype(F32)
    large = max_exact + (jnp.log(nf / max_exact) / math.log(REL_MAX_DIST_2 / max_exact)
                         * (REL_BUCKETS - max_exact)).astype(jnp.int32)
    large = jnp.minimum(large, REL_BUCKETS - 1)
    return jnp.where(n < max_exact, n, large)

def moba_attention(q, k, v, rel_bias):
    B, H, S, dh = q.shape
    L = MOBA_BLOCK
    nb = -(-S // L)
    pad = nb * L - S
    kp = jnp.pad(k, ((0, 0), (0, 0), (0, pad), (0, 0))).reshape(B, H, nb, L, dh)
    vp = jnp.pad(v, ((0, 0), (0, 0), (0, pad), (0, 0))).reshape(B, H, nb, L, dh)
    k_mean = jnp.mean(kp, axis=3)
    topk = min(MOBA_TOPK, nb)
    scale = dh ** -0.5
    rel_t = rel_bias.T.astype(F32)
    bi = jnp.arange(B)[:, None, None, None]
    hi = jnp.arange(H)[None, :, None, None]
    Qc = MOBA_Q_CHUNK
    nc = S // Qc
    q_chunks = q.reshape(B, H, nc, Qc, dh).transpose(2, 0, 1, 3, 4)

    def attend(args):
        qi, ci = args
        q_pos = ci * Qc + jnp.arange(Qc, dtype=jnp.int32)
        own = (ci * Qc) // L
        gate = jnp.einsum('bhqd,bhnd->bhqn', qi, k_mean)
        gate = jnp.where(jnp.arange(nb) < own, gate, -jnp.inf)
        _, sel = lax.top_k(gate, topk)
        sel_valid = jnp.arange(topk) < own
        kg = kp[bi, hi, sel]
        vg = vp[bi, hi, sel]
        k_pos_sel = sel[..., None] * L + jnp.arange(L, dtype=jnp.int32)
        b_sel = rel_t[hi[..., None], t5_bucket_2(q_pos[:, None, None] - k_pos_sel)]
        s_sel = jnp.einsum('bhqd,bhqjld->bhqjl', qi, kg) * scale + b_sel
        s_sel = jnp.where(sel_valid[:, None], s_sel, -jnp.inf)
        k_own = lax.dynamic_index_in_dim(kp, own, axis=2, keepdims=False)
        v_own = lax.dynamic_index_in_dim(vp, own, axis=2, keepdims=False)
        k_pos_own = own * L + jnp.arange(L, dtype=jnp.int32)
        dist_own = q_pos[:, None] - k_pos_own[None, :]
        b_own = rel_t[:, t5_bucket_2(dist_own)]
        s_own = jnp.einsum('bhqd,bhld->bhql', qi, k_own) * scale + b_own[None]
        s_own = jnp.where(dist_own >= 0, s_own, -jnp.inf)
        logits = jnp.concatenate([s_sel.reshape(B, H, Qc, topk * L), s_own], axis=-1)
        p = jax.nn.softmax(logits, axis=-1)
        p_sel = p[..., : topk * L].reshape(B, H, Qc, topk, L)
        p_own = p[..., topk * L:]
        return (jnp.einsum('bhqjl,bhqjld->bhqd', p_sel, vg)
                + jnp.einsum('bhql,bhld->bhqd', p_own, v_own))

    out = lax.map(attend, (q_chunks, jnp.arange(nc, dtype=jnp.int32)))
    return out.transpose(1, 2, 0, 3, 4).reshape(B, H, S, dh)

def head_group_norm(t):
    mu = jnp.mean(t, axis=-1, keepdims=True)
    var = jnp.mean(jnp.square(t - mu), axis=-1, keepdims=True)
    return (t - mu) * lax.rsqrt(var + LN_EPS)

def hybrid_mixer(h, w_in, conv_w, w_out, rel_bias):
    proj = h @ w_in
    o = np.cumsum([0, RET_WIDTH, RET_WIDTH, RET_WIDTH, RET_WIDTH,
                   MOBA_WIDTH, MOBA_WIDTH, MOBA_WIDTH, CONV_WIDTH, CONV_WIDTH, CONV_WIDTH])
    parts = [proj[..., int(o[i]):int(o[i + 1])] for i in range(10)]
    rq, rk, rv, rg, mq, mk, mv, cb, cc, ch = parts
    scale = HEAD_DIM ** -0.5
    q_r = rotary(split_heads(rq, RET_HEADS).astype(F32))
    k_r = rotary(split_heads(rk, RET_HEADS).astype(F32)) * scale
    v_r = split_heads(rv, RET_HEADS).astype(F32)
    y_ret = merge_heads(head_group_norm(retention(q_r, k_r, v_r))) * jax.nn.silu(rg.astype(F32))
    y_moba = merge_heads(moba_attention(split_heads(mq, MOBA_HEADS).astype(F32),
                                        split_heads(mk, MOBA_HEADS).astype(F32),
                                        split_heads(mv, MOBA_HEADS).astype(F32), rel_bias))
    y_conv = cb.astype(F32) * causal_dwconv(cc.astype(F32) * ch.astype(F32), conv_w.astype(F32))
    cat = jnp.concatenate([y_ret, y_moba, y_conv], axis=-1).astype(h.dtype)
    return cat @ w_out

def conv_ffn(h, w_up, ffn_conv_w, w_down):
    u = h @ w_up
    a, b = u[..., :D_FF_2], u[..., D_FF_2:]
    a = causal_dwconv(a, ffn_conv_w)
    return (jax.nn.gelu(a.astype(F32), approximate=False) * b.astype(F32)).astype(h.dtype) @ w_down

def second_inputs(seed: int = 0) -> dict:
    key = jax.random.key(seed)
    ks = jax.random.split(key, 12)
    nrm = jax.random.normal
    x = nrm(ks[0], (BATCH, SEQ, D_MODEL), F32)
    w_in = nrm(ks[1], (DEPTH, D_MODEL, IN_COLS), F32) * D_MODEL ** -0.5
    conv_w = nrm(ks[2], (DEPTH, CONV_K, CONV_WIDTH), F32) * CONV_K ** -0.5
    w_out = nrm(ks[3], (DEPTH, D_MODEL, D_MODEL), F32) * (D_MODEL ** -0.5 * DN_BETA)
    ln1_g = 1.0 + 0.02 * nrm(ks[4], (DEPTH, D_MODEL), F32)
    ln1_b = 0.02 * nrm(ks[5], (DEPTH, D_MODEL), F32)
    w_up = nrm(ks[6], (DEPTH, D_MODEL, 2 * D_FF_2), F32) * D_MODEL ** -0.5
    ffn_conv_w = nrm(ks[7], (DEPTH, CONV_K, D_FF_2), F32) * CONV_K ** -0.5
    w_down = nrm(ks[8], (DEPTH, D_FF_2, D_MODEL), F32) * (D_FF_2 ** -0.5 * DN_BETA)
    ln2_g = 1.0 + 0.02 * nrm(ks[9], (DEPTH, D_MODEL), F32)
    ln2_b = 0.02 * nrm(ks[10], (DEPTH, D_MODEL), F32)
    rel_bias = 0.2 * nrm(ks[11], (REL_BUCKETS, MOBA_HEADS), F32)
    return {"x": x, "w_in": w_in, "conv_w": conv_w, "w_out": w_out,
            "ln1_g": ln1_g, "ln1_b": ln1_b, "w_up": w_up, "ffn_conv_w": ffn_conv_w,
            "w_down": w_down, "ln2_g": ln2_g, "ln2_b": ln2_b, "rel_bias": rel_bias}

def second_block(x, w_in, conv_w, w_out, ln1_g, ln1_b, w_up, ffn_conv_w, w_down, ln2_g, ln2_b, rel_bias):
    for l in range(DEPTH):
        mix = hybrid_mixer(x, w_in[l], conv_w[l], w_out[l], rel_bias)
        x = layer_norm(DN_ALPHA * x + mix, ln1_g[l], ln1_b[l])
        f = conv_ffn(x, w_up[l], ffn_conv_w[l], w_down[l])
        x = layer_norm(DN_ALPHA * x + f, ln2_g[l], ln2_b[l])
    return x


def setup_inputs(seed=0):
    out = dict(first_inputs(seed))
    for name, value in second_inputs(seed + 1).items():
        if name != "x":
            out[name + "_2"] = value
    return out


def reference(
    x, p, positions, norm_g, ffn_w_in, ffn_w_out, ple_w_proj, ple_w_gate, rel_bias, mla_w_a,
    mla_q_norm, mla_kv_norm, mla_w_uq, mla_w_ukv, mla_w_o, dil_w_qkv, dil_w_o, fox_w_qkvf,
    fox_b_f, fox_w_o, w_in_2, conv_w_2, w_out_2, ln1_g_2, ln1_b_2, w_up_2, ffn_conv_w_2,
    w_down_2, ln2_g_2, ln2_b_2, rel_bias_2,
):
    x = first_block(
        x, p, positions, norm_g, ffn_w_in, ffn_w_out, ple_w_proj, ple_w_gate, rel_bias, mla_w_a,
        mla_q_norm, mla_kv_norm, mla_w_uq, mla_w_ukv, mla_w_o, dil_w_qkv, dil_w_o, fox_w_qkvf,
        fox_b_f, fox_w_o,
    )
    return second_block(
        x, w_in_2, conv_w_2, w_out_2, ln1_g_2, ln1_b_2, w_up_2, ffn_conv_w_2, w_down_2, ln2_g_2,
        ln2_b_2, rel_bias_2,
    )


_drawn_inputs = setup_inputs


def setup_inputs(seed=0):
    import zlib

    import numpy as np

    out = dict(_drawn_inputs(seed))
    spreads = {}
    factors = {'rel_bias_2': 4.709}
    for name, (base, spread) in spreads.items():
        noise = np.random.default_rng([zlib.crc32(name.encode()), seed]).standard_normal(out[name].shape)
        drawn = base * np.exp(spread * noise) if base else spread * noise
        out[name] = jnp.asarray(drawn.astype(out[name].dtype))
    for name, factor in factors.items():
        out[name] = (out[name] * factor).astype(out[name].dtype)
    return out
```

```python
from contextlib import ExitStack, contextmanager
import math

import numpy as np
import concourse.bass as bass
from concourse import mybir

F32 = mybir.dt.float32
F32R = mybir.dt.float32r
I32 = mybir.dt.int32
ALU = mybir.AluOpType
ACT = mybir.ActivationFunctionType
AX = mybir.AxisListType

P = 128
SEQ = 256
TB = SEQ // P
D = 1024
KT = D // P
D_FF = 2816
FT = D_FF // P
BANK = 512
W = 2048
SLOTS = 3

MLA_Q, MLA_KV, NOPE, ROPE, MLA_V = 384, 256, 64, 32, 64
MLA_A = MLA_Q + MLA_KV + ROPE
MLA_HD = NOPE + ROPE
MLA_GROUP = 4
MLA_STEPS = 16 // MLA_GROUP
DIL = ((128, 1), (512, 4), (2048, 16))
NG = len(DIL)
PAIRS = 8
HD = 64
RH = 6
RW = RH * HD
BUCKETS = 32
CAUSAL_W = P + 2 * P
SPAN = 3 * P
NEG = -1e30
RMS_EPS, LN_EPS = 1e-6, 1e-5
ALPHA = 4.0 ** 0.25

MLA_WIDTHS = (3 * MLA_GROUP * MLA_HD, 2 * MLA_GROUP * NOPE, 2 * MLA_GROUP * MLA_V)
DIL_WIDTHS = (W, W, W, 3 * 384, 3 * 384, 2 * 384)
PROJ_N, FFN_OUT_N = KT // 2, FT // 2
TAIL1 = PROJ_N + FT + FFN_OUT_N + PROJ_N + 1
TAIL2 = PROJ_N + FT + FFN_OUT_N
MIX2_WIDTHS = (W,) * 9 + (3 * 384, 3 * 384, 2 * 384) + (W,) * 3
STAGES = (
    ("w_mla_a", 1, (W, W, W)),
    ("w_mla_heads", MLA_STEPS, MLA_WIDTHS),
    ("w_tail0", TAIL1 // 3, (W, W, W)),
    ("w_dil", PAIRS, DIL_WIDTHS),
    ("w_tail1", TAIL1 // 3, (W, W, W)),
    ("w_mix2", 1, MIX2_WIDTHS),
    ("w_tail2", TAIL2 // 3, (W, W, W)), ("w_tail2b", 1, (W,) * (TAIL2 % 3)),
    ("w_mix3", 1, MIX2_WIDTHS),
    ("w_tail3", TAIL2 // 3, (W, W, W)), ("w_tail3b", 1, (W,) * (TAIL2 % 3)),
)
CHUNKS = sum(n * len(ws) for _, n, ws in STAGES)
C_MLA_A = 0
C_MLA = 3
C_TAIL0 = C_MLA + MLA_STEPS * 3
C_DIL = C_TAIL0 + TAIL1
C_TAIL1 = C_DIL + PAIRS * 6
C_L2 = C_TAIL1 + TAIL1
C_L3 = C_L2 + len(MIX2_WIDTHS) + TAIL2
FIRST = (C_TAIL0, C_TAIL1, C_L2 + len(MIX2_WIDTHS), C_L3 + len(MIX2_WIDTHS))
C_WO = FIRST
C_IN = tuple(c + PROJ_N for c in FIRST)
C_OUT = tuple(c + FT for c in C_IN)
C_GATE = tuple(c + FFN_OUT_N for c in C_OUT[:2])
C_PROJ = tuple(c + PROJ_N for c in C_GATE)
C_MIX = (C_MLA_A, C_DIL, C_L2, C_L3)

TURN_TILES = (8, 5, 8, 8, 8, 8, 8, 8, 3, 8, 8, 3, 8)
(T_MLA, T_MLA_C, T_FFN0, T_PLE0, T_DIL, T_FFN1, T_PLE1,
 T_MIX2, T_RET2, T_FFN2, T_MIX3, T_RET3, T_FFN3) = range(len(TURN_TILES))
T_FFN = (T_FFN0, T_FFN1, T_FFN2, T_FFN3)
TURN_BANKS = tuple((n + 1) // 2 for n in TURN_TILES)
BANKS_BEFORE = tuple(sum(TURN_BANKS[:t]) for t in range(len(TURN_TILES)))


def build(nc, x, pT, positions, inv_freq, gain_fm, gain_rows, onehot, rel_table, rel_table_2, causal, decay,
          ret_cos, ret_sin, ffn_conv, mix_conv, identity, weights, out):
    heads_all = NG * 16 + RH
    bias_rows = nc.dram_tensor("bias_rows", [heads_all, SPAN], F32, kind="Internal").ap()
    bias_tiles = nc.dram_tensor("bias_tiles", [heads_all, P, 2 * P], F32, kind="Internal").ap()

    ctx = ExitStack()
    with ctx:
        def sb(name, shape, dt=F32, at=ctx):
            return at.enter_context(nc.sbuf_tensor(name, shape, dt))

        def sem(name):
            return ctx.enter_context(nc.semaphore(name))

        raw = sb("raw", [P, SLOTS, W])
        w_hi = sb("w_hi", [P, SLOTS, W], F32R)
        w_lo = sb("w_lo", [P, SLOTS, W], F32R)
        h = sb("h", [P, TB, D])
        t1 = sb("t1", [P, TB, D])
        xt_hi = sb("xt_hi", [P, KT, SEQ], F32R)
        xt_lo = sb("xt_lo", [P, KT, SEQ], F32R)
        ot_hi = sb("ot_hi", [P, KT, SEQ], F32R)
        ot_lo = sb("ot_lo", [P, KT, SEQ], F32R)
        p_hi = sb("p_hi", [P, 2, 2, SEQ], F32R)
        p_lo = sb("p_lo", [P, 2, 2, SEQ], F32R)
        gbuf = sb("gbuf", [P, 2, D])
        ident = sb("ident", [P, P])
        mask = sb("mask", [P, CAUSAL_W])
        gains = sb("gains", [P, len(TURN_TILES), KT])
        fconv = sb("fconv", [P, 2, FT, 3])
        mconv = sb("mconv", [P, 2, 2, 3])
        rcos = sb("rcos", [P, TB, HD // 2])
        rsin = sb("rsin", [P, TB, HD // 2])
        pos_i = sb("pos_i", [P, TB], I32)
        pos_f = sb("pos_f", [P, TB])
        inv_f = sb("inv_f", [P, ROPE // 2])
        cos_p = sb("cos_p", [P, TB, ROPE // 2])
        sin_p = sb("sin_p", [P, TB, ROPE // 2])
        stat = sb("stat", [P, TB, 2])
        bn6 = sb("bn6", [P, TB, 2, 6])
        mv = sb("mv", [P, TB, 2])
        var = sb("var", [P, 2 * RH])
        rstd = sb("rstd", [P, 2 * RH])
        newton = sb("newton", [P, 2 * RH])
        mark = sb("mark", [P, 24])
        mean12 = sb("mean12", [P, 2 * RH])
        nmax = sb("nmax", [P, 2 * RH])
        rsum = sb("rsum", [P, 2 * RH])
        rinv = sb("rinv", [P, 2 * RH])
        gate = sb("gate", [P, SLOTS, SEQ])
        conv = sb("conv", [P, SLOTS, SEQ])

        with ExitStack() as part:
            ht_hi = sb("ht_hi", [P, FT, SEQ], F32R, part)
            ht_lo = sb("ht_lo", [P, FT, SEQ], F32R, part)
        with ExitStack() as part:
            oneh = sb("oneh", [BUCKETS + 1, NG + 1, SPAN], F32, part)
            table = sb("table", [BUCKETS + 1, heads_all], F32, part)
            brow = sb("brow", [16, NG + 1, SPAN], F32, part)
            p_raw = sb("p_raw", [P, 2, 2, SEQ], F32, part)
            ang = sb("ang", [P, 3, TB, ROPE // 2], F32, part)
        with ExitStack() as part:
            a_rows = sb("a_rows", [P, TB, MLA_A], F32, part)
            a_norm = sb("a_norm", [P, TB, MLA_Q + MLA_KV], F32, part)
            k_rot = sb("k_rot", [P, TB, ROPE], F32, part)
            rtmp = sb("rtmp", [P, 4, TB, MLA_GROUP, ROPE // 2], F32, part)
            q_rows = sb("q_rows", [P, TB, MLA_GROUP, MLA_HD], F32, part)
            k_rows = sb("k_rows", [P, TB, MLA_GROUP, MLA_HD], F32, part)
            v_rows = sb("v_rows", [P, TB, MLA_GROUP, MLA_V], F32, part)
            qT = sb("qT", [MLA_HD, MLA_GROUP, SEQ], F32, part)
            kT = sb("kT", [MLA_HD, MLA_GROUP, SEQ], F32, part)
            prob0 = sb("prob0", [P, MLA_GROUP, CAUSAL_W], F32, part)
            probT0 = sb("probT0", [P, MLA_GROUP * 3, P], F32, part)
        with ExitStack() as part:
            dqk = sb("dqk", [P, 2, NG, 2, SEQ], F32, part)
            dv = sb("dv", [P, 2, TB, NG, 2, HD], F32, part)
            dbias = sb("dbias", [P, 2, 2, 3 * NG * P], F32, part)
            prob1 = sb("prob1", [P, 3 * NG * P], F32, part)
            probT1 = sb("probT1", [P, 3 * NG, P], F32, part)
        with ExitStack() as part:
            ret = sb("ret", [P, TB, 4 * RW], F32, part)
            rqk = sb("rqk", [P, RH, SEQ], F32, part)
            sc2 = sb("sc2", [P, RH, CAUSAL_W], F32, part)
            dec = sb("dec", [P, RH, CAUSAL_W], F32, part)
            mqk = sb("mqk", [P, RH // 2, 2, SEQ], F32, part)
            mvr = sb("mvr", [P, TB, RH, HD], F32, part)
            cv = sb("cv", [P, 3, 2, SEQ], F32, part)
            mbias = sb("mbias", [P, RH, CAUSAL_W], F32, part)
        probT2 = ret[:, :, :].rearrange("p b f -> p (b f)")[:, 0:3 * RH * P].rearrange("p (j q) -> p j q", q=P)

        psum = ctx.enter_context(nc.psum_tensor("psum", [P, 8, BANK], F32))
        flat = psum[:, :, :].rearrange("p b n -> p (b n)")

        landed = [sem(f"landed{s}") for s in range(SLOTS)]
        hi_split = sem("hi_split")
        lo_split = sem("lo_split")
        chunk_used = sem("chunk_used")
        const_in = sem("const_in")
        p_in = sem("p_in")
        x_in = sem("x_in")
        g_in = [sem("g0_in"), sem("g1_in")]
        bias_src_in = sem("bias_src_in")
        table_set = sem("table_set")
        bias_made = sem("bias_made")
        brow_out = sem("brow_out")
        rows_stored = sem("rows_stored")
        tiles_stored = sem("tiles_stored")
        dbias_in = [sem("dbias0_in"), sem("dbias1_in")]
        mbias_in = sem("mbias_in")
        dec_in = sem("dec_in")
        rows_ready = sem("rows_ready")
        turned = sem("turned")
        turned_hi = sem("turned_hi")
        xt_ready = sem("xt_ready")
        squared = sem("squared")
        h_ready = sem("h_ready")
        gate_ready = sem("gate_ready")
        conv_ready = sem("conv_ready")
        hidden_ready = sem("hidden_ready")
        sig_ready = sem("sig_ready")
        p_hi_ready = sem("p_hi_ready")
        p_ready = sem("p_ready")
        a_copied = sem("a_copied")
        ang_ready = sem("ang_ready")
        sincos = sem("sincos")
        heads_copied = sem("heads_copied")
        roped = sem("roped")
        qk_turned = sem("qk_turned")
        q_ready = sem("q_ready")
        k_ready = sem("k_ready")
        scored = sem("scored")
        maxed = sem("maxed")
        exped = sem("exped")
        probs_ready = sem("probs_ready")
        p_turned = sem("p_turned")
        pt_ready = sem("pt_ready")
        o_summed = sem("o_summed")
        o_hi = sem("o_hi")
        ot_ready = sem("ot_ready")
        dqk_copied = sem("dqk_copied")
        d_copied = sem("d_copied")
        d_scored = sem("d_scored")
        d_maxed = sem("d_maxed")
        d_exped = sem("d_exped")
        d_probs = sem("d_probs")
        d_turned = sem("d_turned")
        d_pt = sem("d_pt")
        d_summed = sem("d_summed")
        d_hi = sem("d_hi")
        d_ready = sem("d_ready")
        ret_copied = sem("ret_copied")
        mqk_copied = sem("mqk_copied")
        mv_copied = sem("mv_copied")
        cv_copied = sem("cv_copied")
        ret_roped = sem("ret_roped")
        ret_turned = sem("ret_turned")
        rqk_ready = sem("rqk_ready")
        ret_scored = sem("ret_scored")
        ret_decayed = sem("ret_decayed")
        ret_summed = sem("ret_summed")
        m_scored = sem("m_scored")
        m_maxed = sem("m_maxed")
        m_exped = sem("m_exped")
        m_probs = sem("m_probs")
        m_turned = sem("m_turned")
        m_pt = sem("m_pt")
        m_summed = sem("m_summed")
        m_hi = sem("m_hi")
        m_ready = sem("m_ready")
        cv_ready = sem("cv_ready")
        dve_step = sem("dve_step")
        act_step = sem("act_step")
        stored = sem("stored")

        block = ctx.enter_context(nc.Block())

        @block.sync
        def _(sp):
            sp.dma_start(h[:, :, :], x.rearrange("(b p) d -> p b d", p=P)).then_inc(x_in, 16)

            def stream(name, at, u, i, per, first):
                c = at + u
                width = STAGE_WIDTHS[name][u]
                off = sum(STAGE_WIDTHS[name][:u])
                if c >= SLOTS:
                    sp.wait_ge(lo_split, c - SLOTS + 1 + per * i)
                src = weights[name][first, :, off:off + width]
                sp.dma_start(raw[:, c % SLOTS, 0:width], src).then_inc(landed[c % SLOTS], 16)

            at = 0
            for name, n, widths in STAGES:
                per = len(widths)
                if n > 1:
                    with sp.Fori(0, n) as i:
                        for u in range(per):
                            stream(name, at, u, i, per, i)
                else:
                    for u in range(per):
                        stream(name, at, u, 0, per, 0)
                at += n * per

            sp.wait_ge(h_ready, H_READY_END)
            sp.dma_start(out.rearrange("(b p) d -> p b d", p=P), h[:, :, :]).then_inc(stored, 16)
            sp.wait_ge(stored, 16)

        @block.gpsimd
        def _(pool):
            for dst, src in ((ident[:, :], identity), (mask[:, :], causal), (gains[:, :, :], gain_fm),
                             (fconv[:, :, :, :], ffn_conv), (mconv[:, :, :, :], mix_conv),
                             (rcos[:, :, :], ret_cos), (rsin[:, :, :], ret_sin), (inv_f[:, :], inv_freq),
                             (pos_i[:, :], positions)):
                pool.dma_start(dst, src).then_inc(const_in, 16)
            pool.dma_start(p_raw[:, :, :, :], pT).then_inc(p_in, 16)
            pool.dma_start(oneh[:, :, :], onehot).then_inc(bias_src_in, 16)
            pool.wait_ge(table_set, 1)
            pool.dma_start(table[0:BUCKETS, 0:NG * 16], rel_table).then_inc(bias_src_in, 16)
            pool.dma_start(table[0:BUCKETS, NG * 16:], rel_table_2).then_inc(bias_src_in, 16)

            def lo_part(c, turn):
                s = c % SLOTS
                pool.wait_ge(hi_split, c + 1 + turn * SLOTS)
                nc.gpsimd.tensor_tensor(w_lo[:, s, :], raw[:, s, :], w_hi[:, s, :].bitcast(F32),
                                        ALU.subtract).then_inc(lo_split, 1)

            with pool.Fori(0, CHUNKS // SLOTS) as i:
                for u in range(SLOTS):
                    lo_part(u, i)
            for c in range(CHUNKS // SLOTS * SLOTS, CHUNKS):
                lo_part(c, 0)

        @block.tensor
        def _(pe):
            def mm(dst, lhsT, rhs, start, stop):
                return nc.tensor.matmul(dst, lhsT, rhs, start=start, stop=stop)

            def split_x(dst, x_hi, x_lo, hi, lo, start, stop):
                mm(dst, x_hi, hi, start, False)
                mm(dst, x_hi, lo, False, False)
                return mm(dst, x_lo, hi, False, stop)

            def split_w(dst, hi, lo, x_hi, x_lo, start, stop):
                mm(dst, hi, x_hi, start, False)
                mm(dst, hi, x_lo, False, False)
                return mm(dst, lo, x_hi, False, stop)

            def chunk(c, cols, more=0):
                pe.wait_ge(lo_split, c + 1 + more)
                s = c % SLOTS
                n = W // cols
                return (w_hi[:, s, 0:n * cols].rearrange("p (k n) -> p k n", n=cols),
                        w_lo[:, s, 0:n * cols].rearrange("p (k n) -> p k n", n=cols))

            def rows_product(c, cols, kts, lhs, banks, first, last, more=0):
                hi, lo = chunk(c, cols, more)
                for tb in range(TB):
                    tok = slice(tb * P, (tb + 1) * P)
                    for j, kt in enumerate(kts):
                        ins = split_x(banks[tb], lhs[0][:, kt, tok], lhs[1][:, kt, tok], hi[:, j, :], lo[:, j, :],
                                      first and j == 0, last and j == len(kts) - 1)
                ins.then_inc(chunk_used, 1)

            def tiles_product(c, bank, more=0):
                hi, lo = chunk(c, 2 * P, more)
                for half in range(2):
                    f = slice(half * P, (half + 1) * P)
                    for kt in range(KT):
                        ins = split_w(psum[:, bank, half * SEQ:(half + 1) * SEQ], hi[:, kt, f], lo[:, kt, f],
                                      xt_hi[:, kt, :], xt_lo[:, kt, :], kt == 0, kt == KT - 1)
                ins.then_inc(chunk_used, 1)

            def wide_product(c, n, lhs, bank0):
                for m in range(n):
                    hi, lo = chunk(c + m, D)
                    yield_ready = lhs[2]
                    if yield_ready is not None:
                        yield_ready(m)
                    for j in range(2):
                        kt = 2 * m + j
                        for tb in range(TB):
                            tok = slice(tb * P, (tb + 1) * P)
                            start, stop = kt == 0, kt == 2 * n - 1
                            a_hi, a_lo = lhs[0][:, kt, tok], lhs[1][:, kt, tok]
                            dst = [psum[:, bank0 + 2 * tb + nb, :] for nb in range(2)]
                            col = [slice(nb * BANK, (nb + 1) * BANK) for nb in range(2)]
                            for nb in range(2):
                                mm(dst[nb], a_hi, hi[:, j, col[nb]], start, False)
                            for nb in range(2):
                                mm(dst[nb], a_hi, lo[:, j, col[nb]], False, False)
                            for nb in range(2):
                                ins = mm(dst[nb], a_lo, hi[:, j, col[nb]], False, stop)
                    ins.then_inc(chunk_used, 1)

            def turn(t, src):
                pe.wait_ge(rows_ready, t + 1)
                for b in range(TURN_BANKS[t]):
                    for kt in range(2 * b, min(2 * b + 2, TURN_TILES[t])):
                        for tb in range(TB):
                            at = (kt % 2) * SEQ + tb * P
                            ins = nc.tensor.transpose(psum[:, 4 + b, at:at + P],
                                                      src[:, tb, kt * P:(kt + 1) * P], ident[:, :])
                    ins.then_inc(turned, 1)

            def turned_ready(t):
                pe.wait_ge(xt_ready, BANKS_BEFORE[t] + TURN_BANKS[t])

            xt = (xt_hi, xt_lo)

            def ffn(l):
                def pair(u, i):
                    j = u
                    if u >= SLOTS:
                        pe.wait_ge(hidden_ready, l * FT + j - SLOTS + 1 + SLOTS * i)
                    tiles_product(C_IN[l] + u, 4 + u % SLOTS, SLOTS * i)

                for u in range(SLOTS):
                    pair(u, 0)
                full = FT // SLOTS
                with pe.Fori(0, full - 1) as i:
                    for u in range(SLOTS):
                        pair(SLOTS + u, i)
                for u in range(full * SLOTS, FT):
                    pair(u, 0)
                wide_product(C_OUT[l], FFN_OUT_N,
                             (ht_hi, ht_lo, lambda m: pe.wait_ge(hidden_ready, l * FT + 2 * m + 2)), 0)

            def tail(l, mixed):
                wide_product(C_WO[l], PROJ_N, (ot_hi, ot_lo, lambda m: mixed() if m == 0 else None), 0)
                turn(T_FFN[l], t1 if l < 2 else h)
                turned_ready(T_FFN[l])
                ffn(l)

            def ple(l, t):
                turn(t, h)
                turned_ready(t)
                wide_product(C_GATE[l], PROJ_N, (xt_hi, xt_lo, None), 0)
                if l == 0:
                    pe.wait_ge(p_ready, 1)
                wide_product(C_PROJ[l], 1, (p_hi[:, l], p_lo[:, l], None), 4)

            pe.wait_ge(bias_src_in, 48)
            for g in range(NG + 1):
                n = 16 if g < NG else RH
                ins = mm(psum[0:n, g, 0:SPAN], table[:, 16 * g:16 * g + n], oneh[:, g, :], True, True)
            ins.then_inc(bias_made, 1)

            pe.wait_ge(const_in, 16 * 9)
            turn(T_MLA, t1)
            turned_ready(T_MLA)
            pe.wait_ge(brow_out, 1)
            for half in range(2):
                rows_product(half, BANK, range(4 * half, 4 * half + 4), xt,
                             [psum[:, 0, :], psum[:, 2, :]], half == 0, half == 1)
            rows_product(2, MLA_A - BANK, range(KT), xt,
                         [psum[:, 1, 0:MLA_A - BANK], psum[:, 3, 0:MLA_A - BANK]], True, True)
            turn(T_MLA_C, a_norm)
            turned_ready(T_MLA_C)
            with pe.Fori(0, MLA_STEPS) as i:
                gq = MLA_GROUP * MLA_HD
                gk = MLA_GROUP * NOPE
                rows_product(C_MLA, gq, range(3), xt, [psum[:, 0, 0:gq], psum[:, 1, 0:gq]], True, True, 3 * i)
                kv = (xt_hi[:, 3:5, :], xt_lo[:, 3:5, :])
                rows_product(C_MLA + 1, gk, range(2), kv, [psum[:, 2, 0:gk], psum[:, 2, gk:2 * gk]], True, True, 3 * i)
                rows_product(C_MLA + 2, gk, range(2), kv, [psum[:, 3, 0:gk], psum[:, 3, gk:2 * gk]], True, True, 3 * i)
                pe.wait_ge(roped, i + 1)
                for n, rows in enumerate((q_rows, k_rows)):
                    for hh in range(MLA_GROUP):
                        for tb in range(TB):
                            bank, off = 4 + 2 * n + hh // 2, (hh % 2) * SEQ + tb * P
                            ins = nc.tensor.transpose(psum[0:MLA_HD, bank, off:off + P], rows[:, tb, hh, :], ident[:, :])
                ins.then_inc(qk_turned, 1)
                pe.wait_ge(q_ready, i + 1)
                pe.wait_ge(k_ready, i + 1)
                for hh in range(MLA_GROUP):
                    mm(psum[:, hh, 0:P], qT[:, hh, 0:P], kT[:, hh, 0:P], True, True)
                    ins = mm(psum[:, hh, P:CAUSAL_W], qT[:, hh, P:SEQ], kT[:, hh, :], True, True)
                ins.then_inc(scored, 1)
                pe.wait_ge(probs_ready, i + 1)
                for hh in range(MLA_GROUP):
                    for j in range(3):
                        n = 3 * hh + j
                        ins = nc.tensor.transpose(psum[:, 4 + n // 4, (n % 4) * P:(n % 4 + 1) * P],
                                                  prob0[:, hh, j * P:(j + 1) * P], ident[:, :])
                ins.then_inc(p_turned, 1)
                pe.wait_ge(pt_ready, i + 1)
                for hh in range(MLA_GROUP):
                    rows = slice(64 * (hh % 2), 64 * (hh % 2) + 64)
                    off = (hh // 2) * SEQ
                    mm(psum[rows, 7, off:off + P], v_rows[:, 0, hh, :], probT0[:, 3 * hh, :], True, True)
                    mm(psum[rows, 7, off + P:off + SEQ], v_rows[:, 0, hh, :], probT0[:, 3 * hh + 1, :], True, False)
                    ins = mm(psum[rows, 7, off + P:off + SEQ], v_rows[:, 1, hh, :], probT0[:, 3 * hh + 2, :], False, True)
                ins.then_inc(o_summed, 1)
                pe.wait_ge(ot_ready, i + 1)
            tail(0, lambda: None)
            ple(0, T_PLE0)

            turn(T_DIL, t1)
            turned_ready(T_DIL)
            def d_tiles(u, pair0, more, first=False):
                if u == 2:
                    pe.wait_ge(dqk_copied, NG * (pair0 + more) + 1)
                elif not first:
                    pe.wait_ge(dqk_copied, NG * (pair0 + more))
                tiles_product(C_DIL + 6 * pair0 + u, u % 2, 6 * more)

            def d_values(n, pair0, more, first=False):
                if n == 0 and not first:
                    pe.wait_ge(d_copied, pair0 + more)
                kts = (range(0, 3), range(3, 6), range(6, 8))[n]
                rows_product(C_DIL + 6 * pair0 + 3 + n, 3 * P, kts, xt, [psum[:, 3, 0:3 * P], psum[:, 4, 0:3 * P]],
                             n == 0, n == 2, 6 * more)

            def d_scores(pair, par, hh):
                if hh == 0:
                    pe.wait_ge(d_copied, pair + 1)
                rows = slice(64 * hh, 64 * hh + 64)
                for g in range(NG):
                    q, k = dqk[rows, par, g, 0, :], dqk[rows, par, g, 1, :]
                    mm(psum[:, 5, g * P:(g + 1) * P], q[:, 0:P], k[:, 0:P], True, True)
                    ins = mm(flat[:, 6 * BANK + g * SEQ:6 * BANK + (g + 1) * SEQ], q[:, P:SEQ], k[:, :], True, True)
                ins.then_inc(d_scored, 1)

            def d_turn(pair, hh):
                pe.wait_ge(d_probs, 2 * pair + hh + 1)
                for j in range(3 * NG):
                    ins = nc.tensor.transpose(flat[:, 5 * BANK + j * P:5 * BANK + (j + 1) * P],
                                              prob1[:, j * P:(j + 1) * P], ident[:, :])
                ins.then_inc(d_turned, 1)

            def d_values_sum(pair, par, hh, first=False):
                pe.wait_ge(d_pt, 2 * pair + hh + 1)
                if hh == 0 and not first:
                    pe.wait_ge(d_ready, pair)
                rows = slice(64 * hh, 64 * hh + 64)
                for g in range(NG):
                    mm(psum[rows, 2, 0:P], dv[:, par, 0, g, hh, :], probT1[:, g, :], g == 0, g == NG - 1)
                for g in range(NG):
                    for kb in range(2):
                        ins = mm(psum[rows, 2, P:SEQ], dv[:, par, kb, g, hh, :], probT1[:, NG + 2 * g + kb, :],
                                 g == 0 and kb == 0, g == NG - 1 and kb == 1)
                if hh == 1:
                    ins.then_inc(d_summed, 1)

            def d_step(i0, par, more, first=False):
                pair = i0 + more
                d_scores(pair, par, 0)
                d_tiles(0, i0 + 1, more)
                d_turn(pair, 0)
                d_tiles(1, i0 + 1, more)
                d_values_sum(pair, par, 0, first)
                d_scores(pair, par, 1)
                d_tiles(2, i0 + 1, more)
                d_turn(pair, 1)
                d_values(0, i0 + 1, more)
                d_values_sum(pair, par, 1)
                d_values(1, i0 + 1, more)
                d_values(2, i0 + 1, more)

            for u in range(NG):
                d_tiles(u, 0, 0, True)
            for n in range(3):
                d_values(n, 0, 0, True)
            d_step(0, 0, 0, True)
            with pe.Fori(0, PAIRS // 2 - 1) as i:
                for u in range(2):
                    d_step(1 + u, 1 - u, 2 * i)
            last = PAIRS - 1
            for hh in range(2):
                d_scores(last, 1, hh)
                d_turn(last, hh)
                d_values_sum(last, 1, hh)
            pe.wait_ge(d_ready, PAIRS)
            tail(1, lambda: None)
            ple(1, T_PLE1)

            for l in (2, 3):
                n = l - 2
                c = C_MIX[l]
                turn((T_MIX2, T_MIX3)[n], h)
                turned_ready((T_MIX2, T_MIX3)[n])
                for b in range(3):
                    if b == 2:
                        pe.wait_ge(ret_copied, 3 * n + 1)
                    for half in range(2):
                        rows_product(c + 2 * b + half, BANK, range(4 * half, 4 * half + 4), xt,
                                     [psum[:, 2 * (b % 2) + tb, :] for tb in range(TB)], half == 0, half == 1)
                for b in range(3):
                    tiles_product(c + 6 + b, 4 + b)
                pe.wait_ge(ret_copied, 3 * n + 2)
                for b, kts in enumerate((range(0, 3), range(3, 6), range(6, 8))):
                    rows_product(c + 9 + b, RW, kts, xt, [psum[:, 2, 0:RW], psum[:, 3, 0:RW]], b == 0, b == 2)
                pe.wait_ge(mqk_copied, n + 1)
                for b in range(3):
                    tiles_product(c + 12 + b, 4 + b)

                pe.wait_ge(ret_roped, n + 1)
                pe.wait_ge(ret_copied, 3 * n + 3)
                pe.wait_ge(mv_copied, n + 1)
                for f in range(RH):
                    for tb in range(TB):
                        off = f * SEQ + tb * P
                        ins = nc.tensor.transpose(flat[:, off:off + P], ret[:, tb, f * P:(f + 1) * P], ident[:, :])
                ins.then_inc(ret_turned, 1)
                pe.wait_ge(rqk_ready, n + 1)
                pe.wait_ge(cv_copied, n + 1)
                for hh in range(RH):
                    rows = slice(64 * (hh % 2), 64 * (hh % 2) + 64)
                    q, k = rqk[rows, hh // 2, :], rqk[rows, 3 + hh // 2, :]
                    mm(psum[:, 2 + hh, 0:SEQ], k[:, 0:P], q, True, True)
                    ins = mm(psum[:, 2 + hh, SEQ:CAUSAL_W], k[:, P:SEQ], q[:, P:SEQ], True, True)
                ins.then_inc(ret_scored, 1)
                pe.wait_ge(ret_decayed, n + 1)
                for hh in range(RH):
                    o = slice(hh * HD, (hh + 1) * HD)
                    v = [ret[:, tb, 2 * RW + hh * HD:2 * RW + (hh + 1) * HD] for tb in range(TB)]
                    mm(psum[:, 0, o], sc2[:, hh, 0:P], v[0], True, True)
                    mm(psum[:, 1, o], sc2[:, hh, P:SEQ], v[0], True, False)
                    ins = mm(psum[:, 1, o], sc2[:, hh, SEQ:CAUSAL_W], v[1], False, True)
                ins.then_inc(ret_summed, 1)

                for hh in range(RH):
                    rows = slice(64 * (hh % 2), 64 * (hh % 2) + 64)
                    q, k = mqk[rows, hh // 2, 0, :], mqk[rows, hh // 2, 1, :]
                    mm(psum[:, 2 + hh, 0:P], q[:, 0:P], k[:, 0:P], True, True)
                    ins = mm(psum[:, 2 + hh, P:CAUSAL_W], q[:, P:SEQ], k, True, True)
                ins.then_inc(m_scored, 1)
                pe.wait_ge(m_probs, n + 1)
                for j in range(3 * RH):
                    ins = nc.tensor.transpose(flat[:, 2 * BANK + j * P:2 * BANK + (j + 1) * P],
                                              sc2[:, j // 3, (j % 3) * P:(j % 3 + 1) * P], ident[:, :])
                ins.then_inc(m_turned, 1)
                pe.wait_ge(m_pt, n + 1)
                for hh in range(RH):
                    rows = slice(64 * (hh % 2), 64 * (hh % 2) + 64)
                    off = (hh // 2) * SEQ
                    mm(flat[rows, off:off + P], mvr[:, 0, hh, :], probT2[:, 3 * hh, :], True, True)
                    mm(flat[rows, off + P:off + SEQ], mvr[:, 0, hh, :], probT2[:, 3 * hh + 1, :], True, False)
                    ins = mm(flat[rows, off + P:off + SEQ], mvr[:, 1, hh, :], probT2[:, 3 * hh + 2, :], False, True)
                ins.then_inc(m_summed, 1)
                t = (T_RET2, T_RET3)[n]
                turn(t, t1)

                def mixed(n=n, t=t):
                    turned_ready(t)
                    pe.wait_ge(m_ready, n + 1)
                    pe.wait_ge(cv_ready, n + 1)
                tail(l, mixed)

        @block.scalar
        def _(act):
            def hi_part(c, more=0, turns=0):
                s = c % SLOTS
                act.wait_ge(landed[s], 16 * (c // SLOTS + 1) + 16 * turns)
                if c >= SLOTS:
                    act.wait_ge(chunk_used, c - SLOTS + 1 + more)
                nc.scalar.activation(w_hi[:, s, :], raw[:, s, :], ACT.Copy).then_inc(hi_split, 1)

            def ahead(c, more=0, turns=0):
                if c + 2 < CHUNKS:
                    hi_part(c + 2, more, turns)

            def turn_hi(t, dst):
                for b in range(TURN_BANKS[t]):
                    act.wait_ge(turned, BANKS_BEFORE[t] + b + 1)
                    for kt in range(2 * b, min(2 * b + 2, TURN_TILES[t])):
                        ins = nc.scalar.activation(dst[:, kt, :], psum[:, 4 + b, (kt % 2) * SEQ:(kt % 2 + 1) * SEQ],
                                                   ACT.Copy, scale=gains[:, t, kt:kt + 1])
                    ins.then_inc(turned_hi, 1)

            def squares_y(c):
                act.wait_ge(chunk_used, c + 1)
                for tb in range(TB):
                    for nb in range(2):
                        ins = nc.scalar.activation(t1[:, tb, nb * BANK:(nb + 1) * BANK], psum[:, 2 * tb + nb, :],
                                                   ACT.Square, accum_out=stat[:, tb, nb:nb + 1])
                ins.then_inc(squared, 1)

            def squares_h(ready):
                act.wait_ge(h_ready, ready)
                for tb in range(TB):
                    ins = nc.scalar.activation(t1[:, tb, :], h[:, tb, :], ACT.Square, accum_out=stat[:, tb, 0:1])
                ins.then_inc(squared, 1)

            def load_gain(row, slot):
                act.dma_start(gbuf[:, slot, :], gain_rows[row:row + 1, :].to_broadcast([P, D])).then_inc(g_in[slot], 16)

            def ffn(l):
                func = ACT.Silu if l < 2 else ACT.Gelu

                def tile(u, i):
                    ahead(C_IN[l] + u, SLOTS * i, i)
                    if l < 2:
                        act.wait_ge(chunk_used, C_IN[l] + u + 1 + SLOTS * i)
                        src = psum[:, 4 + u % SLOTS, 0:SEQ]
                    else:
                        act.wait_ge(conv_ready, (l - 2) * FT + u + 1 + SLOTS * i)
                        src = conv[:, u % SLOTS, :]
                    nc.scalar.activation(gate[:, u % SLOTS, :], src, func).then_inc(gate_ready, 1)

                full = FT // SLOTS
                with act.Fori(0, full) as i:
                    for u in range(SLOTS):
                        tile(u, i)
                for u in range(full * SLOTS, FT):
                    tile(u, 0)
                for m in range(FFN_OUT_N):
                    ahead(C_OUT[l] + m)

            def ple(l, t):
                turn_hi(t, xt_hi)
                for m in range(PROJ_N + 1):
                    ahead(C_GATE[l] + m)
                act.wait_ge(chunk_used, C_PROJ[l])
                for tb in range(TB):
                    for nb in range(2):
                        ins = nc.scalar.activation(t1[:, tb, nb * BANK:(nb + 1) * BANK], psum[:, 2 * tb + nb, :],
                                                   ACT.Sigmoid)
                ins.then_inc(sig_ready, 1)

            load_gain(0, 0)
            load_gain(1, 1)
            hi_part(0)
            hi_part(1)
            squares_h(1)
            act.wait_ge(bias_made, 1)
            for g in range(NG + 1):
                n = 16 if g < NG else RH
                ins = nc.scalar.activation(brow[0:n, g, :], psum[0:n, g, 0:SPAN], ACT.Copy)
            ins.then_inc(brow_out, 1)
            act.wait_ge(brow_out, 1)
            for g in range(NG + 1):
                n = 16 if g < NG else RH
                act.dma_start(bias_rows[16 * g:16 * g + n, :], brow[0:n, g, :]).then_inc(rows_stored, 16)
            act.wait_ge(p_in, 16)
            nc.scalar.activation(p_hi[:, :, :, :], p_raw[:, :, :, :], ACT.Copy).then_inc(p_hi_ready, 1)
            act.wait_ge(ang_ready, 1)
            nc.scalar.activation(sin_p[:, :, :], ang[:, 0], ACT.Sin)
            nc.scalar.activation(cos_p[:, :, :], ang[:, 1], ACT.Sin).then_inc(sincos, 1)
            act.wait_ge(rows_stored, 16 * (NG + 1))
            toeplitz = bass.AP(tensor=bias_rows.tensor, offset=P - 1, ap=[[SPAN, heads_all], [-1, P], [1, 2 * P]])
            act.dma_start(bias_tiles, toeplitz).then_inc(tiles_stored, 16)

            act.wait_ge(const_in, 16 * 9)
            turn_hi(T_MLA, xt_hi)
            for c in range(3):
                ahead(c)
            act.wait_ge(chunk_used, 3)
            act.wait_ge(p_ready, 1)
            for tb in range(TB):
                ins = nc.scalar.activation(a_rows[:, tb, :], flat[:, 2 * tb * BANK:2 * tb * BANK + MLA_A], ACT.Copy)
            ins.then_inc(act_step, 1)
            act.wait_ge(act_step, 1)
            for tb in range(TB):
                nc.scalar.activation(t1[:, tb, 0:MLA_Q], a_rows[:, tb, 0:MLA_Q], ACT.Square, accum_out=stat[:, tb, 0:1])
                ins = nc.scalar.activation(t1[:, tb, MLA_Q:MLA_Q + MLA_KV], a_rows[:, tb, MLA_Q:MLA_Q + MLA_KV],
                                           ACT.Square, accum_out=stat[:, tb, 1:2])
            ins.then_inc(squared, 1)
            turn_hi(T_MLA_C, xt_hi)
            with act.Fori(0, MLA_STEPS) as i:
                gq, gk = MLA_GROUP * MLA_HD, MLA_GROUP * NOPE
                ahead(C_MLA, 3 * i, i)
                act.wait_ge(chunk_used, C_MLA + 1 + 3 * i)
                nc.scalar.activation(q_rows[:, :, :, :].rearrange("p b h d -> p b (h d)"), psum[:, 0:2, 0:gq], ACT.Copy)
                ahead(C_MLA + 1, 3 * i, i)
                act.wait_ge(chunk_used, C_MLA + 2 + 3 * i)
                nc.scalar.activation(k_rows[:, :, :, 0:NOPE],
                                     psum[:, 2, :].rearrange("p (b h d) -> p b h d", b=TB, d=NOPE), ACT.Copy)
                ahead(C_MLA + 2, 3 * i, i)
                act.wait_ge(chunk_used, C_MLA + 3 + 3 * i)
                nc.scalar.activation(v_rows[:, :, :, :],
                                     psum[:, 3, :].rearrange("p (b h d) -> p b h d", b=TB, d=MLA_V), ACT.Copy).then_inc(heads_copied, 1)
                act.wait_ge(qk_turned, i + 1)
                nc.scalar.activation(qT[:, :, :].rearrange("p h t -> p (h t)"), flat[0:MLA_HD, 4 * BANK:6 * BANK],
                                     ACT.Copy).then_inc(q_ready, 1)
                act.wait_ge(maxed, i + 1)
                for hh in range(MLA_GROUP):
                    for qb, part in enumerate((slice(0, P), slice(P, CAUSAL_W))):
                        m = qb * MLA_GROUP + hh
                        ins = nc.scalar.activation(prob0[:, hh, part], prob0[:, hh, part], ACT.Exp,
                                                   bias=nmax[:, m:m + 1], accum_out=rsum[:, m:m + 1])
                ins.then_inc(exped, 1)
                act.wait_ge(p_turned, i + 1)
                nc.scalar.activation(probT0[:, :, :].rearrange("p j q -> p (j q)"), flat[:, 4 * BANK:7 * BANK],
                                     ACT.Copy).then_inc(pt_ready, 1)
                act.wait_ge(o_summed, i + 1)
                nc.scalar.activation(ot_hi[:, bass.ds(2 * i, 2), :].rearrange("p j t -> p (j t)"), psum[:, 7, :],
                                     ACT.Copy).then_inc(o_hi, 1)
            for m in range(PROJ_N):
                ahead(C_WO[0] + m)
            squares_y(C_WO[0] + PROJ_N - 1)
            squares_h(2)
            turn_hi(T_FFN0, xt_hi)
            load_gain(2, 0)
            ffn(0)
            squares_y(C_OUT[0] + FFN_OUT_N - 1)
            ple(0, T_PLE0)
            load_gain(3, 1)
            squares_h(4)

            turn_hi(T_DIL, xt_hi)

            def load_dbias(pair, slot):
                of_head = bias_tiles[0:NG * 16, :, :].rearrange("(g r) q k -> r q g k", g=NG)
                for hh in range(2):
                    src = of_head[pair * 2 + hh]
                    act.dma_start(dbias[:, slot, hh, 0:3 * P].rearrange("p (g k) -> p g k", g=NG),
                                  src[:, :, P:]).then_inc(dbias_in[slot], 16)
                    act.dma_start(dbias[:, slot, hh, 3 * P:].rearrange("p (g k) -> p g k", g=NG),
                                  src).then_inc(dbias_in[slot], 16)

            def d_chunk(u, pair0, more, turns):
                ahead(C_DIL + 6 * pair0 + u, 6 * more, turns)

            def d_copy(u, par, pair0, more):
                act.wait_ge(chunk_used, C_DIL + 6 * pair0 + u + 1 + 6 * more)
                if u < NG:
                    nc.scalar.activation(dqk[:, par, u].rearrange("p a t -> p (a t)"), psum[:, u % 2, :],
                                         ACT.Copy).then_inc(dqk_copied, 1)
                else:
                    nc.scalar.activation(dv[:, par].rearrange("p b g h d -> p b (g h d)"), psum[:, 3:5, 0:3 * P],
                                         ACT.Copy).then_inc(d_copied, 1)

            def d_exp(pair, hh):
                act.wait_ge(d_maxed, 2 * pair + hh + 1)
                for qb, part in enumerate((slice(0, 3 * P), slice(3 * P, 9 * P))):
                    ins = nc.scalar.activation(prob1[:, part], prob1[:, part], ACT.Exp, bias=nmax[:, qb:qb + 1],
                                               accum_out=rsum[:, qb:qb + 1])
                ins.then_inc(d_exped, 1)

            def d_pcopy(pair, hh):
                act.wait_ge(d_turned, 2 * pair + hh + 1)
                nc.scalar.activation(probT1[:, :, :].rearrange("p j q -> p (j q)"),
                                     flat[:, 5 * BANK:5 * BANK + 9 * P], ACT.Copy).then_inc(d_pt, 1)

            def d_out(pair):
                act.wait_ge(d_summed, pair + 1)
                nc.scalar.activation(ot_hi[:, bass.ds(pair, 1), :].rearrange("p j t -> p (j t)"), psum[:, 2, 0:SEQ],
                                     ACT.Copy).then_inc(d_hi, 1)

            def d_step(i0, par, more, turns):
                pair, nxt = i0 + more, i0 + 1
                load_dbias(pair + 1, 1 - par)
                d_chunk(0, nxt, more, turns)
                d_exp(pair, 0)
                d_copy(0, 1 - par, nxt, more)
                d_chunk(1, nxt, more, turns)
                d_pcopy(pair, 0)
                d_copy(1, 1 - par, nxt, more)
                d_chunk(2, nxt, more, turns)
                d_exp(pair, 1)
                d_copy(2, 1 - par, nxt, more)
                d_chunk(3, nxt, more, turns)
                d_pcopy(pair, 1)
                d_chunk(4, nxt, more, turns)
                d_out(pair)
                d_chunk(5, nxt, more, turns)
                d_copy(5, 1 - par, nxt, more)

            act.wait_ge(tiles_stored, 16)
            load_dbias(0, 0)
            for u in range(6):
                d_chunk(u, 0, 0, 0)
                if u < NG or u == 5:
                    d_copy(u, 0, 0, 0)
            d_step(0, 0, 0, 0)
            with act.Fori(0, PAIRS // 2 - 1) as i:
                for u in range(2):
                    d_step(1 + u, 1 - u, 2 * i, 4 * i)
            last = PAIRS - 1
            for hh in range(2):
                d_exp(last, hh)
                d_pcopy(last, hh)
            d_out(last)
            for m in range(PROJ_N):
                ahead(C_WO[1] + m)
            squares_y(C_WO[1] + PROJ_N - 1)
            squares_h(5)
            turn_hi(T_FFN1, xt_hi)
            load_gain(4, 0)
            ffn(1)
            squares_y(C_OUT[1] + FFN_OUT_N - 1)
            ple(1, T_PLE1)
            load_gain(5, 1)

            for l in (2, 3):
                n = l - 2
                c = C_MIX[l]
                act.wait_ge(h_ready, (7, 9)[n])
                m_src = bias_tiles[NG * 16:, :, :].rearrange("h q k -> q h k")
                act.dma_start(mbias[:, :, 0:P], m_src[:, :, P:2 * P]).then_inc(mbias_in, 16)
                act.dma_start(mbias[:, :, P:], m_src).then_inc(mbias_in, 16)
                act.dma_start(dec[:, :, :], decay).then_inc(dec_in, 16)
                turn_hi((T_MIX2, T_MIX3)[n], xt_hi)
                if n == 1:
                    load_gain(8, 0)
                    load_gain(9, 1)
                for b in range(3):
                    ahead(c + 2 * b)
                    ahead(c + 2 * b + 1)
                    act.wait_ge(chunk_used, c + 2 * b + 2)
                    src = psum[:, 2 * (b % 2):2 * (b % 2) + 2, :]
                    if b < 2:
                        ins = nc.scalar.activation(ret[:, :, b * BANK:(b + 1) * BANK], src, ACT.Copy)
                    else:
                        nc.scalar.activation(ret[:, :, 2 * BANK:3 * RW], src[:, :, 0:3 * RW - 2 * BANK], ACT.Copy)
                        ins = nc.scalar.activation(ret[:, :, 3 * RW:], src[:, :, 3 * RW - 2 * BANK:], ACT.Silu)
                    ins.then_inc(ret_copied, 1)
                for b in range(3):
                    ahead(c + 6 + b)
                    act.wait_ge(chunk_used, c + 7 + b)
                    ins = nc.scalar.activation(mqk[:, b].rearrange("p a t -> p (a t)"), psum[:, 4 + b, :], ACT.Copy)
                ins.then_inc(mqk_copied, 1)
                for b in range(3):
                    ahead(c + 9 + b)
                act.wait_ge(chunk_used, c + 12)
                nc.scalar.activation(mvr[:, :, :, :].rearrange("p b h d -> p b (h d)"), psum[:, 2:4, 0:RW],
                                     ACT.Copy).then_inc(mv_copied, 1)
                for b in range(3):
                    ahead(c + 12 + b)
                    act.wait_ge(chunk_used, c + 13 + b)
                    ins = nc.scalar.activation(cv[:, b].rearrange("p f t -> p (f t)"), psum[:, 4 + b, :], ACT.Copy)
                ins.then_inc(cv_copied, 1)
                act.wait_ge(ret_turned, n + 1)
                nc.scalar.activation(rqk[:, :, :].rearrange("p f t -> p (f t)"), flat[:, 0:RH * SEQ],
                                     ACT.Copy).then_inc(rqk_ready, 1)
                act.wait_ge(m_maxed, n + 1)
                for hh in range(RH):
                    for qb, part in enumerate((slice(0, P), slice(P, CAUSAL_W))):
                        m = qb * RH + hh
                        ins = nc.scalar.activation(sc2[:, hh, part], sc2[:, hh, part], ACT.Exp,
                                                   bias=nmax[:, m:m + 1], accum_out=rsum[:, m:m + 1])
                ins.then_inc(m_exped, 1)
                act.wait_ge(m_turned, n + 1)
                nc.scalar.activation(probT2.rearrange("p j q -> p (j q)"), flat[:, 2 * BANK:2 * BANK + 3 * RH * P],
                                     ACT.Copy).then_inc(m_pt, 1)
                act.wait_ge(m_summed, n + 1)
                nc.scalar.activation(ot_hi[:, 3:6, :].rearrange("p j t -> p (j t)"), flat[:, 0:3 * SEQ],
                                     ACT.Copy).then_inc(m_hi, 1)
                turn_hi((T_RET2, T_RET3)[n], ot_hi)
                for m in range(PROJ_N):
                    ahead(C_WO[l] + m)
                turn_hi(T_FFN[l], xt_hi)
                load_gain(4 + 4 * n + 2, 0)
                load_gain(4 + 4 * n + 3, 1)
                ffn(l)

        @block.vector
        def _(dve):
            v = nc.vector
            steps = [0, None, 0]

            def step(ins):
                steps[0] += 1
                ins.then_inc(dve_step, 1)
                dve.wait_ge(dve_step, steps[0] if steps[1] is None else steps[0] + steps[1] * steps[2])

            @contextmanager
            def loop(n, per):
                begin = steps[0]
                with dve.Fori(0, n) as i:
                    steps[1:] = [i, per]
                    yield i
                assert steps[0] - begin == per, (steps[0] - begin, per)
                steps[0] = begin + per * n
                steps[1:] = [None, 0]

            def rsqrt(n):
                a, y, w = var[:, 0:n], rstd[:, 0:n], newton[:, 0:n]
                step(v.tensor_scalar(w.bitcast(I32), a.bitcast(I32), 1, None, ALU.logical_shift_right))
                step(v.tensor_scalar(y.bitcast(I32), w.bitcast(I32), -1, 0x5F3759DF, ALU.mult, ALU.add))
                for _ in range(4):
                    step(v.tensor_tensor(w, y, y, ALU.mult))
                    step(v.scalar_tensor_tensor(w, w, -0.5, a, ALU.mult, ALU.mult))
                    step(v.scalar_tensor_tensor(y, w, 1.5, y, ALU.add, ALU.mult))

            squares = [0]

            def sums_ready():
                squares[0] += 1
                dve.wait_ge(squared, squares[0])

            def rms_rows():
                sums_ready()
                step(v.tensor_scalar(var[:, 0:TB], stat[:, :, 0], 1.0 / D, RMS_EPS, ALU.mult, ALU.add))
                rsqrt(TB)
                for tb in range(TB):
                    ins = v.tensor_scalar(t1[:, tb, :], h[:, tb, :], rstd[:, tb:tb + 1], None, ALU.mult)
                ins.then_inc(rows_ready, 1)

            def add_rms_y(slot, load):
                sums_ready()
                step(v.tensor_tensor(var[:, 0:TB], stat[:, :, 0], stat[:, :, 1], ALU.add))
                step(v.tensor_scalar(var[:, 0:TB], var[:, 0:TB], 1.0 / D, RMS_EPS, ALU.mult, ALU.add))
                rsqrt(TB)
                dve.wait_ge(g_in[slot], 16 * load)
                for tb in range(TB):
                    for nb in range(2):
                        col = slice(nb * BANK, (nb + 1) * BANK)
                        step(v.scalar_tensor_tensor(t1[:, tb, col], psum[:, 2 * tb + nb, :], rstd[:, tb:tb + 1],
                                                    gbuf[:, slot, col], ALU.mult, ALU.mult))
                step(v.tensor_tensor(h[:, :, :], h[:, :, :], t1[:, :, :], ALU.add))

            marks = [0]

            def signal(ready):
                m = marks[0]
                marks[0] += 1
                v.tensor_copy(mark[:, m:m + 1], h[:, 0, 0:1]).then_inc(ready, 1)

            def h_done():
                signal(h_ready)

            def turn_lo(t, hi, lo):
                for b in range(TURN_BANKS[t]):
                    dve.wait_ge(turned_hi, BANKS_BEFORE[t] + b + 1)
                    for kt in range(2 * b, min(2 * b + 2, TURN_TILES[t])):
                        ins = v.scalar_tensor_tensor(lo[:, kt, :], psum[:, 4 + b, (kt % 2) * SEQ:(kt % 2 + 1) * SEQ],
                                                     gains[:, t, kt:kt + 1], hi[:, kt, :].bitcast(F32),
                                                     ALU.mult, ALU.subtract)
                    ins.then_inc(xt_ready, 1)

            def ffn(l):
                def tile(u, i):
                    bank = psum[:, 4 + u % SLOTS, :]
                    j = u if i is None else u + SLOTS * i
                    if l >= 2:
                        cw = [fconv[:, l - 2, j, k:k + 1] if i is None else fconv[:, l - 2, bass.ds(j, 1), k:k + 1].rearrange("p a k -> p (a k)")
                              for k in range(3)]
                        s = conv[:, u % SLOTS, :]
                        dve.wait_ge(chunk_used, C_IN[l] + j + 1)
                        step(v.tensor_scalar(s, bank[:, 0:SEQ], cw[2], None, ALU.mult))
                        step(v.scalar_tensor_tensor(s[:, 1:], bank[:, 0:SEQ - 1], cw[1], s[:, 1:], ALU.mult, ALU.add))
                        v.scalar_tensor_tensor(s[:, 2:], bank[:, 0:SEQ - 2], cw[0], s[:, 2:], ALU.mult,
                                               ALU.add).then_inc(conv_ready, 1)
                    dve.wait_ge(gate_ready, l * FT + j + 1)
                    hi = ht_hi[:, j, :] if i is None else ht_hi[:, bass.ds(j, 1), :].rearrange("p a t -> p (a t)")
                    lo = ht_lo[:, j, :] if i is None else ht_lo[:, bass.ds(j, 1), :].rearrange("p a t -> p (a t)")
                    hid = conv[:, u % SLOTS, :]
                    step(v.tensor_tensor(hid, gate[:, u % SLOTS, :], bank[:, SEQ:2 * SEQ], ALU.mult))
                    step(v.tensor_copy(hi, hid))
                    v.tensor_tensor(lo, hid, hi.bitcast(F32), ALU.subtract).then_inc(hidden_ready, 1)

                full = FT // SLOTS
                with loop(full, SLOTS * (2 if l < 2 else 4)) as i:
                    for u in range(SLOTS):
                        tile(u, i)
                for u in range(full * SLOTS, FT):
                    tile(u, None)

            def ple(l, t):
                turn_lo(t, xt_hi, xt_lo)
                dve.wait_ge(sig_ready, l + 1)
                dve.wait_ge(chunk_used, C_PROJ[l] + 1)
                for tb in range(TB):
                    step(v.tensor_tensor(t1[:, tb, :], t1[:, tb, :], flat[:, (4 + 2 * tb) * BANK:(6 + 2 * tb) * BANK], ALU.mult))
                step(v.tensor_tensor(h[:, :, :], h[:, :, :], t1[:, :, :], ALU.add))
                h_done()

            def layer_norm_y(c, load):
                dve.wait_ge(chunk_used, c + 1)
                for tb in range(TB):
                    step(v.scalar_tensor_tensor(t1[:, tb, :], h[:, tb, :], ALPHA,
                                                flat[:, 2 * tb * BANK:(2 * tb + 2) * BANK], ALU.mult, ALU.add))
                    for nb in range(2):
                        step(v.bn_stats(bn6[:, tb, nb, :], t1[:, tb, nb * BANK:(nb + 1) * BANK]))
                    step(v.bn_aggr(mv[:, tb, :], bn6[:, tb, :, :]))
                step(v.tensor_scalar(var[:, 0:TB], mv[:, :, 1], LN_EPS, None, ALU.add))
                rsqrt(TB)
                for tb in range(TB):
                    step(v.tensor_scalar(t1[:, tb, :], t1[:, tb, :], mv[:, tb, 0:1], rstd[:, tb:tb + 1],
                                         ALU.subtract, ALU.mult))
                for slot in range(2):
                    dve.wait_ge(g_in[slot], 16 * load)
                for tb in range(TB):
                    step(v.tensor_tensor(t1[:, tb, :], t1[:, tb, :], gbuf[:, 0, :], ALU.mult))
                    step(v.tensor_tensor(h[:, tb, :], t1[:, tb, :], gbuf[:, 1, :], ALU.add))

            def rotate(x1, x2, cos, sin, tmp):
                step(v.tensor_tensor(tmp[0], x1, cos, ALU.mult))
                step(v.tensor_tensor(tmp[1], x2, sin, ALU.mult))
                step(v.tensor_tensor(tmp[2], x2, cos, ALU.mult))
                step(v.tensor_tensor(tmp[3], x1, sin, ALU.mult))
                step(v.tensor_tensor(x1, tmp[0], tmp[1], ALU.subtract))
                return v.tensor_tensor(x2, tmp[2], tmp[3], ALU.add)

            v.memset(table[:, :], 1.0).then_inc(table_set, 1)
            dve.wait_ge(x_in, 16)
            h_done()
            rms_rows()
            dve.wait_ge(const_in, 16 * 9)
            two_pi = 2 * math.pi
            c1 = 6.28125
            c2 = float(np.float32(np.round((two_pi - c1) * 2 ** 20) / 2 ** 20))
            c3 = float(np.float32(two_pi - c1 - c2))
            rounder = 1.5 * 2 ** 23
            step(v.tensor_copy(pos_f[:, :], pos_i[:, :]))
            for tb in range(TB):
                step(v.tensor_scalar(ang[:, 0, tb, :], inv_f[:, :], pos_f[:, tb:tb + 1], None, ALU.mult))
            step(v.tensor_scalar(ang[:, 1], ang[:, 0], 1 / two_pi, rounder, ALU.mult, ALU.add))
            step(v.tensor_scalar(ang[:, 1], ang[:, 1], rounder, None, ALU.subtract))
            for part in (c1, c2, c3):
                step(v.scalar_tensor_tensor(ang[:, 0], ang[:, 1], -part, ang[:, 0], ALU.mult, ALU.add))
            step(v.tensor_scalar(ang[:, 0], ang[:, 0], 3.1415925, -3.1415925, ALU.min, ALU.max))
            step(v.tensor_scalar(ang[:, 2], ang[:, 0], -1.0, None, ALU.mult))
            step(v.tensor_tensor(ang[:, 2], ang[:, 2], ang[:, 0], ALU.max))
            v.tensor_scalar(ang[:, 1], ang[:, 2], -1.0, math.pi / 2, ALU.mult, ALU.add).then_inc(ang_ready, 1)
            dve.wait_ge(p_hi_ready, 1)
            v.tensor_tensor(p_lo[:, :, :, :], p_raw[:, :, :, :], p_hi[:, :, :, :].bitcast(F32),
                            ALU.subtract).then_inc(p_ready, 1)

            turn_lo(T_MLA, xt_hi, xt_lo)
            sums_ready()
            step(v.tensor_scalar(var[:, 0:2], stat[:, :, 0], 1.0 / MLA_Q, RMS_EPS, ALU.mult, ALU.add))
            step(v.tensor_scalar(var[:, 2:4], stat[:, :, 1], 1.0 / MLA_KV, RMS_EPS, ALU.mult, ALU.add))
            rsqrt(4)
            for tb in range(TB):
                v.tensor_scalar(a_norm[:, tb, 0:MLA_Q], a_rows[:, tb, 0:MLA_Q], rstd[:, tb:tb + 1], None, ALU.mult)
                ins = v.tensor_scalar(a_norm[:, tb, MLA_Q:], a_rows[:, tb, MLA_Q:MLA_Q + MLA_KV],
                                      rstd[:, 2 + tb:3 + tb], None, ALU.mult)
            ins.then_inc(rows_ready, 1)
            dve.wait_ge(sincos, 1)
            half = ROPE // 2
            step(v.tensor_copy(k_rot[:, :, :], a_rows[:, :, MLA_Q + MLA_KV:]))
            step(rotate(k_rot[:, :, 0:half], k_rot[:, :, half:], cos_p[:, :, :], sin_p[:, :, :],
                        [rtmp[:, k, :, 0, :] for k in range(4)]))
            turn_lo(T_MLA_C, xt_hi, xt_lo)
            with loop(MLA_STEPS, 5 + 2 + 2) as i:
                heads = [P, TB, MLA_GROUP, half]
                dve.wait_ge(heads_copied, i + 1)
                rotate(q_rows[:, :, :, NOPE:NOPE + half], q_rows[:, :, :, NOPE + half:],
                       cos_p[:, :, :].unsqueeze(2).to_broadcast(heads), sin_p[:, :, :].unsqueeze(2).to_broadcast(heads),
                       [rtmp[:, k] for k in range(4)])
                v.tensor_copy(k_rows[:, :, :, NOPE:],
                              k_rot[:, :, :].unsqueeze(2).to_broadcast([P, TB, MLA_GROUP, ROPE])).then_inc(roped, 1)
                dve.wait_ge(qk_turned, i + 1)
                v.tensor_copy(kT[:, :, :].rearrange("p h t -> p (h t)"), flat[0:MLA_HD, 6 * BANK:8 * BANK]).then_inc(k_ready, 1)
                dve.wait_ge(scored, i + 1)
                step(v.scalar_tensor_tensor(prob0[:, :, :], psum[:, 0:MLA_GROUP, 0:CAUSAL_W], MLA_HD ** -0.5,
                                            mask[:, :].unsqueeze(1).to_broadcast([P, MLA_GROUP, CAUSAL_W]), ALU.mult, ALU.add))
                step(v.tensor_reduce(nmax[:, 0:MLA_GROUP], prob0[:, :, 0:P], AX.X, ALU.max, negate=True))
                v.tensor_reduce(nmax[:, MLA_GROUP:2 * MLA_GROUP], prob0[:, :, P:], AX.X, ALU.max, negate=True).then_inc(maxed, 1)
                dve.wait_ge(exped, i + 1)
                step(v.reciprocal(rinv[:, 0:2 * MLA_GROUP], rsum[:, 0:2 * MLA_GROUP]))
                step(v.tensor_tensor(prob0[:, :, 0:P], prob0[:, :, 0:P],
                                     rinv[:, 0:MLA_GROUP].unsqueeze(2).to_broadcast([P, MLA_GROUP, P]), ALU.mult))
                v.tensor_tensor(prob0[:, :, P:], prob0[:, :, P:],
                                rinv[:, MLA_GROUP:2 * MLA_GROUP].unsqueeze(2).to_broadcast([P, MLA_GROUP, SEQ]),
                                ALU.mult).then_inc(probs_ready, 1)
                dve.wait_ge(o_hi, i + 1)
                v.tensor_tensor(ot_lo[:, bass.ds(2 * i, 2), :].rearrange("p j t -> p (j t)"), psum[:, 7, :],
                                ot_hi[:, bass.ds(2 * i, 2), :].rearrange("p j t -> p (j t)").bitcast(F32),
                                ALU.subtract).then_inc(ot_ready, 1)
            add_rms_y(0, 1)
            h_done()
            rms_rows()
            turn_lo(T_FFN0, xt_hi, xt_lo)
            ffn(0)
            add_rms_y(1, 1)
            h_done()
            signal(rows_ready)
            ple(0, T_PLE0)
            rms_rows()

            turn_lo(T_DIL, xt_hi, xt_lo)
            def d_step(pair, par, loads):
                dve.wait_ge(dbias_in[par], 16 * 4 * loads)
                for hh in range(2):
                    bias = dbias[:, par, hh, :]
                    dve.wait_ge(d_scored, 2 * pair + hh + 1)
                    v.scalar_tensor_tensor(prob1[:, 0:3 * P], psum[:, 5, 0:3 * P], HD ** -0.5, bias[:, 0:3 * P],
                                           ALU.mult, ALU.add)
                    step(v.scalar_tensor_tensor(prob1[:, 3 * P:], flat[:, 6 * BANK:6 * BANK + 6 * P], HD ** -0.5,
                                                bias[:, 3 * P:], ALU.mult, ALU.add))
                    v.tensor_reduce(nmax[:, 0:1], prob1[:, 0:3 * P], AX.X, ALU.max, negate=True)
                    v.tensor_reduce(nmax[:, 1:2], prob1[:, 3 * P:], AX.X, ALU.max, negate=True).then_inc(d_maxed, 1)
                    dve.wait_ge(d_exped, 2 * pair + hh + 1)
                    step(v.reciprocal(rinv[:, 0:2], rsum[:, 0:2]))
                    v.tensor_scalar(prob1[:, 0:3 * P], prob1[:, 0:3 * P], rinv[:, 0:1], None, ALU.mult)
                    v.tensor_scalar(prob1[:, 3 * P:], prob1[:, 3 * P:], rinv[:, 1:2], None, ALU.mult).then_inc(d_probs, 1)
                dve.wait_ge(d_hi, pair + 1)
                sl = bass.ds(pair, 1)
                v.tensor_tensor(ot_lo[:, sl, :].rearrange("p j t -> p (j t)"), psum[:, 2, 0:SEQ],
                                ot_hi[:, sl, :].rearrange("p j t -> p (j t)").bitcast(F32), ALU.subtract).then_inc(d_ready, 1)

            d_step(0, 0, 1)
            with loop(PAIRS // 2 - 1, 2 * 2 * 2) as i:
                for u in range(2):
                    d_step(1 + u + 2 * i, 1 - u, 1 + u + i)
            d_step(PAIRS - 1, 1, PAIRS // 2)
            add_rms_y(0, 2)
            h_done()
            rms_rows()
            turn_lo(T_FFN1, xt_hi, xt_lo)
            ffn(1)
            add_rms_y(1, 2)
            h_done()
            signal(rows_ready)
            ple(1, T_PLE1)

            for l in (2, 3):
                n = l - 2
                c = C_MIX[l]
                signal(rows_ready)
                turn_lo((T_MIX2, T_MIX3)[n], xt_hi, xt_lo)
                dve.wait_ge(ret_copied, 3 * n + 2)
                for part in range(2):
                    qk = ret[:, :, part * RW:(part + 1) * RW].rearrange("p b (h d) -> p b h d", d=HD)
                    shape = [P, TB, RH, HD // 2]
                    size = TB * RH * HD // 2
                    tmp = [t1[:, :, :].rearrange("p b f -> p (b f)")[:, k * size:(k + 1) * size]
                           .rearrange("p (b h d) -> p b h d", b=TB, h=RH) for k in range(4)]
                    ins = rotate(qk[:, :, :, 0:HD // 2], qk[:, :, :, HD // 2:],
                                 rcos[:, :, :].unsqueeze(2).to_broadcast(shape), rsin[:, :, :].unsqueeze(2).to_broadcast(shape), tmp)
                    if part == 0:
                        step(ins)
                ins.then_inc(ret_roped, 1)
                dve.wait_ge(cv_copied, n + 1)
                prod, acc = cv[:, 1], cv[:, 2]
                step(v.tensor_tensor(prod, cv[:, 1], cv[:, 2], ALU.mult))
                for f in range(2):
                    step(v.tensor_scalar(acc[:, f, :], prod[:, f, :], mconv[:, n, f, 2:3], None, ALU.mult))
                    step(v.scalar_tensor_tensor(acc[:, f, 1:], prod[:, f, 0:SEQ - 1], mconv[:, n, f, 1:2], acc[:, f, 1:],
                                                ALU.mult, ALU.add))
                    step(v.scalar_tensor_tensor(acc[:, f, 2:], prod[:, f, 0:SEQ - 2], mconv[:, n, f, 0:1], acc[:, f, 2:],
                                                ALU.mult, ALU.add))
                step(v.tensor_tensor(acc, acc, cv[:, 0], ALU.mult))
                step(v.tensor_copy(ot_hi[:, 6:8, :], acc))
                v.tensor_tensor(ot_lo[:, 6:8, :], acc, ot_hi[:, 6:8, :].bitcast(F32), ALU.subtract).then_inc(cv_ready, 1)
                dve.wait_ge(dec_in, 16 * (n + 1))
                dve.wait_ge(ret_scored, n + 1)
                v.tensor_tensor(sc2[:, :, :], psum[:, 2:2 + RH, 0:CAUSAL_W], dec[:, :, :], ALU.mult).then_inc(ret_decayed, 1)
                dve.wait_ge(ret_summed, n + 1)
                heads = [P, 2 * RH, HD]
                rows = t1[:, :, 0:RW]
                sq = t1[:, :, RW:2 * RW]
                per_head = lambda a: a.rearrange("p b (h d) -> p b h d", d=HD)
                spread = lambda s: s.rearrange("p (b h) -> p b h", b=TB).unsqueeze(3).to_broadcast([P, TB, RH, HD])
                pairs = lambda s: s.rearrange("p (b h) -> p b h", b=TB)
                o_rows = psum[:, 0:2, 0:RW].rearrange("p b (h d) -> p b h d", d=HD)
                step(v.tensor_reduce(pairs(mean12[:, :]), o_rows, AX.X, ALU.add))
                step(v.tensor_scalar(mean12[:, :], mean12[:, :], 1.0 / HD, None, ALU.mult))
                step(v.tensor_tensor(per_head(rows), o_rows, spread(mean12[:, :]), ALU.subtract))
                step(v.tensor_tensor(sq, rows, rows, ALU.mult))
                step(v.tensor_reduce(pairs(var[:, :]), per_head(sq), AX.X, ALU.add))
                step(v.tensor_scalar(var[:, :], var[:, :], 1.0 / HD, LN_EPS, ALU.mult, ALU.add))
                rsqrt(2 * RH)
                step(v.tensor_tensor(per_head(rows), per_head(rows), spread(rstd[:, :]), ALU.mult))
                v.tensor_tensor(rows, rows, ret[:, :, 3 * RW:], ALU.mult).then_inc(rows_ready, 1)
                dve.wait_ge(mbias_in, 32 * (n + 1))
                dve.wait_ge(m_scored, n + 1)
                step(v.scalar_tensor_tensor(sc2[:, :, :], psum[:, 2:2 + RH, 0:CAUSAL_W], HD ** -0.5, mbias[:, :, :],
                                            ALU.mult, ALU.add))
                step(v.tensor_reduce(nmax[:, 0:RH], sc2[:, :, 0:P], AX.X, ALU.max, negate=True))
                v.tensor_reduce(nmax[:, RH:], sc2[:, :, P:], AX.X, ALU.max, negate=True).then_inc(m_maxed, 1)
                dve.wait_ge(m_exped, n + 1)
                step(v.reciprocal(rinv[:, :], rsum[:, :]))
                step(v.tensor_tensor(sc2[:, :, 0:P], sc2[:, :, 0:P], rinv[:, 0:RH].unsqueeze(2).to_broadcast([P, RH, P]), ALU.mult))
                v.tensor_tensor(sc2[:, :, P:], sc2[:, :, P:], rinv[:, RH:].unsqueeze(2).to_broadcast([P, RH, SEQ]),
                                ALU.mult).then_inc(m_probs, 1)
                dve.wait_ge(m_hi, n + 1)
                v.tensor_tensor(ot_lo[:, 3:6, :].rearrange("p j t -> p (j t)"), flat[:, 0:3 * SEQ],
                                ot_hi[:, 3:6, :].rearrange("p j t -> p (j t)").bitcast(F32), ALU.subtract).then_inc(m_ready, 1)
                turn_lo((T_RET2, T_RET3)[n], ot_hi, ot_lo)
                layer_norm_y(C_WO[l] + PROJ_N - 1, 3 + 2 * n)
                h_done()
                signal(rows_ready)
                turn_lo(T_FFN[l], xt_hi, xt_lo)
                ffn(l)
                layer_norm_y(C_OUT[l] + FFN_OUT_N - 1, 4 + 2 * n)
                h_done()


STAGE_WIDTHS = {name: ws for name, _, ws in STAGES}
H_READY_END = 11


def bucket_rows():
    d = (2 * P - 1 - np.arange(SPAN)).astype(np.int64)
    rows = np.zeros((BUCKETS + 1, NG + 1, SPAN), np.float32)
    for g in range(NG + 1):
        far = 2048 if g < NG else 128
        if g < NG:
            window, dil = DIL[g]
            valid = (d >= 0) & (d % dil == 0) & (d <= window // dil * dil)
        else:
            valid = d >= 0
        exact = BUCKETS // 2
        n = np.maximum(d, 1).astype(np.float32)
        large = exact + (np.log(n / np.float32(exact)) / np.float32(math.log(far / exact))
                         * np.float32(BUCKETS - exact)).astype(np.int32)
        bucket = np.where(d < exact, np.maximum(d, 0), np.minimum(large, BUCKETS - 1))
        rows[bucket[valid], g, np.nonzero(valid)[0]] = 1.0
        rows[BUCKETS, g, ~valid] = NEG
    return rows


def constants():
    q, k = np.arange(P)[:, None], np.arange(P)[None, :]
    tri = np.where(k <= q, 0.0, NEG).astype(np.float32)
    causal = np.concatenate([tri, np.zeros((P, P), np.float32), tri], axis=1)
    gamma = 1.0 - 2.0 ** (-5.0 - np.arange(RH, dtype=np.float64))
    key, query = np.arange(P)[:, None, None], np.arange(SEQ)[None, None, :]
    far = np.where(query >= key, gamma[None, :, None] ** np.maximum(query - key, 0), 0.0)
    decay = (np.concatenate([far, far[:, :, 0:P]], axis=2) * HD ** -0.5).astype(np.float32)
    inv = (np.float32(10000.0) ** (-np.arange(0, HD, 2, dtype=np.float32) / np.float32(HD))).astype(np.float32)
    ang = (np.arange(SEQ, dtype=np.float32)[:, None] * inv[None, :]).astype(np.float32)
    rows = lambda t: np.ascontiguousarray(t.astype(np.float32).reshape(TB, P, HD // 2).transpose(1, 0, 2))
    inv_mla = (np.float32(10000.0) ** (-np.arange(ROPE // 2, dtype=np.float32) / np.float32(ROPE // 2))).astype(np.float32)
    return {
        "causal": causal, "decay": decay, "ret_cos": rows(np.cos(ang)), "ret_sin": rows(np.sin(ang)),
        "inv_freq": np.ascontiguousarray(np.broadcast_to(inv_mla, (P, ROPE // 2))),
        "onehot": bucket_rows(), "identity": np.eye(P, dtype=np.float32),
    }


def tile(w, kts, cols):
    t = w.reshape(-1, P, w.shape[1])[kts.start:kts.stop][:, :, cols]
    return t.transpose(1, 0, 2).reshape(P, -1)


def pad(chunk, width=W):
    full = np.zeros((P, width), chunk.dtype)
    full[:, :chunk.shape[1]] = chunk
    return full


def wide(w):
    return [tile(w, range(k, k + 2), slice(0, D)) for k in range(0, w.shape[0] // P, 2)]


def paired(w, n, left, right, step=P):
    return [tile(w, range(0, KT), np.r_[left + j * step:left + j * step + P, right + j * step:right + j * step + P])
            for j in range(n)]


def by_three(w, cols):
    return [tile(w, r, cols) for r in (range(0, 3), range(3, 6), range(6, 8))]


def pack(a):
    out = {}
    wa = a["mla_w_a"][0]
    out["w_mla_a"] = [[tile(wa, range(0, 4), slice(0, BANK)), tile(wa, range(4, 8), slice(0, BANK)),
                       pad(tile(wa, range(0, KT), slice(BANK, MLA_A)))]]
    uq, ukv = a["mla_w_uq"][0], a["mla_w_ukv"][0].reshape(MLA_KV, 16, NOPE + MLA_V)
    uk = np.ascontiguousarray(ukv[:, :, :NOPE]).reshape(MLA_KV, -1)
    uv = np.ascontiguousarray(ukv[:, :, NOPE:]).reshape(MLA_KV, -1)
    nq, nk = MLA_GROUP * MLA_HD, MLA_GROUP * NOPE
    out["w_mla_heads"] = [[tile(uq, range(0, 3), slice(i * nq, (i + 1) * nq)),
                           tile(uk, range(0, 2), slice(i * nk, (i + 1) * nk)),
                           tile(uv, range(0, 2), slice(i * nk, (i + 1) * nk))] for i in range(MLA_STEPS)]
    threes = lambda chunks: [chunks[i:i + 3] for i in range(0, len(chunks) // 3 * 3, 3)]
    for l, w_o in ((0, a["mla_w_o"][0]), (1, a["dil_w_o"][0])):
        out[f"w_tail{l}"] = threes(wide(w_o) + paired(a["ffn_w_in"][l], FT, 0, D_FF) + wide(a["ffn_w_out"][l])
                                   + wide(a["ple_w_gate"][l]) + wide(a["ple_w_proj"][l]))
    wd = a["dil_w_qkv"][0]
    steps = []
    for i in range(PAIRS):
        at = lambda g, kind: (3 * g + kind) * D + i * P
        vcols = np.concatenate([np.arange(at(g, 2), at(g, 2) + P) for g in range(NG)])
        steps.append([paired(wd, 1, at(g, 0), at(g, 1))[0] for g in range(NG)] + by_three(wd, vcols))
    out["w_dil"] = steps
    for l in (2, 3):
        w = a["w_in_2"][l - 2]
        mq, cb = 4 * RW, 7 * RW
        chunks = [tile(w, range(4 * hf, 4 * hf + 4), slice(b * BANK, (b + 1) * BANK)) for b in range(3) for hf in range(2)]
        chunks += paired(w, 3, mq, mq + RW) + by_three(w, slice(mq + 2 * RW, mq + 3 * RW))
        chunks += [tile(w, range(0, KT), slice(cb + b * 2 * P, cb + (b + 1) * 2 * P)) for b in range(3)]
        out[f"w_mix{l}"] = [chunks]
        rest = wide(a["w_out_2"][l - 2]) + paired(a["w_up_2"][l - 2], FT, 0, D_FF) + wide(a["w_down_2"][l - 2])
        out[f"w_tail{l}"] = threes(rest)
        out[f"w_tail{l}b"] = [rest[len(rest) // 3 * 3:]]
    return {name: np.stack([np.concatenate(it, axis=1) for it in its]) for name, its in out.items()}


def kernel(**inputs):
    import concourse.bacc as bacc
    from concourse.bass_utils import run_bass_kernel_spmd

    a = {name: np.asarray(v) for name, v in inputs.items()}
    feat = lambda g: g.reshape(-1, P).T
    ones = np.ones((P, KT), np.float32)
    norm_g = a["norm_g"]
    c_gain = np.concatenate([feat(a["mla_q_norm"][0]), feat(a["mla_kv_norm"][0]), ones[:, 0:3]], axis=1)
    by_turn = {T_MLA: feat(norm_g[0, 0]), T_MLA_C: c_gain, T_FFN0: feat(norm_g[0, 2]),
               T_DIL: feat(norm_g[1, 0]), T_FFN1: feat(norm_g[1, 2])}
    arrays = constants()
    arrays["x"] = a["x"][0]
    arrays["pT"] = np.ascontiguousarray(a["p"][:, 0].transpose(0, 2, 1).reshape(2, 2, P, SEQ).transpose(2, 0, 1, 3))
    arrays["positions"] = np.ascontiguousarray(a["positions"][0].reshape(TB, P).T)
    arrays["gain_fm"] = np.stack([by_turn.get(t, ones) for t in range(len(TURN_TILES))], axis=1)
    arrays["gain_rows"] = np.stack([norm_g[0, 1], norm_g[0, 3], norm_g[1, 1], norm_g[1, 3]] + [
        a[n][l] for l in range(2) for n in ("ln1_g_2", "ln1_b_2", "ln2_g_2", "ln2_b_2")])
    arrays["rel_table"] = a["rel_bias"]
    arrays["rel_table_2"] = a["rel_bias_2"]
    arrays["ffn_conv"] = np.ascontiguousarray(a["ffn_conv_w_2"].reshape(2, 3, FT, P).transpose(3, 0, 2, 1))
    arrays["mix_conv"] = np.ascontiguousarray(a["conv_w_2"].reshape(2, 3, 2, P).transpose(3, 0, 2, 1))
    weights = pack(a)

    nc = bacc.Bacc("TRN2", target_bir_lowering=False, num_devices=1)

    def dram(name, array):
        return nc.dram_tensor(name, list(array.shape), mybir.dt.from_np(array.dtype), kind="ExternalInput").ap()

    aps = {name: dram(name, v) for name, v in arrays.items()}
    streams = {name: dram(name, v) for name, v in weights.items()}
    out = nc.dram_tensor("out", [SEQ, D], F32, kind="ExternalOutput").ap()
    build(nc, weights=streams, out=out, **aps)
    got = run_bass_kernel_spmd(nc, [{**arrays, **weights}], core_ids=[0])
    return got.results[0]["out"].reshape(1, SEQ, D)
```

```python
from contextlib import ExitStack, contextmanager
import math

import numpy as np
import concourse.bass as bass
from concourse import mybir

F32 = mybir.dt.float32
F32R = mybir.dt.float32r
I32 = mybir.dt.int32
BF16 = mybir.dt.bfloat16
ALU = mybir.AluOpType
ACT = mybir.ActivationFunctionType
AX = mybir.AxisListType

P = 128
SEQ = 256
TB = SEQ // P
D = 1024
KT = D // P
D_FF = 2816
FT = D_FF // P
BANK = 512
W = 2048
SLOTS = 3

MLA_Q, MLA_KV, NOPE, ROPE, MLA_V = 384, 256, 64, 32, 64
MLA_A = MLA_Q + MLA_KV + ROPE
MLA_HD = NOPE + ROPE
MLA_GROUP = 4
MLA_STEPS = 16 // MLA_GROUP
DIL = ((128, 1), (512, 4), (2048, 16))
NG = len(DIL)
PAIRS = 8
HD = 64
RH = 6
RW = RH * HD
BUCKETS = 32
CAUSAL_W = P + 2 * P
SPAN = 3 * P
NEG = -1e30
RMS_EPS, LN_EPS = 1e-6, 1e-5
ALPHA = 4.0 ** 0.25

MLA_WIDTHS = (3 * MLA_GROUP * MLA_HD, 2 * MLA_GROUP * NOPE, 2 * MLA_GROUP * MLA_V)
DIL_WIDTHS = (W, W, W, 3 * 384, 3 * 384, 2 * 384)
PROJ_N, FFN_OUT_N = KT // 2, FT // 2
TAIL1 = PROJ_N + FT + FFN_OUT_N + PROJ_N + 1
TAIL2 = PROJ_N + FT + FFN_OUT_N
MIX2_WIDTHS = (W,) * 9 + (3 * 384, 3 * 384, 2 * 384) + (W,) * 3
STAGES = (
    ("w_mla_a", 1, (W, W, W)),
    ("w_mla_heads", MLA_STEPS, MLA_WIDTHS),
    ("w_tail0", TAIL1 // 3, (W, W, W)),
    ("w_dil", PAIRS, DIL_WIDTHS),
    ("w_tail1", TAIL1 // 3, (W, W, W)),
    ("w_mix2", 1, MIX2_WIDTHS),
    ("w_tail2", TAIL2 // 3, (W, W, W)), ("w_tail2b", 1, (W,) * (TAIL2 % 3)),
    ("w_mix3", 1, MIX2_WIDTHS),
    ("w_tail3", TAIL2 // 3, (W, W, W)), ("w_tail3b", 1, (W,) * (TAIL2 % 3)),
)
CHUNKS = sum(n * len(ws) for _, n, ws in STAGES)
C_MLA_A = 0
C_MLA = 3
C_TAIL0 = C_MLA + MLA_STEPS * 3
C_DIL = C_TAIL0 + TAIL1
C_TAIL1 = C_DIL + PAIRS * 6
C_L2 = C_TAIL1 + TAIL1
C_L3 = C_L2 + len(MIX2_WIDTHS) + TAIL2
FIRST = (C_TAIL0, C_TAIL1, C_L2 + len(MIX2_WIDTHS), C_L3 + len(MIX2_WIDTHS))
C_WO = FIRST
C_IN = tuple(c + PROJ_N for c in FIRST)
C_OUT = tuple(c + FT for c in C_IN)
C_GATE = tuple(c + FFN_OUT_N for c in C_OUT[:2])
C_PROJ = tuple(c + PROJ_N for c in C_GATE)
C_MIX = (C_MLA_A, C_DIL, C_L2, C_L3)

TURN_TILES = (8, 5, 8, 8, 8, 8, 8, 8, 3, 8, 8, 3, 8)
(T_MLA, T_MLA_C, T_FFN0, T_PLE0, T_DIL, T_FFN1, T_PLE1,
 T_MIX2, T_RET2, T_FFN2, T_MIX3, T_RET3, T_FFN3) = range(len(TURN_TILES))
T_FFN = (T_FFN0, T_FFN1, T_FFN2, T_FFN3)
TURN_BANKS = tuple((n + 1) // 2 for n in TURN_TILES)
BANKS_BEFORE = tuple(sum(TURN_BANKS[:t]) for t in range(len(TURN_TILES)))
TURN_AT = {T_MLA_C: (0, 1, 2), T_FFN0: (7, 0, 1, 2), T_DIL: (0, 1, 2, 3), T_FFN1: (5, 6, 7, 2), T_MIX2: (0, 1, 2, 3),
           T_RET2: (6, 7), T_RET3: (6, 7)}
Y_AT = {("wo", 0): (3, 5), ("wo", 1): (0, 3)}
GAINED = (T_MLA, T_MLA_C, T_FFN0, T_DIL, T_FFN1)
SHIFTED = (T_FFN2, T_MIX3, T_FFN3)
YS = (("wo", 0), ("out", 0), ("proj", 0), ("wo", 1), ("out", 1), ("proj", 1), ("wo", 2), ("out", 2), ("wo", 3), ("out", 3))


def turn_at(t):
    return TURN_AT.get(t, (4, 5, 6, 7))


def y_at(name, l):
    return Y_AT.get((name, l), (0, 2))


def y_chunk(name, l):
    return {"wo": lambda: C_WO[l] + PROJ_N, "out": lambda: C_OUT[l] + FFN_OUT_N, "proj": lambda: C_PROJ[l] + 1}[name]() - 1


def rows_of(t):
    return TB * (t - T_FFN0)


def build(nc, x, pT, positions, inv_freq, gain_fm, shift_fm, gain_rows, onehot, rel_table, rel_table_2, causal, decay,
          ret_cos, ret_sin, ffn_conv, mix_conv, identity, weights, out):
    heads_all = NG * 16 + RH
    bias_rows = nc.dram_tensor("bias_rows", [heads_all, SPAN], F32, kind="Internal").ap()
    bias_tiles = nc.dram_tensor("bias_tiles", [heads_all, P, 2 * P], F32, kind="Internal").ap()

    ctx = ExitStack()
    with ctx:
        def sb(name, shape, dt=F32, at=ctx):
            return at.enter_context(nc.sbuf_tensor(name, shape, dt))

        def sem(name):
            return ctx.enter_context(nc.semaphore(name))

        raw = sb("raw", [P, SLOTS, W])
        w_hi = sb("w_hi", [P, SLOTS, W], F32R)
        w_lo = sb("w_lo", [P, SLOTS, W], F32R)
        h = sb("h", [P, TB, D])
        t1 = sb("t1", [P, TB, D])
        xt_hi = sb("xt_hi", [P, KT, SEQ], F32R)
        xt_lo = sb("xt_lo", [P, KT, SEQ], F32R)
        ot_hi = sb("ot_hi", [P, KT, SEQ], F32R)
        ot_lo = sb("ot_lo", [P, KT, SEQ], F32R)
        p_hi = sb("p_hi", [P, 2, 2, SEQ], F32R)
        p_lo = sb("p_lo", [P, 2, 2, SEQ], F32R)
        gbuf = sb("gbuf", [P, 2, D])
        ident = sb("ident", [P, P])
        mask = sb("mask", [P, CAUSAL_W])
        gains = sb("gains", [P, len(GAINED + SHIFTED), KT])
        shifts = sb("shifts", [P, len(SHIFTED), KT])
        fconv = sb("fconv", [P, 2, FT, 3])
        mconv = sb("mconv", [P, 2, 2, 3])
        rcos = sb("rcos", [P, TB, HD // 2])
        rsin = sb("rsin", [P, TB, HD // 2])
        pos_i = sb("pos_i", [P, TB], I32)
        pos_f = sb("pos_f", [P, TB])
        inv_f = sb("inv_f", [P, ROPE // 2])
        cos_p = sb("cos_p", [P, TB, ROPE // 2])
        sin_p = sb("sin_p", [P, TB, ROPE // 2])
        stat = sb("stat", [P, 2 * TB])
        bn6 = sb("bn6", [P, TB, 2, 6])
        mv = sb("mv", [P, TB, 2])
        var = sb("var", [P, 2 * RH])
        rstd = sb("rstd", [P, 2 * RH])
        newton = sb("newton", [P, 2 * RH])
        nhalf = sb("nhalf", [P, 8])
        mean12 = sb("mean12", [P, 2 * RH])
        nmax = sb("nmax", [P, 2 * RH])
        rsum = sb("rsum", [P, 2 * RH])
        rinv = sb("rinv", [P, 2 * RH])
        gate = sb("gate", [P, SLOTS, SEQ])
        conv = sb("conv", [P, SLOTS, SEQ])

        with ExitStack() as part:
            ht_hi = sb("ht_hi", [P, FT, SEQ], F32R, part)
            ht_lo = sb("ht_lo", [P, FT, SEQ], F32R, part)
            rb_ffn = sb("rb_ffn", [P, SEQ], F32, part)
        with ExitStack() as part:
            oneh = sb("oneh", [BUCKETS + 1, NG + 1, SPAN], F32, part)
            table = sb("table", [BUCKETS + 1, heads_all], F32, part)
            brow = sb("brow", [16, NG + 1, SPAN], F32, part)
            p_raw = sb("p_raw", [P, 2, 2, SEQ], F32, part)
            ang = sb("ang", [P, 3, TB, ROPE // 2], F32, part)
            a_rows = sb("a_rows", [P, TB, MLA_A], F32, part)
            k_rot = sb("k_rot", [P, TB, ROPE], F32, part)
            rtmp = sb("rtmp", [P, 4, TB, MLA_GROUP, ROPE // 2], F32, part)
            q_rows = sb("q_rows", [P, TB, MLA_GROUP, MLA_HD], F32, part)
            k_rows = sb("k_rows", [P, TB, MLA_GROUP, MLA_HD], F32, part)
            v_next = sb("v_next", [P, TB, MLA_GROUP, MLA_V], F32, part)
            v_rows = sb("v_rows", [P, TB, MLA_GROUP, MLA_V], F32, part)
            qT = sb("qT", [MLA_HD, MLA_GROUP, SEQ], F32, part)
            kT = sb("kT", [MLA_HD, MLA_GROUP, SEQ], F32, part)
            prob0 = sb("prob0", [P, MLA_GROUP * CAUSAL_W], F32, part)
            probT0 = sb("probT0", [P, MLA_GROUP * 3, P], F32, part)
        with ExitStack() as part:
            dqk = sb("dqk", [P, 2, NG, 2, SEQ], F32, part)
            dv = sb("dv", [P, 2, TB, NG, 2, HD], F32, part)
            dbias = sb("dbias", [P, 2, 2, 3 * NG * P], F32, part)
            prob1 = sb("prob1", [P, 3 * NG * P], F32, part)
            probT1 = sb("probT1", [P, 3 * NG, P], F32, part)
            rb_dil = sb("rb_dil", [P, SEQ], F32, part)
        with ExitStack() as part:
            ret = sb("ret", [P, TB, 4 * RW], F32, part)
            rqk = sb("rqk", [P, RH, SEQ], F32, part)
            sc2 = sb("sc2", [P, RH, CAUSAL_W], F32, part)
            dec = sb("dec", [P, RH, CAUSAL_W], F32, part)
            mqk = sb("mqk", [P, RH // 2, 2, SEQ], F32, part)
            mvr = sb("mvr", [P, TB, RH, HD], F32, part)
            cv = sb("cv", [P, 3, 2, SEQ], F32, part)
            mbias = sb("mbias", [P, RH, CAUSAL_W], F32, part)
        probT2 = mbias[:, :, :].rearrange("p h k -> p (h k)").rearrange("p (j q) -> p j q", q=P)

        def by_head(a, k):
            return a.rearrange("p (h k) -> p h k", k=k)

        psum = ctx.enter_context(nc.psum_tensor("psum", [P, 8, BANK], F32))
        flat = psum[:, :, :].rearrange("p b n -> p (b n)")

        logits = psum[:, 2:2 + RH, 0:CAUSAL_W]
        near, far = slice(0, P), slice(P, CAUSAL_W)
        probs_turned = flat[:, 8 * BANK - RH * CAUSAL_W:]

        def y_rows(y, tb):
            return flat[:, y_at(*y)[tb] * BANK:y_at(*y)[tb] * BANK + D]

        staging = (gate, conv)
        unused = [s[:, :, :].rearrange("p a t -> p (a t)").bitcast(BF16)[:, 0:D] for s in staging]

        def table_of(tab, turns, t, kt):
            return tab[:, turns.index(t), kt:kt + 1]

        landed = [sem(f"landed{s}") for s in range(SLOTS)]
        hi_split = sem("hi_split")
        lo_split = sem("lo_split")
        chunk_used = sem("chunk_used")
        const_in = sem("const_in")
        p_in = sem("p_in")
        x_in = [sem(f"x{tb}_in") for tb in range(TB)]
        ident_in = sem("ident_in")
        g_in = [sem("g0_in"), sem("g1_in")]
        bias_src_in = sem("bias_src_in")
        table_set = sem("table_set")
        bias_made = sem("bias_made")
        brow_out = sem("brow_out")
        rows_stored = sem("rows_stored")
        tiles_stored = sem("tiles_stored")
        dbias_in = [sem("dbias0_in"), sem("dbias1_in")]
        mbias_in = sem("mbias_in")
        dec_in = sem("dec_in")
        rows_ready = sem("rows_ready")
        y0_ready = sem("y0_ready")
        r_ready = sem("r_ready")
        r_turned = sem("r_turned")
        ra_ready = sem("ra_ready")
        v_ready = sem("v_ready")
        turned = sem("turned")
        turned_hi = sem("turned_hi")
        xt_ready = sem("xt_ready")
        squared = sem("squared")
        h_rows = sem("h_rows")
        gate_ready = sem("gate_ready")
        conv_ready = sem("conv_ready")
        hidden_ready = sem("hidden_ready")
        sig_ready = sem("sig_ready")
        p_hi_ready = sem("p_hi_ready")
        p_ready = sem("p_ready")
        a_copied = sem("a_copied")
        ang_ready = sem("ang_ready")
        sincos = sem("sincos")
        heads_copied = sem("heads_copied")
        roped = sem("roped")
        qk_turned = sem("qk_turned")
        q_ready = sem("q_ready")
        k_ready = sem("k_ready")
        scored = sem("scored")
        maxed = sem("maxed")
        exped = sem("exped")
        probs_ready = sem("probs_ready")
        p_turned = sem("p_turned")
        pt_ready = sem("pt_ready")
        o_summed = sem("o_summed")
        o_hi = sem("o_hi")
        ot_ready = sem("ot_ready")
        dqk_copied = sem("dqk_copied")
        d_copied = sem("d_copied")
        d_scored = sem("d_scored")
        d_maxed = sem("d_maxed")
        d_exped = sem("d_exped")
        d_probs = sem("d_probs")
        d_turned = sem("d_turned")
        d_pt = sem("d_pt")
        d_summed = sem("d_summed")
        d_hi = sem("d_hi")
        d_ready = sem("d_ready")
        ret_copied = sem("ret_copied")
        mqk_copied = sem("mqk_copied")
        mv_copied = sem("mv_copied")
        cv_copied = sem("cv_copied")
        ret_roped = sem("ret_roped")
        ret_turned = sem("ret_turned")
        rqk_ready = sem("rqk_ready")
        ret_scored = sem("ret_scored")
        ret_decayed = sem("ret_decayed")
        ret_summed = sem("ret_summed")
        m_scored = sem("m_scored")
        m_maxed = sem("m_maxed")
        m_exped = sem("m_exped")
        m_probs = sem("m_probs")
        m_turned = sem("m_turned")
        m_pt = sem("m_pt")
        m_summed = sem("m_summed")
        m_hi = sem("m_hi")
        m_ready = sem("m_ready")
        cv_ready = sem("cv_ready")
        dve_step = sem("dve_step")
        stored = sem("stored")

        block = ctx.enter_context(nc.Block())

        @block.sync
        def _(sp):
            for tb in range(TB):
                sp.dma_start(h[:, tb, :], x[tb * P:(tb + 1) * P, :]).then_inc(x_in[tb], 16)

            def stream(name, at, u, i, per, first):
                c = at + u
                width = STAGE_WIDTHS[name][u]
                off = sum(STAGE_WIDTHS[name][:u])
                if c >= SLOTS:
                    sp.wait_ge(lo_split, c - SLOTS + 1 + per * i)
                src = weights[name][first, :, off:off + width]
                sp.dma_start(raw[:, c % SLOTS, 0:width], src).then_inc(landed[c % SLOTS], 16)

            at = 0
            for name, n, widths in STAGES:
                per = len(widths)
                if n > 1:
                    with sp.Fori(0, n) as i:
                        for u in range(per):
                            stream(name, at, u, i, per, i)
                else:
                    for u in range(per):
                        stream(name, at, u, 0, per, 0)
                at += n * per

            for tb in range(TB):
                sp.wait_ge(rows_ready, rows_of(len(TURN_TILES)) + tb + 1)
                sp.dma_start(out[tb * P:(tb + 1) * P, :], h[:, tb, :]).then_inc(stored, 16)
            sp.wait_ge(stored, 16 * TB)

        @block.gpsimd
        def _(pool):
            pool.dma_start(ident[:, :], identity).then_inc(ident_in, 16)
            for dst, src in ((gains[:, :, :], gain_fm), (shifts[:, :, :], shift_fm), (mask[:, :], causal), (fconv[:, :, :, :], ffn_conv), (mconv[:, :, :, :], mix_conv),
                             (rcos[:, :, :], ret_cos), (rsin[:, :, :], ret_sin), (inv_f[:, :], inv_freq),
                             (pos_i[:, :], positions)):
                pool.dma_start(dst, src).then_inc(const_in, 16)
            pool.dma_start(p_raw[:, :, :, :], pT).then_inc(p_in, 16)
            pool.dma_start(oneh[:, :, :], onehot).then_inc(bias_src_in, 16)
            pool.wait_ge(table_set, 1)
            pool.dma_start(table[0:BUCKETS, 0:NG * 16], rel_table).then_inc(bias_src_in, 16)
            pool.dma_start(table[0:BUCKETS, NG * 16:], rel_table_2).then_inc(bias_src_in, 16)

            def lo_part(c, turn):
                s = c % SLOTS
                pool.wait_ge(hi_split, c + 1 + turn * SLOTS)
                nc.gpsimd.tensor_tensor(w_lo[:, s, :], raw[:, s, :], w_hi[:, s, :].bitcast(F32),
                                        ALU.subtract).then_inc(lo_split, 1)

            with pool.Fori(0, CHUNKS // SLOTS) as i:
                for u in range(SLOTS):
                    lo_part(u, i)
            for c in range(CHUNKS // SLOTS * SLOTS, CHUNKS):
                lo_part(c, 0)

        @block.tensor
        def _(pe):
            def mm(dst, lhsT, rhs, start, stop):
                return nc.tensor.matmul(dst, lhsT, rhs, start=start, stop=stop)

            def split_x(dst, x_hi, x_lo, hi, lo, start, stop):
                mm(dst, x_hi, hi, start, False)
                mm(dst, x_hi, lo, False, False)
                return mm(dst, x_lo, hi, False, stop)

            def split_w(dst, hi, lo, x_hi, x_lo, start, stop):
                mm(dst, hi, x_hi, start, False)
                mm(dst, hi, x_lo, False, False)
                return mm(dst, lo, x_hi, False, stop)

            def chunk(c, cols, more=0):
                pe.wait_ge(lo_split, c + 1 + more)
                s = c % SLOTS
                n = W // cols
                return (w_hi[:, s, 0:n * cols].rearrange("p (k n) -> p k n", n=cols),
                        w_lo[:, s, 0:n * cols].rearrange("p (k n) -> p k n", n=cols))

            def arrive(t, kt):
                if t is not None and kt % 2 == 0:
                    pe.wait_ge(xt_ready, BANKS_BEFORE[t] + kt // 2 + 1)

            def rows_product(c, cols, kts, lhs, banks, first, last, more=0, t=None):
                hi, lo = chunk(c, cols, more)
                for tb in range(TB):
                    tok = slice(tb * P, (tb + 1) * P)
                    for j, kt in enumerate(kts):
                        if tb == 0:
                            arrive(t, kt)
                        ins = split_x(banks[tb], lhs[0][:, kt, tok], lhs[1][:, kt, tok], hi[:, j, :], lo[:, j, :],
                                      first and j == 0, last and j == len(kts) - 1)
                ins.then_inc(chunk_used, 1)

            def tiles_product(c, bank, more=0, t=None):
                hi, lo = chunk(c, 2 * P, more)
                for half in range(2):
                    f = slice(half * P, (half + 1) * P)
                    for kt in range(KT):
                        if half == 0:
                            arrive(t, kt)
                        ins = split_w(psum[:, bank, half * SEQ:(half + 1) * SEQ], hi[:, kt, f], lo[:, kt, f],
                                      xt_hi[:, kt, :], xt_lo[:, kt, :], kt == 0, kt == KT - 1)
                ins.then_inc(chunk_used, 1)

            def wide_chunk(c, m, n, lhs, at, y=False, down=False):
                hi, lo = chunk(c + m, D)
                for tb in range(TB):
                    tok = slice(tb * P, (tb + 1) * P)
                    dst = [psum[:, at[tb] + nb, :] for nb in range(2)]
                    col = [slice(nb * BANK, (nb + 1) * BANK) for nb in range(2)]
                    for j in range(2):
                        start, stop = m + j == 0, m == n - 1 and j == 1
                        kt = 2 * (n - 1 - m if down else m) + j
                        a_hi, a_lo = lhs[0][:, kt, tok], lhs[1][:, kt, tok]
                        for nb in range(2):
                            mm(dst[nb], a_hi, hi[:, j, col[nb]], start, False)
                        for nb in range(2):
                            mm(dst[nb], a_hi, lo[:, j, col[nb]], False, False)
                        for nb in range(2):
                            ins = mm(dst[nb], a_lo, hi[:, j, col[nb]], False, stop)
                    if y and m == n - 1 and tb == 0:
                        ins.then_inc(y0_ready, 1)
                ins.then_inc(chunk_used, 1)

            def turn(t, src, ready):
                for tb in range(TB):
                    ready(tb)
                    for kt in range(TURN_TILES[t]):
                        at = (kt % 2) * SEQ + tb * P
                        ins = nc.tensor.transpose(psum[:, turn_at(t)[kt // 2], at:at + P],
                                                  src[:, tb, kt * P:(kt + 1) * P], ident[:, :])
                        if tb == TB - 1 and (kt % 2 == 1 or kt == TURN_TILES[t] - 1):
                            ins.then_inc(turned, 1)

            def block_ready(t):
                return lambda tb: pe.wait_ge(rows_ready, rows_of(t) + tb + 1)

            def turn_r(count):
                pe.wait_ge(r_ready, count)
                for tb in range(TB):
                    ins = mm(psum[:, 7, tb * P:(tb + 1) * P], rstd[:, tb:tb + 1].to_broadcast([P, P]), ident[:, :], True, True)
                ins.then_inc(r_turned, 1)

            xt = (xt_hi, xt_lo)

            def ffn(l):
                def pair(u, i, t=None):
                    j = u
                    if u >= SLOTS:
                        pe.wait_ge(hidden_ready, l * FT + j - SLOTS + 1 + SLOTS * i)
                    tiles_product(C_IN[l] + u, 4 + u % SLOTS, SLOTS * i, t)

                pair(0, 0, T_FFN[l])
                if l < 2:
                    turn_r((2, 4)[l])
                for u in range(1, SLOTS):
                    pair(u, 0)
                full = FT // SLOTS
                with pe.Fori(0, full - 1) as i:
                    for u in range(SLOTS):
                        pair(SLOTS + u, i)
                for u in range(full * SLOTS, FT):
                    pair(u, 0)
                for m in range(FFN_OUT_N):
                    pe.wait_ge(hidden_ready, l * FT + 2 * m + 2)
                    wide_chunk(C_OUT[l], m, FFN_OUT_N, (ht_hi, ht_lo), y_at("out", l), True)

            def wo(l, m):
                wide_chunk(C_WO[l], m, PROJ_N, (ot_hi, ot_lo), y_at("wo", l), True, l >= 2)

            def tail(l):
                turn(T_FFN[l], t1 if l >= 2 else h, block_ready(T_FFN[l]))
                ffn(l)

            def ple(l, t):
                turn(t, h, block_ready(t))
                for m in range(PROJ_N):
                    arrive(t, 2 * m)
                    wide_chunk(C_GATE[l], m, PROJ_N, xt, (0, 2))
                if l == 0:
                    pe.wait_ge(p_ready, 1)
                wide_chunk(C_PROJ[l], 0, 1, (p_hi[:, l], p_lo[:, l]), (4, 6), True)
                pe.wait_ge(sig_ready, TB * (l + 1))

            pe.wait_ge(ident_in, 16)
            turn(T_MLA, h, lambda tb: pe.wait_ge(x_in[tb], 16))
            for half in range(2):
                rows_product(half, BANK, range(4 * half, 4 * half + 4), xt,
                             [psum[:, 0, :], psum[:, 2, :]], half == 0, half == 1, 0, T_MLA)
            rows_product(2, MLA_A - BANK, range(KT), xt,
                         [psum[:, 1, 0:MLA_A - BANK], psum[:, 3, 0:MLA_A - BANK]], True, True)
            pe.wait_ge(bias_src_in, 48)
            for g in range(NG + 1):
                n = 16 if g < NG else RH
                ins = mm(psum[0:n, 4 + g, 0:SPAN], table[:, 16 * g:16 * g + n], oneh[:, g, :], True, True)
            ins.then_inc(bias_made, 1)
            turn(T_MLA_C, a_rows, lambda tb: pe.wait_ge(a_copied, TB))
            pe.wait_ge(brow_out, 1)
            gq, gk = MLA_GROUP * MLA_HD, MLA_GROUP * NOPE

            def mla_gemm(at, more=0, t=None):
                c = C_MLA + 3 * at
                rows_product(c, gq, range(3), xt, [psum[:, 3, 0:gq], psum[:, 4, 0:gq]], True, True, more, t)
                if t is not None:
                    arrive(t, 4)
                kv = (xt_hi[:, 3:5, :], xt_lo[:, 3:5, :])
                rows_product(c + 1, gk, range(2), kv, [psum[:, 5, 0:gk], psum[:, 5, gk:2 * gk]], True, True, more)
                rows_product(c + 2, gk, range(2), kv, [psum[:, 6, 0:gk], psum[:, 6, gk:2 * gk]], True, True, more)

            def mla_turn(step):
                pe.wait_ge(roped, step + 1)
                for n, qk in enumerate((q_rows, k_rows)):
                    for hh in range(MLA_GROUP):
                        for tb in range(TB):
                            bank, off = 3 + 2 * n + hh // 2, (hh % 2) * SEQ + tb * P
                            ins = nc.tensor.transpose(psum[0:MLA_HD, bank, off:off + P], qk[:, tb, hh, :], ident[:, :])
                ins.then_inc(qk_turned, 1)

            def mla_scores(step):
                pe.wait_ge(q_ready, step + 1)
                pe.wait_ge(k_ready, step + 1)
                for hh in range(MLA_GROUP):
                    mm(psum[:, 0, hh * P:(hh + 1) * P], qT[:, hh, 0:P], kT[:, hh, 0:P], True, True)
                    ins = mm(flat[:, BANK + hh * SEQ:BANK + (hh + 1) * SEQ], qT[:, hh, P:SEQ], kT[:, hh, :], True, True)
                ins.then_inc(scored, 1)

            def mla_probs(step):
                pe.wait_ge(probs_ready, step + 1)
                for j in range(3 * MLA_GROUP):
                    ins = nc.tensor.transpose(flat[:, j * P:(j + 1) * P], prob0[:, j * P:(j + 1) * P], ident[:, :])
                ins.then_inc(p_turned, 1)

            def mla_sum(step, bank_free):
                pe.wait_ge(pt_ready, step + 1)
                pe.wait_ge(v_ready, step + 1)
                bank_free()
                for hh in range(MLA_GROUP):
                    rows = slice(64 * (hh % 2), 64 * (hh % 2) + 64)
                    off = (hh // 2) * SEQ
                    far = MLA_GROUP + 2 * hh
                    mm(psum[rows, 7, off:off + P], v_rows[:, 0, hh, :], probT0[:, hh, :], True, True)
                    mm(psum[rows, 7, off + P:off + SEQ], v_rows[:, 0, hh, :], probT0[:, far, :], True, False)
                    ins = mm(psum[rows, 7, off + P:off + SEQ], v_rows[:, 1, hh, :], probT0[:, far + 1, :], False, True)
                ins.then_inc(o_summed, 1)

            mla_gemm(0, 0, T_MLA_C)
            mla_turn(0)
            mla_scores(0)
            mla_gemm(1)
            mla_probs(0)
            mla_turn(1)
            mla_sum(0, lambda: None)
            with pe.Fori(0, MLA_STEPS - 2) as i:
                mla_scores(i + 1)
                mla_gemm(2, 3 * i)
                mla_probs(i + 1)
                mla_turn(i + 2)
                mla_sum(i + 1, lambda: pe.wait_ge(ot_ready, i + 1))
            last = MLA_STEPS - 1
            mla_scores(last)
            for m in range(2):
                pe.wait_ge(ot_ready, m + 1)
                wo(0, m)
            mla_probs(last)
            pe.wait_ge(ot_ready, last)
            wo(0, 2)
            mla_sum(last, lambda: None)
            pe.wait_ge(ot_ready, last + 1)
            wo(0, 3)
            tail(0)
            ple(0, T_PLE0)

            turn(T_DIL, h, block_ready(T_DIL))

            def d_tiles(u, pair0, more, first=False, t=None):
                if u == 2:
                    pe.wait_ge(dqk_copied, NG * (pair0 + more) + 1)
                elif not first:
                    pe.wait_ge(dqk_copied, NG * (pair0 + more))
                tiles_product(C_DIL + 6 * pair0 + u, u % 2, 6 * more, t)

            def d_values(n, pair0, more, first=False):
                if n == 0 and not first:
                    pe.wait_ge(d_copied, pair0 + more)
                kts = (range(0, 3), range(3, 6), range(6, 8))[n]
                rows_product(C_DIL + 6 * pair0 + 3 + n, 3 * P, kts, xt, [psum[:, 3, 0:3 * P], psum[:, 4, 0:3 * P]],
                             n == 0, n == 2, 6 * more)

            def d_scores(pair, par, hh):
                if hh == 0:
                    pe.wait_ge(dqk_copied, NG * (pair + 1))
                    pe.wait_ge(d_copied, pair + 1)
                rows = slice(64 * hh, 64 * hh + 64)
                for g in range(NG):
                    q, k = dqk[rows, par, g, 0, :], dqk[rows, par, g, 1, :]
                    mm(psum[:, 5, g * P:(g + 1) * P], q[:, 0:P], k[:, 0:P], True, True)
                    ins = mm(flat[:, 6 * BANK + g * SEQ:6 * BANK + (g + 1) * SEQ], q[:, P:SEQ], k[:, :], True, True)
                ins.then_inc(d_scored, 1)

            def d_turn(pair, hh):
                pe.wait_ge(d_probs, 2 * pair + hh + 1)
                for j in range(3 * NG):
                    ins = nc.tensor.transpose(flat[:, 5 * BANK + j * P:5 * BANK + (j + 1) * P],
                                              prob1[:, j * P:(j + 1) * P], ident[:, :])
                ins.then_inc(d_turned, 1)

            def d_values_sum(pair, par, hh, first=False):
                pe.wait_ge(d_pt, 2 * pair + hh + 1)
                if hh == 0 and not first:
                    pe.wait_ge(d_ready, pair)
                rows = slice(64 * hh, 64 * hh + 64)
                for g in range(NG):
                    mm(psum[rows, 2, 0:P], dv[:, par, 0, g, hh, :], probT1[:, g, :], g == 0, g == NG - 1)
                for g in range(NG):
                    for kb in range(2):
                        ins = mm(psum[rows, 2, P:SEQ], dv[:, par, kb, g, hh, :], probT1[:, NG + 2 * g + kb, :],
                                 g == 0 and kb == 0, g == NG - 1 and kb == 1)
                if hh == 1:
                    ins.then_inc(d_summed, 1)

            def d_step(i0, par, more, first=False):
                pair = i0 + more
                d_scores(pair, par, 0)
                d_tiles(0, i0 + 1, more)
                d_turn(pair, 0)
                d_tiles(1, i0 + 1, more)
                d_values_sum(pair, par, 0, first)
                d_scores(pair, par, 1)
                d_tiles(2, i0 + 1, more)
                d_turn(pair, 1)
                d_values(0, i0 + 1, more)
                d_values_sum(pair, par, 1)
                d_values(1, i0 + 1, more)
                d_values(2, i0 + 1, more)

            d_tiles(0, 0, 0, True, T_DIL)
            turn_r(3)
            for u in range(1, NG):
                d_tiles(u, 0, 0, True)
            for n in range(3):
                d_values(n, 0, 0, True)
            d_step(0, 0, 0, True)
            with pe.Fori(0, PAIRS // 2 - 1) as i:
                for u in range(2):
                    d_step(1 + u, 1 - u, 2 * i)
            last = PAIRS - 1
            d_scores(last, 1, 0)
            pe.wait_ge(d_ready, 2)
            wo(1, 0)
            d_turn(last, 0)
            d_values_sum(last, 1, 0)
            d_scores(last, 1, 1)
            pe.wait_ge(d_ready, 4)
            wo(1, 1)
            d_turn(last, 1)
            pe.wait_ge(d_ready, 6)
            wo(1, 2)
            d_values_sum(last, 1, 1)
            pe.wait_ge(d_ready, 8)
            wo(1, 3)
            tail(1)
            ple(1, T_PLE1)

            for l in (2, 3):
                n = l - 2
                c = C_MIX[l]
                t = (T_MIX2, T_MIX3)[n]
                turn(t, (h, t1)[n], block_ready(t))
                for b in range(3):
                    if b == 2:
                        pe.wait_ge(ret_copied, 3 * n + 1)
                    for half in range(2):
                        rows_product(c + 2 * b + half, BANK, range(4 * half, 4 * half + 4), xt,
                                     [psum[:, 2 * (b % 2) + tb, :] for tb in range(TB)], half == 0, half == 1, 0,
                                     t if b == 0 else None)
                for b in range(3):
                    tiles_product(c + 6 + b, 4 + b)
                pe.wait_ge(ret_copied, 3 * n + 2)
                for b, kts in enumerate((range(0, 3), range(3, 6), range(6, 8))):
                    rows_product(c + 9 + b, RW, kts, xt, [psum[:, 2, 0:RW], psum[:, 3, 0:RW]], b == 0, b == 2)
                pe.wait_ge(ret_roped, n + 1)
                pe.wait_ge(ret_copied, 3 * n + 3)
                pe.wait_ge(mv_copied, n + 1)
                for f in range(RH):
                    for tb in range(TB):
                        off = f * SEQ + tb * P
                        ins = nc.tensor.transpose(flat[:, off:off + P], ret[:, tb, f * P:(f + 1) * P], ident[:, :])
                ins.then_inc(ret_turned, 1)

                pe.wait_ge(mqk_copied, n + 1)
                for hh in (1, 2, 3, 4, 5, 0):
                    if hh == 0:
                        pe.wait_ge(rqk_ready, n + 1)
                    rows = slice(64 * (hh % 2), 64 * (hh % 2) + 64)
                    q, k = mqk[rows, hh // 2, 0, :], mqk[rows, hh // 2, 1, :]
                    mm(logits[:, hh, near], q[:, 0:P], k[:, 0:P], True, True)
                    ins = mm(logits[:, hh, far], q[:, P:SEQ], k, True, True)
                ins.then_inc(m_scored, 1)

                tiles_product(c + 12, 0)

                pe.wait_ge(m_maxed, n + 1)
                for hh in range(RH):
                    rows = slice(64 * (hh % 2), 64 * (hh % 2) + 64)
                    q, k = rqk[rows, hh // 2, :], rqk[rows, 3 + hh // 2, :]
                    mm(logits[:, hh, near], k[:, P:SEQ], q[:, P:SEQ], True, True)
                    ins = mm(logits[:, hh, far], k[:, 0:P], q, True, True)
                ins.then_inc(ret_scored, 1)

                tiles_product(c + 13, 1)

                pe.wait_ge(ret_decayed, n + 1)
                pe.wait_ge(cv_copied, 3 * n + 1)
                for hh in range(RH):
                    o = slice(hh * HD, (hh + 1) * HD)
                    v = [ret[:, tb, 2 * RW + hh * HD:2 * RW + (hh + 1) * HD] for tb in range(TB)]
                    mm(psum[:, 0, o], dec[:, hh, far][:, 0:P], v[0], True, True)
                    mm(psum[:, 2, o], dec[:, hh, far][:, P:SEQ], v[0], True, False)
                    ins = mm(psum[:, 2, o], dec[:, hh, near], v[1], False, True)
                ins.then_inc(ret_summed, 1)

                pe.wait_ge(m_probs, n + 1)
                for j in range(3 * RH):
                    ins = nc.tensor.transpose(probs_turned[:, j * P:(j + 1) * P], sc2[:, j // 3, (j % 3) * P:(j % 3 + 1) * P], ident[:, :])
                ins.then_inc(m_turned, 1)

                pe.wait_ge(cv_copied, 3 * n + 2)
                tiles_product(c + 14, 1)

                pe.wait_ge(m_pt, n + 1)
                for hh in range(RH):
                    rows = slice(64 * (hh % 2), 64 * (hh % 2) + 64)
                    off = 4 * BANK + (hh // 2) * SEQ
                    mm(flat[rows, off:off + P], mvr[:, 0, hh, :], probT2[:, 3 * hh, :], True, True)
                    mm(flat[rows, off + P:off + SEQ], mvr[:, 0, hh, :], probT2[:, 3 * hh + 1, :], True, False)
                    ins = mm(flat[rows, off + P:off + SEQ], mvr[:, 1, hh, :], probT2[:, 3 * hh + 2, :], False, True)
                ins.then_inc(m_summed, 1)
                t = (T_RET2, T_RET3)[n]
                turn(t, t1, block_ready(t))
                pe.wait_ge(cv_copied, 3 * n + 3)
                pe.wait_ge(cv_ready, n + 1)
                wo(l, 0)
                pe.wait_ge(m_ready, n + 1)
                wo(l, 1)
                pe.wait_ge(xt_ready, BANKS_BEFORE[t] + TURN_BANKS[t])
                wo(l, 2)
                wo(l, 3)
                tail(l)

        @block.scalar
        def _(act):
            def hi_part(c, more=0, turns=0):
                s = c % SLOTS
                act.wait_ge(landed[s], 16 * (c // SLOTS + 1) + 16 * turns)
                if c >= SLOTS:
                    act.wait_ge(chunk_used, c - SLOTS + 1 + more)
                nc.scalar.activation(w_hi[:, s, :], raw[:, s, :], ACT.Copy).then_inc(hi_split, 1)

            def ahead(c, more=0, turns=0):
                if c + 2 < CHUNKS:
                    hi_part(c + 2, more, turns)

            def turn_hi(t, dst):
                for b in range(TURN_BANKS[t]):
                    act.wait_ge(turned, BANKS_BEFORE[t] + b + 1)
                    kts = range(2 * b, min(2 * b + 2, TURN_TILES[t]))
                    bank = psum[:, turn_at(t)[b], :]
                    if t in SHIFTED:
                        if b >= 2:
                            act.wait_ge(xt_ready, BANKS_BEFORE[t] + b - 1)
                        for j, kt in enumerate(kts):
                            ins = nc.scalar.activation(staging[b % 2][:, j, :], bank[:, j * SEQ:(j + 1) * SEQ], ACT.Identity,
                                                       scale=table_of(gains, GAINED + SHIFTED, t, kt),
                                                       bias=table_of(shifts, SHIFTED, t, kt))
                    elif t in GAINED:
                        for j, kt in enumerate(kts):
                            ins = nc.scalar.activation(dst[:, kt, :], bank[:, j * SEQ:(j + 1) * SEQ], ACT.Copy,
                                                       scale=table_of(gains, GAINED + SHIFTED, t, kt))
                    else:
                        ins = nc.scalar.activation(dst[:, kts.start:kts.stop, :].rearrange("p k t -> p (k t)"),
                                                   bank[:, 0:len(kts) * SEQ], ACT.Copy)
                    ins.then_inc(turned_hi, 1)

            def squares(tb, src, col):
                nc.scalar.activation(unused[tb], src, ACT.Square, accum_out=stat[:, col:col + 1]).then_inc(squared, 1)

            def squares_y(y):
                for tb in range(TB):
                    if tb == 0:
                        act.wait_ge(y0_ready, YS.index(y) + 1)
                    else:
                        act.wait_ge(chunk_used, y_chunk(*y) + 1)
                    squares(tb, y_rows(y, tb), tb)

            def turn_hi_rms(t):
                act.wait_ge(rows_ready, rows_of(t) + 1)
                squares(0, h[:, 0, :], TB)
                turn_hi(t, xt_hi)
                act.wait_ge(rows_ready, rows_of(t) + 2)
                squares(1, h[:, 1, :], TB + 1)

            def load_gain(row, slot):
                act.dma_start(gbuf[:, slot, :], gain_rows[row:row + 1, :].to_broadcast([P, D])).then_inc(g_in[slot], 16)

            def ffn(l):
                func = ACT.Silu if l < 2 else ACT.Gelu

                def tile(u, i):
                    ahead(C_IN[l] + u, SLOTS * i, i)
                    act.wait_ge(conv_ready, l * FT + u + 1 + SLOTS * i)
                    nc.scalar.activation(gate[:, u % SLOTS, :], conv[:, u % SLOTS, :], func).then_inc(gate_ready, 1)

                full = FT // SLOTS
                with act.Fori(0, full) as i:
                    for u in range(SLOTS):
                        tile(u, i)
                for u in range(full * SLOTS, FT):
                    tile(u, 0)
                if l >= 2:
                    load_norm(2 * (l - 2) + 1)
                for m in range(FFN_OUT_N):
                    ahead(C_OUT[l] + m)

            def load_norm(count):
                act.wait_ge(h_rows, count)
                for slot in range(2):
                    load_gain(4 + 2 * count + slot, slot)

            def ple(l, t):
                turn_hi(t, xt_hi)
                for m in range(PROJ_N):
                    ahead(C_GATE[l] + m)
                act.wait_ge(chunk_used, C_PROJ[l])
                for tb in range(TB):
                    nc.scalar.activation(t1[:, tb, :], flat[:, 2 * tb * BANK:(2 * tb + 2) * BANK],
                                         ACT.Sigmoid).then_inc(sig_ready, 1)
                ahead(C_PROJ[l])

            hi_part(0)
            hi_part(1)
            for tb in range(TB):
                act.wait_ge(x_in[tb], 16)
                squares(tb, h[:, tb, :], TB + tb)
            act.wait_ge(const_in, 16 * CONSTS)
            turn_hi(T_MLA, xt_hi)
            load_gain(0, 0)
            load_gain(1, 1)
            act.wait_ge(p_in, 16)
            nc.scalar.activation(p_hi[:, :, :, :], p_raw[:, :, :, :], ACT.Copy).then_inc(p_hi_ready, 1)
            for c in range(3):
                ahead(c)
            act.wait_ge(ang_ready, 1)
            nc.scalar.activation(sin_p[:, :, :], ang[:, 0], ACT.Sin)
            nc.scalar.activation(cos_p[:, :, :], ang[:, 1], ACT.Sin).then_inc(sincos, 1)

            act.wait_ge(chunk_used, 3)
            act.wait_ge(r_ready, 1)
            for tb in range(TB):
                nc.scalar.activation(a_rows[:, tb, :], flat[:, 2 * tb * BANK:2 * tb * BANK + MLA_A], ACT.Copy,
                                     scale=rstd[:, tb:tb + 1]).then_inc(a_copied, 1)
            act.wait_ge(a_copied, TB)
            for tb in range(TB):
                nc.scalar.activation(unused[tb][:, 0:MLA_Q], a_rows[:, tb, 0:MLA_Q], ACT.Square, accum_out=stat[:, tb:tb + 1])
                nc.scalar.activation(unused[tb][:, MLA_Q:MLA_Q + MLA_KV], a_rows[:, tb, MLA_Q:MLA_Q + MLA_KV],
                                     ACT.Square, accum_out=stat[:, TB + tb:TB + tb + 1]).then_inc(squared, 1)
            act.wait_ge(bias_made, 1)
            for g in range(NG + 1):
                n = 16 if g < NG else RH
                ins = nc.scalar.activation(brow[0:n, g, :], psum[0:n, 4 + g, 0:SPAN], ACT.Copy)
            ins.then_inc(brow_out, 1)
            turn_hi(T_MLA_C, xt_hi)
            act.wait_ge(brow_out, 1)
            for g in range(NG + 1):
                n = 16 if g < NG else RH
                act.dma_start(bias_rows[16 * g:16 * g + n, :], brow[0:n, g, :]).then_inc(rows_stored, 16)
            gq, gk = MLA_GROUP * MLA_HD, MLA_GROUP * NOPE

            def mla_heads(at, more=0, turns=0, between=None):
                c = C_MLA + 3 * at
                ahead(c, more, turns)
                if between is not None:
                    between()
                act.wait_ge(chunk_used, c + 1 + more)
                for tb in range(TB):
                    nc.scalar.activation(q_rows[:, tb, :, :].rearrange("p h d -> p (h d)"), psum[:, 3 + tb, 0:gq], ACT.Copy,
                                         scale=rstd[:, 4 + tb:5 + tb])
                ahead(c + 1, more, turns)
                act.wait_ge(chunk_used, c + 2 + more)
                for tb in range(TB):
                    nc.scalar.activation(k_rows[:, tb, :, 0:NOPE],
                                         psum[:, 5, tb * gk:(tb + 1) * gk].rearrange("p (h d) -> p h d", d=NOPE), ACT.Copy,
                                         scale=rstd[:, 6 + tb:7 + tb])
                ahead(c + 2, more, turns)
                act.wait_ge(chunk_used, c + 3 + more)
                if at > 0:
                    act.wait_ge(v_ready, at + turns)
                for tb in range(TB):
                    ins = nc.scalar.activation(v_next[:, tb, :, :].rearrange("p h d -> p (h d)"),
                                               psum[:, 6, tb * gk:(tb + 1) * gk], ACT.Copy, scale=rstd[:, 6 + tb:7 + tb])
                ins.then_inc(heads_copied, 1)

            def mla_qT(step):
                act.wait_ge(qk_turned, step + 1)
                nc.scalar.activation(qT[:, :, :].rearrange("p h t -> p (h t)"), flat[0:MLA_HD, 3 * BANK:5 * BANK],
                                     ACT.Copy).then_inc(q_ready, 1)

            def mla_exp(step):
                act.wait_ge(maxed, step + 1)
                for m in range(2 * MLA_GROUP):
                    hh = m % MLA_GROUP
                    part = (slice(hh * P, (hh + 1) * P) if m < MLA_GROUP
                            else slice(MLA_GROUP * P + hh * SEQ, MLA_GROUP * P + (hh + 1) * SEQ))
                    ins = nc.scalar.activation(prob0[:, part], prob0[:, part], ACT.Exp, bias=nmax[:, m:m + 1],
                                               accum_out=rsum[:, m:m + 1])
                ins.then_inc(exped, 1)

            def mla_pT(step):
                act.wait_ge(p_turned, step + 1)
                nc.scalar.activation(probT0[:, :, :].rearrange("p j q -> p (j q)"), flat[:, 0:3 * BANK],
                                     ACT.Copy).then_inc(pt_ready, 1)

            def mla_out(step):
                act.wait_ge(o_summed, step + 1)
                nc.scalar.activation(ot_hi[:, bass.ds(2 * step, 2), :].rearrange("p j t -> p (j t)"), psum[:, 7, :],
                                     ACT.Copy).then_inc(o_hi, 1)

            act.wait_ge(ra_ready, 1)
            mla_heads(0)
            mla_qT(0)
            mla_heads(1, 0, 0, lambda: mla_exp(0))
            mla_pT(0)
            mla_qT(1)
            mla_out(0)
            with act.Fori(0, MLA_STEPS - 2) as i:
                mla_heads(2, 3 * i, i, lambda: mla_exp(i + 1))
                mla_pT(i + 1)
                mla_qT(i + 2)
                mla_out(i + 1)
            last = MLA_STEPS - 1
            mla_exp(last)
            ahead(C_WO[0])
            ahead(C_WO[0] + 1)
            mla_pT(last)
            ahead(C_WO[0] + 2)
            mla_out(last)
            ahead(C_WO[0] + 3)
            act.wait_ge(rows_stored, 16 * (NG + 1))
            toeplitz = bass.AP(tensor=bias_rows.tensor, offset=P - 1, ap=[[SPAN, heads_all], [-1, P], [1, 2 * P]])
            act.dma_start(bias_tiles, toeplitz).then_inc(tiles_stored, 16)
            squares_y(("wo", 0))
            turn_hi_rms(T_FFN0)
            load_gain(2, 0)
            ffn(0)
            squares_y(("out", 0))
            ple(0, T_PLE0)
            load_gain(3, 1)

            turn_hi_rms(T_DIL)

            def load_dbias(pair, slot):
                of_head = bias_tiles[0:NG * 16, :, :].rearrange("(g r) q k -> r q g k", g=NG)
                for hh in range(2):
                    src = of_head[pair * 2 + hh]
                    act.dma_start(dbias[:, slot, hh, 0:3 * P].rearrange("p (g k) -> p g k", g=NG),
                                  src[:, :, P:]).then_inc(dbias_in[slot], 16)
                    act.dma_start(dbias[:, slot, hh, 3 * P:].rearrange("p (g k) -> p g k", g=NG),
                                  src).then_inc(dbias_in[slot], 16)

            def d_chunk(u, pair0, more, turns):
                ahead(C_DIL + 6 * pair0 + u, 6 * more, turns)

            def d_copy(par, pair0, more):
                act.wait_ge(chunk_used, C_DIL + 6 * pair0 + 6 + 6 * more)
                for tb in range(TB):
                    ins = nc.scalar.activation(dv[:, par, tb].rearrange("p g h d -> p (g h d)"), psum[:, 3 + tb, 0:3 * P],
                                               ACT.Copy, scale=rstd[:, tb:tb + 1])
                ins.then_inc(d_copied, 1)

            def d_exp(pair, hh):
                act.wait_ge(d_maxed, 2 * pair + hh + 1)
                for qb, part in enumerate((slice(0, 3 * P), slice(3 * P, 9 * P))):
                    ins = nc.scalar.activation(prob1[:, part], prob1[:, part], ACT.Exp, bias=nmax[:, qb:qb + 1],
                                               accum_out=rsum[:, qb:qb + 1])
                ins.then_inc(d_exped, 1)

            def d_pcopy(pair, hh):
                act.wait_ge(d_turned, 2 * pair + hh + 1)
                nc.scalar.activation(probT1[:, :, :].rearrange("p j q -> p (j q)"),
                                     flat[:, 5 * BANK:5 * BANK + 9 * P], ACT.Copy).then_inc(d_pt, 1)

            def d_out(pair):
                act.wait_ge(d_summed, pair + 1)
                nc.scalar.activation(ot_hi[:, bass.ds(pair, 1), :].rearrange("p j t -> p (j t)"), psum[:, 2, 0:SEQ],
                                     ACT.Copy).then_inc(d_hi, 1)

            def d_step(i0, par, more, turns):
                pair, nxt = i0 + more, i0 + 1
                load_dbias(pair + 1, 1 - par)
                d_chunk(0, nxt, more, turns)
                d_exp(pair, 0)
                d_chunk(1, nxt, more, turns)
                d_pcopy(pair, 0)
                d_chunk(2, nxt, more, turns)
                d_exp(pair, 1)
                d_chunk(3, nxt, more, turns)
                d_pcopy(pair, 1)
                d_chunk(4, nxt, more, turns)
                d_out(pair)
                d_chunk(5, nxt, more, turns)
                d_copy(1 - par, nxt, more)

            act.wait_ge(tiles_stored, 16)
            load_dbias(0, 0)
            act.wait_ge(r_ready, 3)
            for u in range(6):
                d_chunk(u, 0, 0, 0)
            d_copy(0, 0, 0)
            d_step(0, 0, 0, 0)
            with act.Fori(0, PAIRS // 2 - 1) as i:
                for u in range(2):
                    d_step(1 + u, 1 - u, 2 * i, 4 * i)
            last = PAIRS - 1
            d_exp(last, 0)
            ahead(C_WO[1])
            d_pcopy(last, 0)
            d_exp(last, 1)
            ahead(C_WO[1] + 1)
            d_pcopy(last, 1)
            ahead(C_WO[1] + 2)
            d_out(last)
            ahead(C_WO[1] + 3)
            squares_y(("wo", 1))
            turn_hi_rms(T_FFN1)
            load_gain(4, 0)
            ffn(1)
            squares_y(("out", 1))
            ple(1, T_PLE1)
            load_gain(5, 1)

            for l in (2, 3):
                n = l - 2
                c = C_MIX[l]
                act.wait_ge(rows_ready, rows_of((T_MIX2, T_MIX3)[n]) + TB)
                m_src = bias_tiles[NG * 16:, :, :].rearrange("h q k -> q h k")
                act.dma_start(mbias[:, :, near], m_src[:, :, P:2 * P]).then_inc(mbias_in, 16)
                act.dma_start(mbias[:, :, far], m_src).then_inc(mbias_in, 16)
                act.dma_start(dec[:, :, :], decay).then_inc(dec_in, 16)
                turn_hi((T_MIX2, T_MIX3)[n], xt_hi)
                for b in range(3):
                    ahead(c + 2 * b)
                    ahead(c + 2 * b + 1)
                    act.wait_ge(chunk_used, c + 2 * b + 2)
                    src = psum[:, 2 * (b % 2):2 * (b % 2) + 2, :]
                    if b < 2:
                        ins = nc.scalar.activation(ret[:, :, b * BANK:(b + 1) * BANK], src, ACT.Copy)
                    else:
                        nc.scalar.activation(ret[:, :, 2 * BANK:3 * RW], src[:, :, 0:3 * RW - 2 * BANK], ACT.Copy)
                        ins = nc.scalar.activation(ret[:, :, 3 * RW:], src[:, :, 3 * RW - 2 * BANK:], ACT.Silu)
                    ins.then_inc(ret_copied, 1)
                for b in range(3):
                    ahead(c + 6 + b)
                    act.wait_ge(chunk_used, c + 7 + b)
                    ins = nc.scalar.activation(mqk[:, b].rearrange("p a t -> p (a t)"), psum[:, 4 + b, :], ACT.Copy)
                ins.then_inc(mqk_copied, 1)
                for b in range(3):
                    ahead(c + 9 + b)
                act.wait_ge(chunk_used, c + 12)
                nc.scalar.activation(mvr[:, :, :, :].rearrange("p b h d -> p b (h d)"), psum[:, 2:4, 0:RW],
                                     ACT.Copy).then_inc(mv_copied, 1)
                act.wait_ge(ret_turned, n + 1)
                nc.scalar.activation(rqk[:, :, :].rearrange("p f t -> p (f t)"), flat[:, 0:RH * SEQ],
                                     ACT.Copy).then_inc(rqk_ready, 1)
                ahead(c + 12)
                act.wait_ge(m_maxed, n + 1)
                for m in range(2 * RH):
                    part = sc2[:, m % RH, near if m < RH else far]
                    ins = nc.scalar.activation(part, part, ACT.Exp, bias=nmax[:, m:m + 1], accum_out=rsum[:, m:m + 1])
                ins.then_inc(m_exped, 1)

                def cv_copy(b, bank):
                    act.wait_ge(chunk_used, c + 13 + b)
                    nc.scalar.activation(cv[:, b].rearrange("p f t -> p (f t)"), psum[:, bank, :],
                                         ACT.Copy).then_inc(cv_copied, 1)

                cv_copy(0, 0)
                ahead(c + 13)
                cv_copy(1, 1)
                ahead(c + 14)
                if n == 1:
                    load_norm(2)
                act.wait_ge(m_turned, n + 1)
                nc.scalar.activation(probT2.rearrange("p j q -> p (j q)"), probs_turned, ACT.Copy).then_inc(m_pt, 1)
                cv_copy(2, 1)
                ahead(C_WO[l])
                act.wait_ge(m_summed, n + 1)
                nc.scalar.activation(ot_hi[:, 3:6, :].rearrange("p j t -> p (j t)"), flat[:, 4 * BANK:4 * BANK + 3 * SEQ],
                                     ACT.Copy).then_inc(m_hi, 1)
                turn_hi((T_RET2, T_RET3)[n], ot_hi)
                for m in range(1, PROJ_N):
                    ahead(C_WO[l] + m)
                turn_hi(T_FFN[l], xt_hi)
                ffn(l)

        @block.vector
        def _(dve):
            v = nc.vector
            steps = [0, None, 0]

            def step(ins):
                steps[0] += 1
                ins.then_inc(dve_step, 1)
                dve.wait_ge(dve_step, steps[0] if steps[1] is None else steps[0] + steps[1] * steps[2])

            @contextmanager
            def loop(n, per):
                begin = steps[0]
                with dve.Fori(0, n) as i:
                    steps[1:] = [i, per]
                    yield i
                assert steps[0] - begin == per, (steps[0] - begin, per)
                steps[0] = begin + per * n
                steps[1:] = [None, 0]

            def rsqrt(n):
                a, y, w = var[:, 0:n], rstd[:, 0:n], newton[:, 0:n]
                step(v.tensor_scalar(w.bitcast(I32), a.bitcast(I32), 1, None, ALU.logical_shift_right))
                step(v.tensor_scalar(y.bitcast(I32), w.bitcast(I32), -1, 0x5F3759DF, ALU.mult, ALU.add))
                for _ in range(3):
                    step(v.tensor_tensor(w, y, y, ALU.mult))
                    step(v.scalar_tensor_tensor(w, w, -0.5, a, ALU.mult, ALU.mult))
                    step(v.scalar_tensor_tensor(y, w, 1.5, y, ALU.add, ALU.mult))

            def rsqrt_of(cols, src, scale, eps):
                col = lambda tile, k: tile[:, k:k + 1]
                rounds = []
                for k in cols:
                    rounds.append((col(var, k), col(nhalf, k), col(newton, k), col(rstd, k), src[k]))
                for ops in range(9):
                    for n, (a, ha, w, y, s) in enumerate(rounds):
                        if ops == 0:
                            ins = v.tensor_scalar(a, s, scale, eps, ALU.mult, ALU.add)
                        elif ops == 1:
                            v.tensor_scalar(ha, a, -0.5, None, ALU.mult)
                            ins = v.tensor_scalar(w.bitcast(I32), a.bitcast(I32), 1, None, ALU.logical_shift_right)
                        elif ops == 2:
                            ins = v.tensor_scalar(y.bitcast(I32), w.bitcast(I32), -1, 0x5F3759DF, ALU.mult, ALU.add)
                        elif ops % 2 == 1:
                            ins = v.scalar_tensor_tensor(w, y, y, ha, ALU.mult, ALU.mult)
                        else:
                            ins = v.scalar_tensor_tensor(y, w, 1.5, y, ALU.add, ALU.mult)
                    if ops < 8:
                        step(ins)
                return ins

            squares = [0]

            def sums_ready():
                squares[0] += 1
                dve.wait_ge(squared, squares[0])

            def rms_r():
                sums_ready()
                sums_ready()
                rsqrt_of((0, 1), {k: stat[:, TB + k:TB + k + 1] for k in range(TB)}, 1.0 / D, RMS_EPS).then_inc(r_ready, 1)

            def r_rows(rb, count):
                dve.wait_ge(r_turned, count)
                step(v.tensor_copy(rb[:, :], psum[:, 7, 0:SEQ]))

            def add_rms_y(y, slot, load):
                dve.wait_ge(g_in[slot], 16 * load)
                for tb in range(TB):
                    sums_ready()
                    v.tensor_tensor(t1[:, tb, :], y_rows(y, tb), gbuf[:, slot, :], ALU.mult)
                    step(rsqrt_of((2 + tb,), {2 + tb: stat[:, tb:tb + 1]}, 1.0 / D, RMS_EPS))
                    v.scalar_tensor_tensor(h[:, tb, :], t1[:, tb, :], rstd[:, 2 + tb:3 + tb], h[:, tb, :],
                                           ALU.mult, ALU.add).then_inc(rows_ready, 1)

            def turn_lo(t, hi, lo):
                for b in range(TURN_BANKS[t]):
                    dve.wait_ge(turned_hi, BANKS_BEFORE[t] + b + 1)
                    kts = range(2 * b, min(2 * b + 2, TURN_TILES[t]))
                    bank = psum[:, turn_at(t)[b], :]
                    if t in SHIFTED:
                        step(v.tensor_copy(hi[:, kts.start:kts.stop, :], staging[b % 2][:, 0:2, :]))
                        ins = v.tensor_tensor(lo[:, kts.start:kts.stop, :], staging[b % 2][:, 0:2, :],
                                              hi[:, kts.start:kts.stop, :].bitcast(F32), ALU.subtract)
                    elif t in GAINED:
                        for j, kt in enumerate(kts):
                            ins = v.scalar_tensor_tensor(lo[:, kt, :], bank[:, j * SEQ:(j + 1) * SEQ],
                                                         table_of(gains, GAINED + SHIFTED, t, kt),
                                                         hi[:, kt, :].bitcast(F32), ALU.mult, ALU.subtract)
                    else:
                        tiles = lambda a: a[:, kts.start:kts.stop, :].rearrange("p k t -> p (k t)")
                        ins = v.tensor_tensor(tiles(lo), bank[:, 0:len(kts) * SEQ], tiles(hi).bitcast(F32), ALU.subtract)
                    ins.then_inc(xt_ready, 1)

            def ffn(l):
                def tile(u, i):
                    bank = psum[:, 4 + u % SLOTS, :]
                    j = u if i is None else u + SLOTS * i
                    dve.wait_ge(chunk_used, C_IN[l] + j + 1)
                    if l < 2:
                        v.tensor_tensor(conv[:, u % SLOTS, :], bank[:, 0:SEQ], rb_ffn[:, :], ALU.mult).then_inc(conv_ready, 1)
                    else:
                        cw = [fconv[:, l - 2, j, k:k + 1] if i is None else fconv[:, l - 2, bass.ds(j, 1), k:k + 1].rearrange("p a k -> p (a k)")
                              for k in range(3)]
                        s = conv[:, u % SLOTS, :]
                        step(v.tensor_scalar(s, bank[:, 0:SEQ], cw[2], None, ALU.mult))
                        step(v.scalar_tensor_tensor(s[:, 1:], bank[:, 0:SEQ - 1], cw[1], s[:, 1:], ALU.mult, ALU.add))
                        v.scalar_tensor_tensor(s[:, 2:], bank[:, 0:SEQ - 2], cw[0], s[:, 2:], ALU.mult,
                                               ALU.add).then_inc(conv_ready, 1)
                    dve.wait_ge(gate_ready, l * FT + j + 1)
                    hi = ht_hi[:, j, :] if i is None else ht_hi[:, bass.ds(j, 1), :].rearrange("p a t -> p (a t)")
                    lo = ht_lo[:, j, :] if i is None else ht_lo[:, bass.ds(j, 1), :].rearrange("p a t -> p (a t)")
                    hid = conv[:, u % SLOTS, :]
                    if l < 2:
                        step(v.tensor_tensor(hid, bank[:, SEQ:2 * SEQ], rb_ffn[:, :], ALU.mult))
                        step(v.tensor_tensor(hid, hid, gate[:, u % SLOTS, :], ALU.mult))
                    else:
                        step(v.tensor_tensor(hid, gate[:, u % SLOTS, :], bank[:, SEQ:2 * SEQ], ALU.mult))
                    step(v.tensor_copy(hi, hid))
                    v.tensor_tensor(lo, hid, hi.bitcast(F32), ALU.subtract).then_inc(hidden_ready, 1)

                full = FT // SLOTS
                with loop(full, SLOTS * (3 if l < 2 else 4)) as i:
                    for u in range(SLOTS):
                        tile(u, i)
                for u in range(full * SLOTS, FT):
                    tile(u, None)

            def ple(l, t):
                turn_lo(t, xt_hi, xt_lo)
                for tb in range(TB):
                    dve.wait_ge(sig_ready, TB * l + tb + 1)
                    if tb == 0:
                        dve.wait_ge(y0_ready, YS.index(("proj", l)) + 1)
                    else:
                        dve.wait_ge(chunk_used, C_PROJ[l] + 1)
                    step(v.tensor_tensor(t1[:, tb, :], t1[:, tb, :], flat[:, (4 + 2 * tb) * BANK:(6 + 2 * tb) * BANK], ALU.mult))
                    v.tensor_tensor(h[:, tb, :], h[:, tb, :], t1[:, tb, :], ALU.add).then_inc(rows_ready, 1)

            def layer_norm(y, last=False):
                for tb in range(TB):
                    if tb == 0:
                        dve.wait_ge(y0_ready, YS.index(y) + 1)
                    else:
                        dve.wait_ge(chunk_used, y_chunk(*y) + 1)
                    step(v.scalar_tensor_tensor(t1[:, tb, :], h[:, tb, :], ALPHA, y_rows(y, tb), ALU.mult, ALU.add))
                    v.bn_stats(bn6[:, tb, 0, :], t1[:, tb, 0:BANK])
                    step(v.bn_stats(bn6[:, tb, 1, :], t1[:, tb, BANK:]))
                    step(v.bn_aggr(mv[:, tb, :], bn6[:, tb, :, :]))
                    step(rsqrt_of((tb,), {tb: mv[:, tb, 1:2]}, 1.0, LN_EPS))
                    ins = v.tensor_scalar(t1[:, tb, :], t1[:, tb, :], mv[:, tb, 0:1], rstd[:, tb:tb + 1],
                                          ALU.subtract, ALU.mult)
                    if last:
                        step(ins)
                        norm_rows(tb).then_inc(rows_ready, 1)
                    else:
                        ins.then_inc(rows_ready, 1)

            def norm_rows(tb):
                step(v.tensor_tensor(t1[:, tb, :], t1[:, tb, :], gbuf[:, 0, :], ALU.mult))
                return v.tensor_tensor(h[:, tb, :], t1[:, tb, :], gbuf[:, 1, :], ALU.add)

            def norm_loaded(load):
                for slot in range(2):
                    dve.wait_ge(g_in[slot], 16 * load)

            def norm_after_turn(count):
                norm_loaded(count + 2)
                for tb in range(TB):
                    ins = norm_rows(tb)
                ins.then_inc(h_rows, 1)
                dve.wait_ge(h_rows, count)

            def rotate(x1, x2, cos, sin, tmp):
                v.tensor_tensor(tmp[0], x1, cos, ALU.mult)
                v.tensor_tensor(tmp[1], x2, sin, ALU.mult)
                v.tensor_tensor(tmp[2], x2, cos, ALU.mult)
                step(v.tensor_tensor(tmp[3], x1, sin, ALU.mult))
                v.tensor_tensor(x1, tmp[0], tmp[1], ALU.subtract)
                return v.tensor_tensor(x2, tmp[2], tmp[3], ALU.add)

            v.memset(table[:, :], 1.0).then_inc(table_set, 1)
            rms_r()
            dve.wait_ge(const_in, 16 * CONSTS)
            turn_lo(T_MLA, xt_hi, xt_lo)
            two_pi = 2 * math.pi
            c1 = 6.28125
            c2 = float(np.float32(np.round((two_pi - c1) * 2 ** 20) / 2 ** 20))
            c3 = float(np.float32(two_pi - c1 - c2))
            rounder = 1.5 * 2 ** 23
            step(v.tensor_copy(pos_f[:, :], pos_i[:, :]))
            for tb in range(TB):
                step(v.tensor_scalar(ang[:, 0, tb, :], inv_f[:, :], pos_f[:, tb:tb + 1], None, ALU.mult))
            step(v.tensor_scalar(ang[:, 1], ang[:, 0], 1 / two_pi, rounder, ALU.mult, ALU.add))
            step(v.tensor_scalar(ang[:, 1], ang[:, 1], rounder, None, ALU.subtract))
            for part in (c1, c2, c3):
                step(v.scalar_tensor_tensor(ang[:, 0], ang[:, 1], -part, ang[:, 0], ALU.mult, ALU.add))
            step(v.tensor_scalar(ang[:, 0], ang[:, 0], 3.1415925, -3.1415925, ALU.min, ALU.max))
            step(v.tensor_scalar(ang[:, 2], ang[:, 0], -1.0, None, ALU.mult))
            step(v.tensor_tensor(ang[:, 2], ang[:, 2], ang[:, 0], ALU.max))
            v.tensor_scalar(ang[:, 1], ang[:, 2], -1.0, math.pi / 2, ALU.mult, ALU.add).then_inc(ang_ready, 1)
            dve.wait_ge(p_hi_ready, 1)
            v.tensor_tensor(p_lo[:, :, :, :], p_raw[:, :, :, :], p_hi[:, :, :, :].bitcast(F32),
                            ALU.subtract).then_inc(p_ready, 1)

            sums_ready()
            sums_ready()
            rsqrt_of((4, 5), {4 + k: stat[:, k:k + 1] for k in range(TB)}, 1.0 / MLA_Q, RMS_EPS)
            rsqrt_of((6, 7), {6 + k: stat[:, TB + k:TB + k + 1] for k in range(TB)}, 1.0 / MLA_KV, RMS_EPS).then_inc(ra_ready, 1)
            turn_lo(T_MLA_C, xt_hi, xt_lo)
            dve.wait_ge(sincos, 1)
            half = ROPE // 2
            step(v.tensor_copy(k_rot[:, :, :], a_rows[:, :, MLA_Q + MLA_KV:]))
            step(rotate(k_rot[:, :, 0:half], k_rot[:, :, half:], cos_p[:, :, :], sin_p[:, :, :],
                        [rtmp[:, k, :, 0, :] for k in range(4)]))
            v.tensor_copy(k_rows[:, :, :, NOPE:], k_rot[:, :, :].unsqueeze(2).to_broadcast([P, TB, MLA_GROUP, ROPE]))
            near4, far4 = slice(0, MLA_GROUP * P), slice(MLA_GROUP * P, MLA_GROUP * CAUSAL_W)

            def mla_rope(at):
                heads = [P, TB, MLA_GROUP, half]
                dve.wait_ge(heads_copied, at + 1)
                rotate(q_rows[:, :, :, NOPE:NOPE + half], q_rows[:, :, :, NOPE + half:],
                       cos_p[:, :, :].unsqueeze(2).to_broadcast(heads), sin_p[:, :, :].unsqueeze(2).to_broadcast(heads),
                       [rtmp[:, k] for k in range(4)]).then_inc(roped, 1)

            def mla_kT(at):
                dve.wait_ge(qk_turned, at + 1)
                v.tensor_copy(kT[:, :, :].rearrange("p h t -> p (h t)"), flat[0:MLA_HD, 5 * BANK:7 * BANK]).then_inc(k_ready, 1)

            def mla_values(at):
                v.tensor_copy(v_rows[:, :, :, :], v_next[:, :, :, :]).then_inc(v_ready, 1)

            def mla_softmax(at):
                dve.wait_ge(scored, at + 1)
                for part, src, msk, k in ((near4, psum[:, 0, :], mask[:, 0:P], P), (far4, flat[:, BANK:3 * BANK], mask[:, P:], SEQ)):
                    ins = v.scalar_tensor_tensor(by_head(prob0[:, part], k), by_head(src, k), MLA_HD ** -0.5,
                                                 msk.unsqueeze(1).to_broadcast([P, MLA_GROUP, k]), ALU.mult, ALU.add)
                step(ins)
                v.tensor_reduce(nmax[:, 0:MLA_GROUP], by_head(prob0[:, near4], P), AX.X, ALU.max, negate=True)
                v.tensor_reduce(nmax[:, MLA_GROUP:2 * MLA_GROUP], by_head(prob0[:, far4], SEQ), AX.X, ALU.max,
                                negate=True).then_inc(maxed, 1)
                dve.wait_ge(exped, at + 1)
                step(v.reciprocal(rinv[:, 0:2 * MLA_GROUP], rsum[:, 0:2 * MLA_GROUP]))
                for n, (part, k) in enumerate(((near4, P), (far4, SEQ))):
                    inv = rinv[:, n * MLA_GROUP:(n + 1) * MLA_GROUP].unsqueeze(2).to_broadcast([P, MLA_GROUP, k])
                    ins = v.tensor_tensor(by_head(prob0[:, part], k), by_head(prob0[:, part], k), inv, ALU.mult)
                ins.then_inc(probs_ready, 1)

            def mla_out(at):
                dve.wait_ge(o_hi, at + 1)
                v.tensor_tensor(ot_lo[:, bass.ds(2 * at, 2), :].rearrange("p j t -> p (j t)"), psum[:, 7, :],
                                ot_hi[:, bass.ds(2 * at, 2), :].rearrange("p j t -> p (j t)").bitcast(F32),
                                ALU.subtract).then_inc(ot_ready, 1)

            def mla_step(at):
                mla_softmax(at)
                mla_rope(at + 1)
                mla_kT(at + 1)
                mla_out(at)
                mla_values(at + 1)

            mla_rope(0)
            mla_values(0)
            mla_kT(0)
            mla_step(0)
            with loop(MLA_STEPS - 2, 3) as i:
                mla_step(i + 1)
            mla_softmax(MLA_STEPS - 1)
            mla_out(MLA_STEPS - 1)
            add_rms_y(("wo", 0), 0, 1)
            turn_lo(T_FFN0, xt_hi, xt_lo)
            rms_r()
            r_rows(rb_ffn, 1)
            ffn(0)
            add_rms_y(("out", 0), 1, 1)
            ple(0, T_PLE0)

            turn_lo(T_DIL, xt_hi, xt_lo)
            rms_r()
            r_rows(rb_dil, 2)

            def d_qk(u, par, pair):
                dve.wait_ge(chunk_used, C_DIL + 6 * pair + u + 1)
                v.tensor_tensor(dqk[:, par, u], psum[:, u % 2, :].rearrange("p (a t) -> p a t", a=2),
                                rb_dil[:, :].unsqueeze(1).to_broadcast([P, 2, SEQ]), ALU.mult).then_inc(dqk_copied, 1)

            def d_step(pair, par, loads, ahead=True):
                dve.wait_ge(dbias_in[par], 16 * 4 * loads)
                for hh in range(2):
                    bias = dbias[:, par, hh, :]
                    dve.wait_ge(d_scored, 2 * pair + hh + 1)
                    v.scalar_tensor_tensor(prob1[:, 0:3 * P], psum[:, 5, 0:3 * P], HD ** -0.5, bias[:, 0:3 * P],
                                           ALU.mult, ALU.add)
                    step(v.scalar_tensor_tensor(prob1[:, 3 * P:], flat[:, 6 * BANK:6 * BANK + 6 * P], HD ** -0.5,
                                                bias[:, 3 * P:], ALU.mult, ALU.add))
                    v.tensor_reduce(nmax[:, 0:1], prob1[:, 0:3 * P], AX.X, ALU.max, negate=True)
                    v.tensor_reduce(nmax[:, 1:2], prob1[:, 3 * P:], AX.X, ALU.max, negate=True).then_inc(d_maxed, 1)
                    dve.wait_ge(d_exped, 2 * pair + hh + 1)
                    step(v.reciprocal(rinv[:, 0:2], rsum[:, 0:2]))
                    v.tensor_scalar(prob1[:, 0:3 * P], prob1[:, 0:3 * P], rinv[:, 0:1], None, ALU.mult)
                    v.tensor_scalar(prob1[:, 3 * P:], prob1[:, 3 * P:], rinv[:, 1:2], None, ALU.mult).then_inc(d_probs, 1)
                    if ahead:
                        for u in ((0, 1), (2,))[hh]:
                            d_qk(u, 1 - par, pair + 1)
                dve.wait_ge(d_hi, pair + 1)
                sl = bass.ds(pair, 1)
                v.tensor_tensor(ot_lo[:, sl, :].rearrange("p j t -> p (j t)"), psum[:, 2, 0:SEQ],
                                ot_hi[:, sl, :].rearrange("p j t -> p (j t)").bitcast(F32), ALU.subtract).then_inc(d_ready, 1)

            for u in range(NG):
                d_qk(u, 0, 0)
            d_step(0, 0, 1)
            with loop(PAIRS // 2 - 1, 2 * 2 * 2) as i:
                for u in range(2):
                    d_step(1 + u + 2 * i, 1 - u, 1 + u + i)
            d_step(PAIRS - 1, 1, PAIRS // 2, False)
            add_rms_y(("wo", 1), 0, 2)
            turn_lo(T_FFN1, xt_hi, xt_lo)
            rms_r()
            r_rows(rb_ffn, 3)
            ffn(1)
            add_rms_y(("out", 1), 1, 2)
            ple(1, T_PLE1)

            for l in (2, 3):
                n = l - 2
                c = C_MIX[l]
                turn_lo((T_MIX2, T_MIX3)[n], xt_hi, xt_lo)
                if n == 1:
                    norm_after_turn(2)
                dve.wait_ge(ret_copied, 3 * n + 2)
                for part in range(2):
                    qk = ret[:, :, part * RW:(part + 1) * RW].rearrange("p b (h d) -> p b h d", d=HD)
                    shape = [P, TB, RH, HD // 2]
                    size = TB * RH * HD // 2
                    tmp = [t1[:, :, :].rearrange("p b f -> p (b f)")[:, k * size:(k + 1) * size]
                           .rearrange("p (b h d) -> p b h d", b=TB, h=RH) for k in range(4)]
                    ins = rotate(qk[:, :, :, 0:HD // 2], qk[:, :, :, HD // 2:],
                                 rcos[:, :, :].unsqueeze(2).to_broadcast(shape), rsin[:, :, :].unsqueeze(2).to_broadcast(shape), tmp)
                    if part == 0:
                        step(ins)
                ins.then_inc(ret_roped, 1)
                dve.wait_ge(mbias_in, 32 * (n + 1))
                dve.wait_ge(m_scored, n + 1)
                step(v.scalar_tensor_tensor(sc2[:, :, :], logits, HD ** -0.5, mbias[:, :, :], ALU.mult, ALU.add))
                v.tensor_reduce(nmax[:, 0:RH], sc2[:, :, near], AX.X, ALU.max, negate=True)
                v.tensor_reduce(nmax[:, RH:], sc2[:, :, far], AX.X, ALU.max, negate=True).then_inc(m_maxed, 1)
                dve.wait_ge(dec_in, 16 * (n + 1))
                dve.wait_ge(ret_scored, n + 1)
                v.tensor_tensor(dec[:, :, :], logits, dec[:, :, :], ALU.mult).then_inc(ret_decayed, 1)
                dve.wait_ge(m_exped, n + 1)
                step(v.reciprocal(rinv[:, :], rsum[:, :]))
                for part, k, inv in ((near, P, rinv[:, 0:RH]), (far, SEQ, rinv[:, RH:])):
                    ins = v.tensor_tensor(sc2[:, :, part], sc2[:, :, part],
                                          inv.unsqueeze(2).to_broadcast([P, RH, k]), ALU.mult)
                ins.then_inc(m_probs, 1)
                dve.wait_ge(cv_copied, 3 * n + 2)
                prod, acc = cv[:, 0], cv[:, 1]
                step(v.tensor_tensor(prod, cv[:, 0], cv[:, 1], ALU.mult))
                for k, op in ((2, None), (1, 1), (0, 2)):
                    for f in range(2):
                        if op is None:
                            ins = v.tensor_scalar(acc[:, f, :], prod[:, f, :], mconv[:, n, f, k:k + 1], None, ALU.mult)
                        else:
                            ins = v.scalar_tensor_tensor(acc[:, f, op:], prod[:, f, 0:SEQ - op], mconv[:, n, f, k:k + 1],
                                                         acc[:, f, op:], ALU.mult, ALU.add)
                    step(ins)
                dve.wait_ge(ret_summed, n + 1)
                rows = t1[:, :, 0:RW]
                sq = t1[:, :, RW:2 * RW]
                per_head = lambda a: a.rearrange("p b (h d) -> p b h d", d=HD)
                spread = lambda s: s.rearrange("p (b h) -> p b h", b=TB).unsqueeze(3).to_broadcast([P, TB, RH, HD])
                pairs = lambda s: s.rearrange("p (b h) -> p b h", b=TB)
                one = lambda a: a.rearrange("p (h d) -> p h d", d=HD)
                o_rows = [one(psum[:, 2 * tb, 0:RW]) for tb in range(TB)]
                for tb in range(TB):
                    ins = v.tensor_reduce(mean12[:, tb * RH:(tb + 1) * RH], o_rows[tb], AX.X, ALU.add)
                step(ins)
                step(v.tensor_scalar(mean12[:, :], mean12[:, :], 1.0 / HD, None, ALU.mult))
                for tb in range(TB):
                    mean = mean12[:, tb * RH:(tb + 1) * RH].unsqueeze(2).to_broadcast([P, RH, HD])
                    ins = v.tensor_tensor(one(rows[:, tb]), o_rows[tb], mean, ALU.subtract)
                step(ins)
                step(v.tensor_tensor(sq, rows, rows, ALU.mult))
                step(v.tensor_reduce(pairs(var[:, :]), per_head(sq), AX.X, ALU.add))
                step(v.tensor_scalar(var[:, :], var[:, :], 1.0 / HD, LN_EPS, ALU.mult, ALU.add))
                rsqrt(2 * RH)
                step(v.tensor_tensor(per_head(rows), per_head(rows), spread(rstd[:, :]), ALU.mult))
                for tb in range(TB):
                    v.tensor_tensor(rows[:, tb], rows[:, tb], ret[:, tb, 3 * RW:], ALU.mult).then_inc(rows_ready, 1)
                dve.wait_ge(cv_copied, 3 * n + 3)
                step(v.tensor_tensor(acc, acc, cv[:, 2], ALU.mult))
                step(v.tensor_copy(ot_hi[:, 6:8, :], acc))
                v.tensor_tensor(ot_lo[:, 6:8, :], acc, ot_hi[:, 6:8, :].bitcast(F32), ALU.subtract).then_inc(cv_ready, 1)
                dve.wait_ge(m_hi, n + 1)
                v.tensor_tensor(ot_lo[:, 3:6, :].rearrange("p j t -> p (j t)"), flat[:, 4 * BANK:4 * BANK + 3 * SEQ],
                                ot_hi[:, 3:6, :].rearrange("p j t -> p (j t)").bitcast(F32), ALU.subtract).then_inc(m_ready, 1)
                turn_lo((T_RET2, T_RET3)[n], ot_hi, ot_lo)
                layer_norm(("wo", l))
                turn_lo(T_FFN[l], xt_hi, xt_lo)
                norm_after_turn(1 + 2 * n)
                ffn(l)
                if l == 2:
                    layer_norm(("out", l))
                else:
                    norm_loaded(6)
                    layer_norm(("out", l), True)


STAGE_WIDTHS = {name: ws for name, _, ws in STAGES}
CONSTS = 9


def bucket_rows():
    d = (2 * P - 1 - np.arange(SPAN)).astype(np.int64)
    rows = np.zeros((BUCKETS + 1, NG + 1, SPAN), np.float32)
    for g in range(NG + 1):
        far = 2048 if g < NG else 128
        if g < NG:
            window, dil = DIL[g]
            valid = (d >= 0) & (d % dil == 0) & (d <= window // dil * dil)
        else:
            valid = d >= 0
        exact = BUCKETS // 2
        n = np.maximum(d, 1).astype(np.float32)
        large = exact + (np.log(n / np.float32(exact)) / np.float32(math.log(far / exact))
                         * np.float32(BUCKETS - exact)).astype(np.int32)
        bucket = np.where(d < exact, np.maximum(d, 0), np.minimum(large, BUCKETS - 1))
        rows[bucket[valid], g, np.nonzero(valid)[0]] = 1.0
        rows[BUCKETS, g, ~valid] = NEG
    return rows


def constants():
    q, k = np.arange(P)[:, None], np.arange(P)[None, :]
    tri = np.where(k <= q, 0.0, NEG).astype(np.float32)
    causal = np.concatenate([tri, np.zeros((P, P), np.float32), tri], axis=1)
    gamma = 1.0 - 2.0 ** (-5.0 - np.arange(RH, dtype=np.float64))
    key, query = np.arange(P)[:, None, None], np.arange(SEQ)[None, None, :]
    far = np.where(query >= key, gamma[None, :, None] ** np.maximum(query - key, 0), 0.0)
    decay = (np.concatenate([far[:, :, 0:P], far], axis=2) * HD ** -0.5).astype(np.float32)
    inv = (np.float32(10000.0) ** (-np.arange(0, HD, 2, dtype=np.float32) / np.float32(HD))).astype(np.float32)
    ang = (np.arange(SEQ, dtype=np.float32)[:, None] * inv[None, :]).astype(np.float32)
    rows = lambda t: np.ascontiguousarray(t.astype(np.float32).reshape(TB, P, HD // 2).transpose(1, 0, 2))
    inv_mla = (np.float32(10000.0) ** (-np.arange(ROPE // 2, dtype=np.float32) / np.float32(ROPE // 2))).astype(np.float32)
    return {
        "causal": causal, "decay": decay, "ret_cos": rows(np.cos(ang)), "ret_sin": rows(np.sin(ang)),
        "inv_freq": np.ascontiguousarray(np.broadcast_to(inv_mla, (P, ROPE // 2))),
        "onehot": bucket_rows(), "identity": np.eye(P, dtype=np.float32),
    }


def tile(w, kts, cols):
    t = w.reshape(-1, P, w.shape[1])[kts.start:kts.stop][:, :, cols]
    return t.transpose(1, 0, 2).reshape(P, -1)


def pad(chunk, width=W):
    full = np.zeros((P, width), chunk.dtype)
    full[:, :chunk.shape[1]] = chunk
    return full


def wide(w):
    return [tile(w, range(k, k + 2), slice(0, D)) for k in range(0, w.shape[0] // P, 2)]


def paired(w, n, left, right, step=P):
    return [tile(w, range(0, KT), np.r_[left + j * step:left + j * step + P, right + j * step:right + j * step + P])
            for j in range(n)]


def by_three(w, cols):
    return [tile(w, r, cols) for r in (range(0, 3), range(3, 6), range(6, 8))]


def pack(a):
    out = {}
    wa = a["mla_w_a"][0]
    out["w_mla_a"] = [[tile(wa, range(0, 4), slice(0, BANK)), tile(wa, range(4, 8), slice(0, BANK)),
                       pad(tile(wa, range(0, KT), slice(BANK, MLA_A)))]]
    uq, ukv = a["mla_w_uq"][0], a["mla_w_ukv"][0].reshape(MLA_KV, 16, NOPE + MLA_V)
    uk = np.ascontiguousarray(ukv[:, :, :NOPE]).reshape(MLA_KV, -1)
    uv = np.ascontiguousarray(ukv[:, :, NOPE:]).reshape(MLA_KV, -1)
    nq, nk = MLA_GROUP * MLA_HD, MLA_GROUP * NOPE
    out["w_mla_heads"] = [[tile(uq, range(0, 3), slice(i * nq, (i + 1) * nq)),
                           tile(uk, range(0, 2), slice(i * nk, (i + 1) * nk)),
                           tile(uv, range(0, 2), slice(i * nk, (i + 1) * nk))] for i in range(MLA_STEPS)]
    threes = lambda chunks: [chunks[i:i + 3] for i in range(0, len(chunks) // 3 * 3, 3)]
    for l, w_o in ((0, a["mla_w_o"][0]), (1, a["dil_w_o"][0])):
        out[f"w_tail{l}"] = threes(wide(w_o) + paired(a["ffn_w_in"][l], FT, 0, D_FF) + wide(a["ffn_w_out"][l])
                                   + wide(a["ple_w_gate"][l]) + wide(a["ple_w_proj"][l]))
    wd = a["dil_w_qkv"][0]
    steps = []
    for i in range(PAIRS):
        at = lambda g, kind: (3 * g + kind) * D + i * P
        vcols = np.concatenate([np.arange(at(g, 2), at(g, 2) + P) for g in range(NG)])
        steps.append([paired(wd, 1, at(g, 0), at(g, 1))[0] for g in range(NG)] + by_three(wd, vcols))
    out["w_dil"] = steps
    for l in (2, 3):
        w = a["w_in_2"][l - 2]
        mq, cb = 4 * RW, 7 * RW
        chunks = [tile(w, range(4 * hf, 4 * hf + 4), slice(b * BANK, (b + 1) * BANK)) for b in range(3) for hf in range(2)]
        chunks += paired(w, 3, mq, mq + RW) + by_three(w, slice(mq + 2 * RW, mq + 3 * RW))
        chunks += [tile(w, range(0, KT), slice(cb + b * 2 * P, cb + (b + 1) * 2 * P)) for b in (1, 2, 0)]
        out[f"w_mix{l}"] = [chunks]
        rest = wide(a["w_out_2"][l - 2])[::-1] + paired(a["w_up_2"][l - 2], FT, 0, D_FF) + wide(a["w_down_2"][l - 2])
        out[f"w_tail{l}"] = threes(rest)
        out[f"w_tail{l}b"] = [rest[len(rest) // 3 * 3:]]
    return {name: np.stack([np.concatenate(it, axis=1) for it in its]) for name, its in out.items()}


def kernel(**inputs):
    import concourse.bacc as bacc
    from concourse.bass_utils import run_bass_kernel_spmd

    a = {name: np.asarray(v) for name, v in inputs.items()}
    feat = lambda g: g.reshape(-1, P).T
    ones = np.ones((P, KT), np.float32)
    norm_g = a["norm_g"]
    c_gain = np.concatenate([feat(a["mla_q_norm"][0]), feat(a["mla_kv_norm"][0]), ones[:, 0:3]], axis=1)
    by_turn = {T_MLA: feat(norm_g[0, 0]), T_MLA_C: c_gain, T_FFN0: feat(norm_g[0, 2]),
               T_DIL: feat(norm_g[1, 0]), T_FFN1: feat(norm_g[1, 2]),
               T_FFN2: feat(a["ln1_g_2"][0]), T_MIX3: feat(a["ln2_g_2"][0]), T_FFN3: feat(a["ln1_g_2"][1])}
    shift = {T_FFN2: feat(a["ln1_b_2"][0]), T_MIX3: feat(a["ln2_b_2"][0]), T_FFN3: feat(a["ln1_b_2"][1])}
    arrays = constants()
    arrays["x"] = a["x"][0]
    arrays["pT"] = np.ascontiguousarray(a["p"][:, 0].transpose(0, 2, 1).reshape(2, 2, P, SEQ).transpose(2, 0, 1, 3))
    arrays["positions"] = np.ascontiguousarray(a["positions"][0].reshape(TB, P).T)
    arrays["gain_fm"] = np.stack([by_turn[t] for t in GAINED + SHIFTED], axis=1)
    arrays["shift_fm"] = np.stack([shift[t] for t in SHIFTED], axis=1)
    arrays["gain_rows"] = np.stack([norm_g[0, 1], norm_g[0, 3], norm_g[1, 1], norm_g[1, 3]] + [
        a[n][l] for l in range(2) for n in ("ln1_g_2", "ln1_b_2", "ln2_g_2", "ln2_b_2")])
    arrays["rel_table"] = a["rel_bias"]
    arrays["rel_table_2"] = a["rel_bias_2"]
    arrays["ffn_conv"] = np.ascontiguousarray(a["ffn_conv_w_2"].reshape(2, 3, FT, P).transpose(3, 0, 2, 1))
    arrays["mix_conv"] = np.ascontiguousarray(a["conv_w_2"].reshape(2, 3, 2, P).transpose(3, 0, 2, 1))
    weights = pack(a)

    nc = bacc.Bacc("TRN2", target_bir_lowering=False, num_devices=1)

    def dram(name, array):
        return nc.dram_tensor(name, list(array.shape), mybir.dt.from_np(array.dtype), kind="ExternalInput").ap()

    aps = {name: dram(name, v) for name, v in arrays.items()}
    streams = {name: dram(name, v) for name, v in weights.items()}
    out = nc.dram_tensor("out", [SEQ, D], F32, kind="ExternalOutput").ap()
    build(nc, weights=streams, out=out, **aps)
    got = run_bass_kernel_spmd(nc, [{**arrays, **weights}], core_ids=[0])
    return got.results[0]["out"].reshape(1, SEQ, D)
```

```python
from contextlib import ExitStack, contextmanager
import math

import numpy as np
import concourse.bass as bass
from concourse import mybir

F32 = mybir.dt.float32
F32R = mybir.dt.float32r
I32 = mybir.dt.int32
BF16 = mybir.dt.bfloat16
ALU = mybir.AluOpType
ACT = mybir.ActivationFunctionType
AX = mybir.AxisListType

P = 128
SEQ = 256
TB = SEQ // P
D = 1024
KT = D // P
D_FF = 2816
FT = D_FF // P
BANK = 512
W = 2048
SLOTS = 3

MLA_Q, MLA_KV, NOPE, ROPE, MLA_V = 384, 256, 64, 32, 64
MLA_A = MLA_Q + MLA_KV + ROPE
MLA_HD = NOPE + ROPE
MLA_GROUP = 4
MLA_STEPS = 16 // MLA_GROUP
DIL = ((128, 1), (512, 4), (2048, 16))
NG = len(DIL)
PAIRS = 8
HD = 64
RH = 6
RW = RH * HD
BUCKETS = 32
CAUSAL_W = P + 2 * P
SPAN = 3 * P
NEG = -1e30
RMS_EPS, LN_EPS = 1e-6, 1e-5
ALPHA = 4.0 ** 0.25

MLA_WIDTHS = (3 * MLA_GROUP * MLA_HD, 2 * MLA_GROUP * NOPE, 2 * MLA_GROUP * MLA_V)
DIL_WIDTHS = (W, W, W, 3 * 384, 3 * 384, 2 * 384)
PROJ_N, FFN_OUT_N = KT // 2, FT // 2
TAIL1 = PROJ_N + FT + FFN_OUT_N + PROJ_N + 1
TAIL2 = PROJ_N + FT + FFN_OUT_N
MIX2_WIDTHS = (W,) * 9 + (3 * 384, 3 * 384, 2 * 384) + (W,) * 3
STAGES = (
    ("w_mla_a", 1, (W, W, W)),
    ("w_mla_heads", MLA_STEPS, MLA_WIDTHS),
    ("w_tail0", TAIL1 // 3, (W, W, W)),
    ("w_dil", PAIRS, DIL_WIDTHS),
    ("w_tail1", TAIL1 // 3, (W, W, W)),
    ("w_mix2", 1, MIX2_WIDTHS),
    ("w_tail2", TAIL2 // 3, (W, W, W)), ("w_tail2b", 1, (W,) * (TAIL2 % 3)),
    ("w_mix3", 1, MIX2_WIDTHS),
    ("w_tail3", TAIL2 // 3, (W, W, W)), ("w_tail3b", 1, (W,) * (TAIL2 % 3)),
)
CHUNKS = sum(n * len(ws) for _, n, ws in STAGES)
C_MLA_A = 0
C_MLA = 3
C_TAIL0 = C_MLA + MLA_STEPS * 3
C_DIL = C_TAIL0 + TAIL1
C_TAIL1 = C_DIL + PAIRS * 6
C_L2 = C_TAIL1 + TAIL1
C_L3 = C_L2 + len(MIX2_WIDTHS) + TAIL2
FIRST = (C_TAIL0, C_TAIL1, C_L2 + len(MIX2_WIDTHS), C_L3 + len(MIX2_WIDTHS))
C_WO = FIRST
C_IN = tuple(c + PROJ_N for c in FIRST)
C_OUT = tuple(c + FT for c in C_IN)
C_GATE = tuple(c + FFN_OUT_N for c in C_OUT[:2])
C_PROJ = tuple(c + PROJ_N for c in C_GATE)
C_MIX = (C_MLA_A, C_DIL, C_L2, C_L3)

TURN_TILES = (8, 5, 8, 8, 8, 8, 8, 8, 3, 8, 8, 3, 8)
(T_MLA, T_MLA_C, T_FFN0, T_PLE0, T_DIL, T_FFN1, T_PLE1,
 T_MIX2, T_RET2, T_FFN2, T_MIX3, T_RET3, T_FFN3) = range(len(TURN_TILES))
T_FFN = (T_FFN0, T_FFN1, T_FFN2, T_FFN3)
TURN_HALVES = tuple((n + 3) // 4 for n in TURN_TILES)
TURN_BANKS = tuple(TB * n for n in TURN_HALVES)
BANKS_BEFORE = tuple(sum(TURN_BANKS[:t]) for t in range(len(TURN_TILES)))
TURN_AT = {T_MLA_C: (0, 1, 2, 7), T_PLE0: (2, 3, 4, 5), T_FFN0: (7, 0, 1, 2), T_DIL: (0, 1, 2, 3), T_FFN1: (5, 6, 7, 2), T_MIX2: (0, 1, 2, 3),
           T_RET2: (6, 7), T_RET3: (6, 7)}
Y_AT = {("wo", 0): (3, 5), ("wo", 1): (0, 3), ("out", 0): (0, 6)}
FFN_AT = (3, 5, 4, 4)
R_AT = {T_FFN0: 7, T_DIL: 7, T_FFN1: 0}
BIAS_AT = (0, 1, 2, 7)
GAINED = (T_MLA, T_MLA_C, T_FFN0, T_DIL, T_FFN1)
SHIFTED = (T_FFN2, T_MIX3, T_FFN3)
SPLIT_TURNS = (T_PLE0, T_PLE1, T_MIX3)
YS = (("wo", 0), ("out", 0), ("proj", 0), ("wo", 1), ("out", 1), ("proj", 1), ("wo", 2), ("out", 2), ("wo", 3), ("out", 3))


def turn_at(t):
    return TURN_AT.get(t, (4, 5, 6, 7))


def turn_parts(t, tb):
    for k in range(TURN_HALVES[t]):
        b = tb * TURN_HALVES[t] + k
        yield b, turn_at(t)[b], range(4 * k, min(4 * k + 4, TURN_TILES[t]))


def y_at(name, l):
    return Y_AT.get((name, l), (0, 2))


def y_chunk(name, l):
    return {"wo": lambda: C_WO[l] + PROJ_N, "out": lambda: C_OUT[l] + FFN_OUT_N, "proj": lambda: C_PROJ[l] + 1}[name]() - 1


def rows_of(t):
    return TB * (t - T_FFN0)


def build(nc, x, pT, positions, inv_freq, gain_fm, shift_fm, gain_rows, onehot, rel_table, rel_table_2, causal, decay,
          ret_cos, ret_sin, ffn_conv, mix_conv, identity, weights, out):
    heads_all = NG * 16 + RH
    bias_rows = nc.dram_tensor("bias_rows", [heads_all, SPAN], F32, kind="Internal").ap()
    bias_tiles = nc.dram_tensor("bias_tiles", [heads_all, P, 2 * P], F32, kind="Internal").ap()

    ctx = ExitStack()
    with ctx:
        def sb(name, shape, dt=F32, at=ctx):
            return at.enter_context(nc.sbuf_tensor(name, shape, dt))

        def sem(name):
            return ctx.enter_context(nc.semaphore(name))

        raw = sb("raw", [P, SLOTS, W])
        w_hi = sb("w_hi", [P, SLOTS, W], F32R)
        w_lo = sb("w_lo", [P, SLOTS, W], F32R)
        h = sb("h", [P, TB, D])
        t1 = sb("t1", [P, TB, D])
        xt_hi = sb("xt_hi", [P, KT, SEQ], F32R)
        xt_lo = sb("xt_lo", [P, KT, SEQ], F32R)
        ot_hi = sb("ot_hi", [P, KT, SEQ], F32R)
        ot_lo = sb("ot_lo", [P, KT, SEQ], F32R)
        p_hi = sb("p_hi", [P, 2, 2, SEQ], F32R)
        p_lo = sb("p_lo", [P, 2, 2, SEQ], F32R)
        gbuf = sb("gbuf", [P, 2, D])
        ident = sb("ident", [P, P])
        mask = sb("mask", [P, CAUSAL_W])
        gains = sb("gains", [P, len(GAINED + SHIFTED), KT])
        shifts = sb("shifts", [P, len(SHIFTED), KT])
        fconv = sb("fconv", [P, 2, FT, 3])
        mconv = sb("mconv", [P, 2, 2, 3])
        rcos = sb("rcos", [P, TB, HD // 2])
        rsin = sb("rsin", [P, TB, HD // 2])
        pos_i = sb("pos_i", [P, TB], I32)
        pos_f = sb("pos_f", [P, TB])
        inv_f = sb("inv_f", [P, ROPE // 2])
        cos_p = sb("cos_p", [P, TB, ROPE // 2])
        sin_p = sb("sin_p", [P, TB, ROPE // 2])
        stat = sb("stat", [P, 2 * TB])
        bn6 = sb("bn6", [P, TB, 2, 6])
        mv = sb("mv", [P, TB, 2])
        var = sb("var", [P, 2 * RH])
        rstd = sb("rstd", [P, 2 * RH])
        newton = sb("newton", [P, 2 * RH])
        nhalf = sb("nhalf", [P, 8])
        mean12 = sb("mean12", [P, 2 * RH])
        nmax = sb("nmax", [P, 2 * RH])
        rsum = sb("rsum", [P, 2 * RH])
        rinv = sb("rinv", [P, 2 * RH])
        gate = sb("gate", [P, SLOTS, SEQ])
        conv = sb("conv", [P, SLOTS, SEQ])

        with ExitStack() as part:
            ht_hi = sb("ht_hi", [P, FT, SEQ], F32R, part)
            ht_lo = sb("ht_lo", [P, FT, SEQ], F32R, part)
            rb_ffn = sb("rb_ffn", [P, SEQ], F32, part)
        with ExitStack() as part:
            oneh = sb("oneh", [BUCKETS + 1, NG + 1, SPAN], F32, part)
            table = sb("table", [BUCKETS + 1, heads_all], F32, part)
            brow = sb("brow", [16, NG + 1, SPAN], F32, part)
            p_raw = sb("p_raw", [P, 2, 2, SEQ], F32, part)
            ang = sb("ang", [P, 3, TB, ROPE // 2], F32, part)
            a_rows = sb("a_rows", [P, TB, MLA_A], F32, part)
            k_rot = sb("k_rot", [P, TB, ROPE], F32, part)
            rtmp = sb("rtmp", [P, 4, TB, MLA_GROUP, ROPE // 2], F32, part)
            q_rows = sb("q_rows", [P, TB, MLA_GROUP, MLA_HD], F32, part)
            k_rows = sb("k_rows", [P, TB, MLA_GROUP, MLA_HD], F32, part)
            v_next = sb("v_next", [P, TB, MLA_GROUP, MLA_V], F32, part)
            v_rows = sb("v_rows", [P, TB, MLA_GROUP, MLA_V], F32, part)
            qT = sb("qT", [MLA_HD, MLA_GROUP, SEQ], F32, part)
            kT = sb("kT", [MLA_HD, MLA_GROUP, SEQ], F32, part)
            prob0 = sb("prob0", [P, MLA_GROUP * CAUSAL_W], F32, part)
            probT0 = sb("probT0", [P, MLA_GROUP * 3, P], F32, part)
        with ExitStack() as part:
            dqk = sb("dqk", [P, 2, NG, 2, SEQ], F32, part)
            dv = sb("dv", [P, 2, TB, NG, 2, HD], F32, part)
            dbias = sb("dbias", [P, 2, 2, 3 * NG * P], F32, part)
            prob1 = sb("prob1", [P, 3 * NG * P], F32, part)
            probT1 = sb("probT1", [P, 2, 3 * NG, P], F32, part)
            rb_dil = sb("rb_dil", [P, SEQ], F32, part)
        with ExitStack() as part:
            ret = sb("ret", [P, TB, 4 * RW], F32, part)
            rqk = sb("rqk", [P, RH, SEQ], F32, part)
            sc2 = sb("sc2", [P, RH, CAUSAL_W], F32, part)
            dec = sb("dec", [P, RH, CAUSAL_W], F32, part)
            mqk = sb("mqk", [P, RH // 2, 2, SEQ], F32, part)
            mvr = sb("mvr", [P, TB, RH, HD], F32, part)
            cv = sb("cv", [P, 3, 2, SEQ], F32, part)
            mbias = sb("mbias", [P, RH, CAUSAL_W], F32, part)
        probT2 = mbias[:, :, :].rearrange("p h k -> p (h k)").rearrange("p (j q) -> p j q", q=P)

        def by_head(a, k):
            return a.rearrange("p (h k) -> p h k", k=k)

        psum = ctx.enter_context(nc.psum_tensor("psum", [P, 8, BANK], F32))
        flat = psum[:, :, :].rearrange("p b n -> p (b n)")

        logits = psum[:, 2:2 + RH, 0:CAUSAL_W]
        near, far = slice(0, P), slice(P, CAUSAL_W)
        probs_turned = flat[:, 8 * BANK - RH * CAUSAL_W:]

        def y_rows(y, tb):
            return flat[:, y_at(*y)[tb] * BANK:y_at(*y)[tb] * BANK + D]

        staging = (gate, conv)
        unused = [s[:, :, :].rearrange("p a t -> p (a t)").bitcast(BF16)[:, 0:D] for s in staging]

        def table_of(tab, turns, t, kt):
            return tab[:, turns.index(t), kt:kt + 1]

        landed = [sem(f"landed{s}") for s in range(SLOTS)]
        hi_split = sem("hi_split")
        lo_split = sem("lo_split")
        chunk_used = sem("chunk_used")
        const_in = sem("const_in")
        p_in = sem("p_in")
        x_in = [sem(f"x{tb}_in") for tb in range(TB)]
        ident_in = sem("ident_in")
        gains_in = sem("gains_in")
        g_in = [sem("g0_in"), sem("g1_in")]
        bias_src_in = sem("bias_src_in")
        table_set = sem("table_set")
        bias_made = sem("bias_made")
        brow_out = sem("brow_out")
        rows_stored = sem("rows_stored")
        tiles_stored = sem("tiles_stored")
        dbias_in = [sem("dbias0_in"), sem("dbias1_in")]
        mbias_in = sem("mbias_in")
        dec_in = sem("dec_in")
        rows_ready = sem("rows_ready")
        y0_ready = sem("y0_ready")
        r_ready = sem("r_ready")
        r_turned = sem("r_turned")
        ra_ready = sem("ra_ready")
        v_ready = sem("v_ready")
        turned = sem("turned")
        turned_hi = sem("turned_hi")
        xt_ready = sem("xt_ready")
        squared = sem("squared")
        h_rows = sem("h_rows")
        gate_ready = sem("gate_ready")
        conv_ready = sem("conv_ready")
        hidden_ready = sem("hidden_ready")
        sig_ready = sem("sig_ready")
        p_hi_ready = sem("p_hi_ready")
        p_ready = sem("p_ready")
        a_copied = sem("a_copied")
        ang_ready = sem("ang_ready")
        sincos = sem("sincos")
        q_copied = sem("q_copied")
        heads_copied = sem("heads_copied")
        roped = sem("roped")
        qk_turned = sem("qk_turned")
        q_ready = sem("q_ready")
        k_ready = sem("k_ready")
        scored = sem("scored")
        maxed = sem("maxed")
        exped = sem("exped")
        probs_ready = sem("probs_ready")
        p_turned = sem("p_turned")
        pt_ready = sem("pt_ready")
        o_summed = sem("o_summed")
        o_hi = sem("o_hi")
        ot_ready = sem("ot_ready")
        dqk_copied = sem("dqk_copied")
        d_copied = sem("d_copied")
        d_scored = sem("d_scored")
        d_maxed = sem("d_maxed")
        d_exped = sem("d_exped")
        d_probs = sem("d_probs")
        d_turned = sem("d_turned")
        d_pt = sem("d_pt")
        d_summed = sem("d_summed")
        d_hi = sem("d_hi")
        d_ready = sem("d_ready")
        ret_copied = sem("ret_copied")
        mqk_copied = sem("mqk_copied")
        mv_copied = sem("mv_copied")
        cv_copied = sem("cv_copied")
        ret_roped = sem("ret_roped")
        ret_turned = sem("ret_turned")
        rqk_ready = sem("rqk_ready")
        ret_scored = sem("ret_scored")
        ret_decayed = sem("ret_decayed")
        ret_summed = sem("ret_summed")
        m_scored = sem("m_scored")
        m_maxed = sem("m_maxed")
        m_exped = sem("m_exped")
        m_probs = sem("m_probs")
        m_turned = sem("m_turned")
        m_pt = sem("m_pt")
        m_summed = sem("m_summed")
        m_hi = sem("m_hi")
        m_ready = sem("m_ready")
        cv_ready = sem("cv_ready")
        dve_step = sem("dve_step")
        pool_step = sem("pool_step")
        out0_ready = sem("out0_ready")
        stored = sem("stored")

        block = ctx.enter_context(nc.Block())

        @block.sync
        def _(sp):
            def load_x(tb):
                sp.dma_start(h[:, tb, :], x[tb * P:(tb + 1) * P, :]).then_inc(x_in[tb], 16)

            def stream(name, at, u, i, per, first):
                c = at + u
                width = STAGE_WIDTHS[name][u]
                off = sum(STAGE_WIDTHS[name][:u])
                if c >= SLOTS:
                    sp.wait_ge(lo_split, c - SLOTS + 1 + per * i)
                src = weights[name][first, :, off:off + width]
                sp.dma_start(raw[:, c % SLOTS, 0:width], src).then_inc(landed[c % SLOTS], 16)

            stream("w_mla_a", 0, 0, 0, 3, 0)
            load_x(0)
            sp.dma_start(ident[:, :], identity).then_inc(ident_in, 16)
            load_x(1)
            sp.dma_start(gains[:, :, :], gain_fm).then_inc(gains_in, 16)
            sp.dma_start(shifts[:, :, :], shift_fm).then_inc(gains_in, 16)
            stream("w_mla_a", 0, 1, 0, 3, 0)
            stream("w_mla_a", 0, 2, 0, 3, 0)
            for dst, src in ((inv_f[:, :], inv_freq), (pos_i[:, :], positions), (mask[:, :], causal),
                             (fconv[:, :, :, :], ffn_conv), (mconv[:, :, :, :], mix_conv),
                             (rcos[:, :, :], ret_cos), (rsin[:, :, :], ret_sin)):
                sp.dma_start(dst, src).then_inc(const_in, 16)
            sp.dma_start(p_raw[:, :, :, :], pT).then_inc(p_in, 16)
            sp.dma_start(oneh[:, :, :], onehot).then_inc(bias_src_in, 16)
            sp.wait_ge(table_set, 1)
            sp.dma_start(table[0:BUCKETS, 0:NG * 16], rel_table).then_inc(bias_src_in, 16)
            sp.dma_start(table[0:BUCKETS, NG * 16:], rel_table_2).then_inc(bias_src_in, 16)

            at = C_MLA
            for name, n, widths in STAGES[1:]:
                per = len(widths)
                if n > 1:
                    with sp.Fori(0, n) as i:
                        for u in range(per):
                            stream(name, at, u, i, per, i)
                else:
                    for u in range(per):
                        stream(name, at, u, 0, per, 0)
                at += n * per

            for tb in range(TB):
                if tb == 0:
                    sp.wait_ge(out0_ready, 1)
                else:
                    sp.wait_ge(rows_ready, rows_of(len(TURN_TILES)) + 1)
                sp.dma_start(out[tb * P:(tb + 1) * P, :], h[:, tb, :]).then_inc(stored, 16)
            sp.wait_ge(stored, 16 * TB)

        @block.gpsimd
        def _(pool):
            def lo_part(at, u, per, i, width):
                c = at + u
                s = c % SLOTS
                pool.wait_ge(hi_split, c + 1 + per * i)
                nc.gpsimd.tensor_tensor(w_lo[:, s, 0:width], raw[:, s, 0:width], w_hi[:, s, 0:width].bitcast(F32),
                                        ALU.subtract).then_inc(lo_split, 1)

            at = 0
            for name, n, widths in STAGES:
                per = len(widths)
                if n > 1:
                    with pool.Fori(0, n) as i:
                        for u, width in enumerate(widths):
                            lo_part(at, u, per, i, width)
                else:
                    for u, width in enumerate(widths):
                        lo_part(at, u, per, 0, width)
                at += n * per

            pool.wait_ge(h_rows, 4)
            for slot in range(2):
                pool.wait_ge(g_in[slot], 16 * 6)
            nc.gpsimd.tensor_tensor(t1[:, 0, :], t1[:, 0, :], gbuf[:, 0, :], ALU.mult).then_inc(pool_step, 1)
            pool.wait_ge(pool_step, 1)
            nc.gpsimd.tensor_tensor(h[:, 0, :], t1[:, 0, :], gbuf[:, 1, :], ALU.add).then_inc(out0_ready, 1)

        @block.tensor
        def _(pe):
            def mm(dst, lhsT, rhs, start, stop):
                return nc.tensor.matmul(dst, lhsT, rhs, start=start, stop=stop)

            def split_x(dst, x_hi, x_lo, hi, lo, start, stop):
                mm(dst, x_hi, hi, start, False)
                mm(dst, x_hi, lo, False, False)
                return mm(dst, x_lo, hi, False, stop)

            def split_w(dst, hi, lo, x_hi, x_lo, start, stop):
                mm(dst, hi, x_hi, start, False)
                mm(dst, hi, x_lo, False, False)
                return mm(dst, lo, x_hi, False, stop)

            def chunk(c, cols, more=0):
                pe.wait_ge(lo_split, c + 1 + more)
                s = c % SLOTS
                n = W // cols
                return (w_hi[:, s, 0:n * cols].rearrange("p (k n) -> p k n", n=cols),
                        w_lo[:, s, 0:n * cols].rearrange("p (k n) -> p k n", n=cols))

            def arrive(t, tb, kt):
                if t is not None and kt % 4 == 0:
                    pe.wait_ge(xt_ready, BANKS_BEFORE[t] + tb * TURN_HALVES[t] + kt // 4 + 1)

            def rows_product(c, cols, kts, lhs, banks, first, last, more=0, t=None):
                hi, lo = chunk(c, cols, more)
                for tb in range(TB):
                    tok = slice(tb * P, (tb + 1) * P)
                    for j, kt in enumerate(kts):
                        arrive(t, tb, kt)
                        ins = split_x(banks[tb], lhs[0][:, kt, tok], lhs[1][:, kt, tok], hi[:, j, :], lo[:, j, :],
                                      first and j == 0, last and j == len(kts) - 1)
                ins.then_inc(chunk_used, 1)

            def begin(t, src, ready, c, cols, part):
                turn_block(t, src, ready, 0)
                first = chunk(c, cols)
                part(0, *first, 0)
                turn_block(t, src, ready, 1)
                second = chunk(c + 1, cols)
                part(1, *second, 0)
                part(0, *first, 1).then_inc(chunk_used, 1)
                part(1, *second, 1).then_inc(chunk_used, 1)

            def tiles_product(c, bank, more=0, t=None):
                hi, lo = chunk(c, 2 * P, more)
                for half in range(2):
                    f = slice(half * P, (half + 1) * P)
                    for kt in range(KT):
                        if half == 0:
                            arrive(t, 0, kt)
                            arrive(t, 1, kt)
                        ins = split_w(psum[:, bank, half * SEQ:(half + 1) * SEQ], hi[:, kt, f], lo[:, kt, f],
                                      xt_hi[:, kt, :], xt_lo[:, kt, :], kt == 0, kt == KT - 1)
                ins.then_inc(chunk_used, 1)

            def wide_chunk(c, m, n, lhs, at, y=False, down=False):
                hi, lo = chunk(c + m, D)
                for tb in range(TB):
                    ins = wide_block(tb, m, hi, lo, n, lhs, at, down)
                    if y and m == n - 1 and tb == 0:
                        ins.then_inc(y0_ready, 1)
                ins.then_inc(chunk_used, 1)

            def wide_block(tb, m, hi, lo, n, lhs, at, down):
                tok = slice(tb * P, (tb + 1) * P)
                dst = [psum[:, at[tb] + nb, :] for nb in range(2)]
                col = [slice(nb * BANK, (nb + 1) * BANK) for nb in range(2)]
                for j in range(2):
                    start, stop = m + j == 0, m == n - 1 and j == 1
                    kt = 2 * (n - 1 - m if down else m) + j
                    a_hi, a_lo = lhs[0][:, kt, tok], lhs[1][:, kt, tok]
                    for nb in range(2):
                        mm(dst[nb], a_hi, hi[:, j, col[nb]], start, False)
                    for nb in range(2):
                        mm(dst[nb], a_hi, lo[:, j, col[nb]], False, False)
                    for nb in range(2):
                        ins = mm(dst[nb], a_lo, hi[:, j, col[nb]], False, stop)
                return ins

            def wide_end(c, n, lhs, at, down=False, ready=lambda k: None):
                parts = []
                for m in (n - 2, n - 1):
                    hi, lo = chunk(c + m, D)
                    ready(m - (n - 2))
                    parts.append((m, hi, lo))
                    ins = wide_block(0, m, hi, lo, n, lhs, at, down)
                ins.then_inc(y0_ready, 1)
                for m, hi, lo in parts:
                    wide_block(1, m, hi, lo, n, lhs, at, down).then_inc(chunk_used, 1)

            def turn_block(t, src, ready, tb):
                ready(tb)
                for b, bank, kts in turn_parts(t, tb):
                    for n, kt in enumerate(kts):
                        ins = nc.tensor.transpose(psum[:, bank, n * P:(n + 1) * P], src[:, tb, kt * P:(kt + 1) * P], ident[:, :])
                    ins.then_inc(turned, 1)

            def turn(t, src, ready):
                for tb in range(TB):
                    turn_block(t, src, ready, tb)

            def block_ready(t):
                return lambda tb: pe.wait_ge(rows_ready, rows_of(t) + tb + 1)

            def turn_r(count, t):
                pe.wait_ge(r_ready, count)
                for tb in range(TB):
                    ins = mm(psum[:, R_AT[t], tb * P:(tb + 1) * P], rstd[:, tb:tb + 1].to_broadcast([P, P]), ident[:, :], True, True)
                ins.then_inc(r_turned, 1)

            xt = (xt_hi, xt_lo)

            def ffn(l):
                def pair(u, i, t=None):
                    j = u
                    if u >= SLOTS:
                        pe.wait_ge(hidden_ready, l * FT + j - SLOTS + 1 + SLOTS * i)
                    tiles_product(C_IN[l] + u, FFN_AT[l] + u % SLOTS, SLOTS * i, t)

                t = T_FFN[l]
                turn(t, t1 if l >= 2 else h, block_ready(t))
                pair(0, 0, t)
                if l < 2:
                    turn_r((2, 4)[l], t)
                for u in range(1, SLOTS):
                    pair(u, 0)
                full = FT // SLOTS
                with pe.Fori(0, full - 1) as i:
                    for u in range(SLOTS):
                        pair(SLOTS + u, i)
                for u in range(full * SLOTS, FT):
                    pair(u, 0)
                for m in range(FFN_OUT_N - 2):
                    pe.wait_ge(hidden_ready, l * FT + 2 * m + 2)
                    wide_chunk(C_OUT[l], m, FFN_OUT_N, (ht_hi, ht_lo), y_at("out", l))
                pe.wait_ge(hidden_ready, l * FT + FT)
                wide_end(C_OUT[l], FFN_OUT_N, (ht_hi, ht_lo), y_at("out", l))

            def wo_end(l, ready):
                wide_end(C_WO[l], PROJ_N, (ot_hi, ot_lo), y_at("wo", l), l >= 2, ready)

            def wo(l, m):
                wide_chunk(C_WO[l], m, PROJ_N, (ot_hi, ot_lo), y_at("wo", l), True, l >= 2)

            def ple(l, t):
                def gate_part(m, hi, lo, tb):
                    arrive(t, tb, 0)
                    return wide_block(tb, m, hi, lo, PROJ_N, xt, (0, 2), False)

                begin(t, h, block_ready(t), C_GATE[l], D, gate_part)
                for m in range(2, PROJ_N):
                    arrive(t, 1, 4)
                    wide_chunk(C_GATE[l], m, PROJ_N, xt, (0, 2))
                if l == 0:
                    pe.wait_ge(p_ready, 1)
                wide_chunk(C_PROJ[l], 0, 1, (p_hi[:, l], p_lo[:, l]), (4, 6), True)
                pe.wait_ge(sig_ready, TB * (l + 1))

            pe.wait_ge(ident_in, 16)
            turn(T_MLA, h, lambda tb: pe.wait_ge(x_in[tb], 16))
            for half in range(2):
                rows_product(half, BANK, range(4 * half, 4 * half + 4), xt,
                             [psum[:, 0, :], psum[:, 2, :]], half == 0, half == 1, 0, T_MLA)
            rows_product(2, MLA_A - BANK, range(KT), xt,
                         [psum[:, 1, 0:MLA_A - BANK], psum[:, 3, 0:MLA_A - BANK]], True, True)
            turn(T_MLA_C, a_rows, lambda tb: pe.wait_ge(a_copied, TB))
            gq, gk = MLA_GROUP * MLA_HD, MLA_GROUP * NOPE

            def mla_gemm(at, more=0, t=None):
                c = C_MLA + 3 * at
                rows_product(c, gq, range(3), xt, [psum[:, 3, 0:gq], psum[:, 4, 0:gq]], True, True, more, t)
                if t is not None:
                    arrive(t, 1, 4)
                kv = (xt_hi[:, 3:5, :], xt_lo[:, 3:5, :])
                rows_product(c + 1, gk, range(2), kv, [psum[:, 5, 0:gk], psum[:, 5, gk:2 * gk]], True, True, more)
                rows_product(c + 2, gk, range(2), kv, [psum[:, 6, 0:gk], psum[:, 6, gk:2 * gk]], True, True, more)

            def mla_turn(step):
                pe.wait_ge(roped, step + 1)
                pe.wait_ge(heads_copied, step + 1)
                for n, qk in enumerate((q_rows, k_rows)):
                    for hh in range(MLA_GROUP):
                        for tb in range(TB):
                            bank, off = 3 + 2 * n + hh // 2, (hh % 2) * SEQ + tb * P
                            ins = nc.tensor.transpose(psum[0:MLA_HD, bank, off:off + P], qk[:, tb, hh, :], ident[:, :])
                ins.then_inc(qk_turned, 1)

            def mla_scores(step):
                pe.wait_ge(q_ready, step + 1)
                pe.wait_ge(k_ready, step + 1)
                for hh in range(MLA_GROUP):
                    mm(psum[:, 0, hh * P:(hh + 1) * P], qT[:, hh, 0:P], kT[:, hh, 0:P], True, True)
                    ins = mm(flat[:, BANK + hh * SEQ:BANK + (hh + 1) * SEQ], qT[:, hh, P:SEQ], kT[:, hh, :], True, True)
                ins.then_inc(scored, 1)

            def mla_probs(step):
                pe.wait_ge(probs_ready, step + 1)
                for j in range(3 * MLA_GROUP):
                    ins = nc.tensor.transpose(flat[:, j * P:(j + 1) * P], prob0[:, j * P:(j + 1) * P], ident[:, :])
                ins.then_inc(p_turned, 1)

            def mla_sum(step, bank_free):
                pe.wait_ge(pt_ready, step + 1)
                pe.wait_ge(v_ready, step + 1)
                bank_free()
                for hh in range(MLA_GROUP):
                    rows = slice(64 * (hh % 2), 64 * (hh % 2) + 64)
                    off = (hh // 2) * SEQ
                    far = MLA_GROUP + 2 * hh
                    mm(psum[rows, 7, off:off + P], v_rows[:, 0, hh, :], probT0[:, hh, :], True, True)
                    mm(psum[rows, 7, off + P:off + SEQ], v_rows[:, 0, hh, :], probT0[:, far, :], True, False)
                    ins = mm(psum[rows, 7, off + P:off + SEQ], v_rows[:, 1, hh, :], probT0[:, far + 1, :], False, True)
                ins.then_inc(o_summed, 1)

            mla_gemm(0, 0, T_MLA_C)
            pe.wait_ge(bias_src_in, 48)
            for g in range(NG + 1):
                n = 16 if g < NG else RH
                ins = mm(psum[0:n, BIAS_AT[g], 0:SPAN], table[:, 16 * g:16 * g + n], oneh[:, g, :], True, True)
            ins.then_inc(bias_made, 1)
            mla_turn(0)
            pe.wait_ge(brow_out, 1)
            mla_scores(0)
            mla_gemm(1)
            mla_probs(0)
            mla_turn(1)
            mla_sum(0, lambda: None)
            with pe.Fori(0, MLA_STEPS - 2) as i:
                mla_scores(i + 1)
                mla_gemm(2, 3 * i)
                mla_probs(i + 1)
                mla_turn(i + 2)
                mla_sum(i + 1, lambda: pe.wait_ge(ot_ready, i + 1))
            last = MLA_STEPS - 1
            mla_scores(last)
            for m in range(2):
                pe.wait_ge(ot_ready, m + 1)
                wo(0, m)
            mla_probs(last)
            pe.wait_ge(ot_ready, last)
            wo(0, 2)
            mla_sum(last, lambda: None)
            pe.wait_ge(ot_ready, last + 1)
            wo(0, 3)
            ffn(0)
            ple(0, T_PLE0)

            def d_tiles(u, pair0, more, first=False, t=None):
                if u == 2:
                    pe.wait_ge(dqk_copied, NG * (pair0 + more) + 1)
                elif not first:
                    pe.wait_ge(dqk_copied, NG * (pair0 + more))
                tiles_product(C_DIL + 6 * pair0 + u, u % 2, 6 * more, t)

            def d_values(n, pair0, more, first=False):
                if n == 0 and not first:
                    pe.wait_ge(d_copied, pair0 + more)
                kts = (range(0, 3), range(3, 6), range(6, 8))[n]
                rows_product(C_DIL + 6 * pair0 + 3 + n, 3 * P, kts, xt, [psum[:, 3, 0:3 * P], psum[:, 4, 0:3 * P]],
                             n == 0, n == 2, 6 * more)

            def d_scores(pair, par, hh):
                if hh == 0:
                    pe.wait_ge(dqk_copied, NG * (pair + 1))
                else:
                    pe.wait_ge(d_pt, 2 * pair + 1)
                rows = slice(64 * hh, 64 * hh + 64)
                for g in range(NG):
                    q, k = dqk[rows, par, g, 0, :], dqk[rows, par, g, 1, :]
                    mm(psum[:, 5, g * P:(g + 1) * P], q[:, 0:P], k[:, 0:P], True, True)
                    ins = mm(flat[:, 6 * BANK + g * SEQ:6 * BANK + (g + 1) * SEQ], q[:, P:SEQ], k[:, :], True, True)
                ins.then_inc(d_scored, 1)

            def d_turn(pair, hh):
                pe.wait_ge(d_probs, 2 * pair + hh + 1)
                for j in range(3 * NG):
                    ins = nc.tensor.transpose(flat[:, 5 * BANK + j * P:5 * BANK + (j + 1) * P],
                                              prob1[:, j * P:(j + 1) * P], ident[:, :])
                ins.then_inc(d_turned, 1)

            def d_values_sum(pair, par, first=False):
                pe.wait_ge(d_pt, 2 * pair + 2)
                pe.wait_ge(d_copied, pair + 1)
                if not first:
                    pe.wait_ge(d_ready, pair)
                for g in range(NG):
                    for hh in range(2):
                        rows = slice(64 * hh, 64 * hh + 64)
                        mm(psum[rows, 2, 0:P], dv[:, par, 0, g, hh, :], probT1[:, hh, g, :], g == 0, g == NG - 1)
                for g in range(NG):
                    for kb in range(2):
                        for hh in range(2):
                            rows = slice(64 * hh, 64 * hh + 64)
                            ins = mm(psum[rows, 2, P:SEQ], dv[:, par, kb, g, hh, :], probT1[:, hh, NG + 2 * g + kb, :],
                                     g == 0 and kb == 0, g == NG - 1 and kb == 1)
                ins.then_inc(d_summed, 1)

            def d_step(i0, par, more, first=False):
                pair = i0 + more
                d_scores(pair, par, 0)
                d_tiles(0, i0 + 1, more)
                d_turn(pair, 0)
                d_tiles(1, i0 + 1, more)
                d_scores(pair, par, 1)
                d_tiles(2, i0 + 1, more)
                d_turn(pair, 1)
                d_values(0, i0 + 1, more)
                d_values_sum(pair, par, first)
                d_values(1, i0 + 1, more)
                d_values(2, i0 + 1, more)

            turn(T_DIL, h, block_ready(T_DIL))
            d_tiles(0, 0, 0, True, T_DIL)
            turn_r(3, T_DIL)
            for u in range(1, NG):
                d_tiles(u, 0, 0, True)
            for n in range(3):
                d_values(n, 0, 0, True)
            d_step(0, 0, 0, True)
            with pe.Fori(0, PAIRS // 2 - 1) as i:
                for u in range(2):
                    d_step(1 + u, 1 - u, 2 * i)
            last = PAIRS - 1
            d_scores(last, 1, 0)
            pe.wait_ge(d_ready, 2)
            pe.wait_ge(d_copied, PAIRS)
            wo(1, 0)
            d_turn(last, 0)
            d_scores(last, 1, 1)
            pe.wait_ge(d_ready, 4)
            wo(1, 1)
            d_turn(last, 1)
            d_values_sum(last, 1)
            wo_end(1, lambda k: pe.wait_ge(d_ready, 6 + 2 * k))
            ffn(1)
            ple(1, T_PLE1)

            for l in (2, 3):
                n = l - 2
                c = C_MIX[l]
                t = (T_MIX2, T_MIX3)[n]
                def mix_part(half, hi, lo, tb):
                    arrive(t, tb, 4 * half)
                    tok = slice(tb * P, (tb + 1) * P)
                    for j in range(4):
                        kt = 4 * half + j
                        ins = split_x(psum[:, tb, :], xt_hi[:, kt, tok], xt_lo[:, kt, tok], hi[:, j, :], lo[:, j, :],
                                      kt == 0, kt == KT - 1)
                    return ins

                begin(t, (h, t1)[n], block_ready(t), c, BANK, mix_part)
                for b in range(1, 3):
                    if b == 2:
                        pe.wait_ge(ret_copied, 3 * n + 1)
                    for half in range(2):
                        rows_product(c + 2 * b + half, BANK, range(4 * half, 4 * half + 4), xt,
                                     [psum[:, 2 * (b % 2) + tb, :] for tb in range(TB)], half == 0, half == 1)
                for b in range(3):
                    tiles_product(c + 6 + b, 4 + b)
                pe.wait_ge(ret_copied, 3 * n + 2)
                for b, kts in enumerate((range(0, 3), range(3, 6), range(6, 8))):
                    rows_product(c + 9 + b, RW, kts, xt, [psum[:, 2, 0:RW], psum[:, 3, 0:RW]], b == 0, b == 2)
                pe.wait_ge(ret_roped, n + 1)
                pe.wait_ge(ret_copied, 3 * n + 3)
                pe.wait_ge(mv_copied, n + 1)
                for f in range(RH):
                    for tb in range(TB):
                        off = f * SEQ + tb * P
                        ins = nc.tensor.transpose(flat[:, off:off + P], ret[:, tb, f * P:(f + 1) * P], ident[:, :])
                ins.then_inc(ret_turned, 1)

                pe.wait_ge(mqk_copied, n + 1)
                for hh in (1, 2, 3, 4, 5, 0):
                    if hh == 0:
                        pe.wait_ge(rqk_ready, n + 1)
                    rows = slice(64 * (hh % 2), 64 * (hh % 2) + 64)
                    q, k = mqk[rows, hh // 2, 0, :], mqk[rows, hh // 2, 1, :]
                    mm(logits[:, hh, near], q[:, 0:P], k[:, 0:P], True, True)
                    ins = mm(logits[:, hh, far], q[:, P:SEQ], k, True, True)
                ins.then_inc(m_scored, 1)

                tiles_product(c + 12, 0)

                pe.wait_ge(m_maxed, n + 1)
                for hh in range(RH):
                    rows = slice(64 * (hh % 2), 64 * (hh % 2) + 64)
                    q, k = rqk[rows, hh // 2, :], rqk[rows, 3 + hh // 2, :]
                    mm(logits[:, hh, near], k[:, P:SEQ], q[:, P:SEQ], True, True)
                    ins = mm(logits[:, hh, far], k[:, 0:P], q, True, True)
                ins.then_inc(ret_scored, 1)

                tiles_product(c + 13, 1)

                pe.wait_ge(ret_decayed, n + 1)
                pe.wait_ge(cv_copied, 3 * n + 1)
                for hh in range(RH):
                    o = slice(hh * HD, (hh + 1) * HD)
                    v = [ret[:, tb, 2 * RW + hh * HD:2 * RW + (hh + 1) * HD] for tb in range(TB)]
                    mm(psum[:, 0, o], dec[:, hh, far][:, 0:P], v[0], True, True)
                    mm(psum[:, 2, o], dec[:, hh, far][:, P:SEQ], v[0], True, False)
                    ins = mm(psum[:, 2, o], dec[:, hh, near], v[1], False, True)
                ins.then_inc(ret_summed, 1)

                pe.wait_ge(m_probs, n + 1)
                for j in range(3 * RH):
                    ins = nc.tensor.transpose(probs_turned[:, j * P:(j + 1) * P], sc2[:, j // 3, (j % 3) * P:(j % 3 + 1) * P], ident[:, :])
                ins.then_inc(m_turned, 1)

                pe.wait_ge(cv_copied, 3 * n + 2)
                tiles_product(c + 14, 1)

                pe.wait_ge(m_pt, n + 1)
                for hh in range(RH):
                    rows = slice(64 * (hh % 2), 64 * (hh % 2) + 64)
                    off = 4 * BANK + (hh // 2) * SEQ
                    mm(flat[rows, off:off + P], mvr[:, 0, hh, :], probT2[:, 3 * hh, :], True, True)
                    mm(flat[rows, off + P:off + SEQ], mvr[:, 0, hh, :], probT2[:, 3 * hh + 1, :], True, False)
                    ins = mm(flat[rows, off + P:off + SEQ], mvr[:, 1, hh, :], probT2[:, 3 * hh + 2, :], False, True)
                ins.then_inc(m_summed, 1)
                t = (T_RET2, T_RET3)[n]
                turn(t, t1, block_ready(t))
                pe.wait_ge(cv_copied, 3 * n + 3)
                pe.wait_ge(cv_ready, n + 1)
                wo(l, 0)
                pe.wait_ge(m_ready, n + 1)
                wo(l, 1)
                pe.wait_ge(xt_ready, BANKS_BEFORE[t] + TURN_BANKS[t])
                wo_end(l, lambda k: None)
                ffn(l)

        @block.scalar
        def _(act):
            def hi_part(c, more=0, turns=0):
                s = c % SLOTS
                act.wait_ge(landed[s], 16 * (c // SLOTS + 1) + 16 * turns)
                if c >= SLOTS:
                    act.wait_ge(chunk_used, c - SLOTS + 1 + more)
                width = HI_WIDTHS[c]
                nc.scalar.activation(w_hi[:, s, 0:width], raw[:, s, 0:width], ACT.Copy).then_inc(hi_split, 1)

            def ahead(c, more=0, turns=0):
                if c + 2 < CHUNKS:
                    hi_part(c + 2, more, turns)

            def turn_hi_block(t, dst, tb):
                tok = slice(tb * P, (tb + 1) * P)
                for b, at, kts in turn_parts(t, tb):
                    act.wait_ge(turned, BANKS_BEFORE[t] + b + 1)
                    if t in SHIFTED and b >= 2:
                        act.wait_ge(xt_ready, BANKS_BEFORE[t] + b - 1)
                    staged = staging[b % 2][:, :, :].rearrange("p a t -> p (a t)")
                    for n, kt in enumerate(kts):
                        src = psum[:, at, n * P:(n + 1) * P]
                        if t in SHIFTED:
                            ins = nc.scalar.activation(staged[:, n * P:(n + 1) * P], src, ACT.Identity,
                                                       scale=table_of(gains, GAINED + SHIFTED, t, kt),
                                                       bias=table_of(shifts, SHIFTED, t, kt))
                        elif t in GAINED:
                            ins = nc.scalar.activation(dst[:, kt, tok], src, ACT.Copy,
                                                       scale=table_of(gains, GAINED + SHIFTED, t, kt))
                    if t not in SHIFTED + GAINED:
                        ins = nc.scalar.activation(dst[:, kts.start:kts.stop, tok],
                                                   psum[:, at, 0:len(kts) * P].rearrange("p (k t) -> p k t", t=P), ACT.Copy)
                    ins.then_inc(turned_hi, 1)

            def turn_hi(t, dst):
                for tb in range(TB):
                    turn_hi_block(t, dst, tb)

            def squares(tb, src, col):
                nc.scalar.activation(unused[tb], src, ACT.Square, accum_out=stat[:, col:col + 1]).then_inc(squared, 1)

            def squares_y(y, between=None):
                for tb in range(TB):
                    if tb == 0:
                        act.wait_ge(y0_ready, YS.index(y) + 1)
                    else:
                        if between is not None:
                            between()
                        act.wait_ge(chunk_used, y_chunk(*y) + 1)
                    squares(tb, y_rows(y, tb), tb)

            def turn_hi_rms(t):
                for tb in range(TB):
                    turn_hi_block(t, xt_hi, tb)
                    act.wait_ge(rows_ready, rows_of(t) + tb + 1)
                    squares(tb, h[:, tb, :], TB + tb)

            def load_gain(row, slot):
                act.dma_start(gbuf[:, slot, :], gain_rows[row:row + 1, :].to_broadcast([P, D])).then_inc(g_in[slot], 16)

            def ffn(l):
                func = ACT.Silu if l < 2 else ACT.Gelu

                def tile(u, i):
                    ahead(C_IN[l] + u + 1, SLOTS * i, i)
                    act.wait_ge(conv_ready, l * FT + u + 1 + SLOTS * i)
                    nc.scalar.activation(gate[:, u % SLOTS, :], conv[:, u % SLOTS, :], func).then_inc(gate_ready, 1)

                ahead(C_IN[l])
                full = FT // SLOTS
                with act.Fori(0, full) as i:
                    for u in range(SLOTS):
                        tile(u, i)
                for u in range(full * SLOTS, FT):
                    tile(u, 0)
                if l >= 2:
                    load_norm(2 * (l - 2) + 1)
                for m in range(1, FFN_OUT_N - 1):
                    ahead(C_OUT[l] + m)
                last = lambda: ahead(C_OUT[l] + FFN_OUT_N - 1)
                if l < 2:
                    squares_y(("out", l), last)
                else:
                    last()

            def load_norm(count):
                act.wait_ge(h_rows, count)
                for slot in range(2):
                    load_gain(4 + 2 * count + slot, slot)

            def ple(l, t):
                turn_hi(t, xt_hi)
                for m in range(PROJ_N):
                    ahead(C_GATE[l] + m)
                act.wait_ge(chunk_used, C_PROJ[l])
                for tb in range(TB):
                    nc.scalar.activation(t1[:, tb, :], flat[:, 2 * tb * BANK:(2 * tb + 2) * BANK],
                                         ACT.Sigmoid).then_inc(sig_ready, 1)
                ahead(C_PROJ[l])

            hi_part(0)
            act.wait_ge(gains_in, 32)
            turn_hi(T_MLA, xt_hi)
            hi_part(1)
            for tb in range(TB):
                act.wait_ge(x_in[tb], 16)
                squares(tb, h[:, tb, :], TB + tb)
            ahead(0)
            load_gain(0, 0)
            load_gain(1, 1)
            act.wait_ge(p_in, 16)
            nc.scalar.activation(p_hi[:, :, :, :], p_raw[:, :, :, :], ACT.Copy).then_inc(p_hi_ready, 1)
            for c in range(1, 3):
                ahead(c)
            act.wait_ge(ang_ready, 1)
            nc.scalar.activation(sin_p[:, :, :], ang[:, 0], ACT.Sin)
            nc.scalar.activation(cos_p[:, :, :], ang[:, 1], ACT.Sin).then_inc(sincos, 1)

            act.wait_ge(chunk_used, 3)
            act.wait_ge(r_ready, 1)
            for tb in range(TB):
                nc.scalar.activation(a_rows[:, tb, :], flat[:, 2 * tb * BANK:2 * tb * BANK + MLA_A], ACT.Copy,
                                     scale=rstd[:, tb:tb + 1]).then_inc(a_copied, 1)
            act.wait_ge(a_copied, TB)
            for tb in range(TB):
                nc.scalar.activation(unused[tb][:, 0:MLA_Q], a_rows[:, tb, 0:MLA_Q], ACT.Square, accum_out=stat[:, tb:tb + 1])
                nc.scalar.activation(unused[tb][:, MLA_Q:MLA_Q + MLA_KV], a_rows[:, tb, MLA_Q:MLA_Q + MLA_KV],
                                     ACT.Square, accum_out=stat[:, TB + tb:TB + tb + 1]).then_inc(squared, 1)
            turn_hi(T_MLA_C, xt_hi)
            gq, gk = MLA_GROUP * MLA_HD, MLA_GROUP * NOPE

            def mla_heads(at, more=0, turns=0, between=None, after=None):
                c = C_MLA + 3 * at
                ahead(c, more, turns)
                if between is not None:
                    between()
                act.wait_ge(chunk_used, c + 1 + more)
                for tb in range(TB):
                    ins = nc.scalar.activation(q_rows[:, tb, :, :].rearrange("p h d -> p (h d)"), psum[:, 3 + tb, 0:gq],
                                               ACT.Copy, scale=rstd[:, 4 + tb:5 + tb])
                ins.then_inc(q_copied, 1)
                act.wait_ge(chunk_used, c + 2 + more)
                for tb in range(TB):
                    nc.scalar.activation(k_rows[:, tb, :, 0:NOPE],
                                         psum[:, 5, tb * gk:(tb + 1) * gk].rearrange("p (h d) -> p h d", d=NOPE), ACT.Copy,
                                         scale=rstd[:, 6 + tb:7 + tb])
                act.wait_ge(chunk_used, c + 3 + more)
                if at > 0:
                    act.wait_ge(v_ready, at + turns)
                for tb in range(TB):
                    ins = nc.scalar.activation(v_next[:, tb, :, :].rearrange("p h d -> p (h d)"),
                                               psum[:, 6, tb * gk:(tb + 1) * gk], ACT.Copy, scale=rstd[:, 6 + tb:7 + tb])
                ins.then_inc(heads_copied, 1)
                if after is not None:
                    after()
                ahead(c + 1, more, turns)

            def mla_qT(step):
                act.wait_ge(qk_turned, step + 1)
                nc.scalar.activation(qT[:, :, :].rearrange("p h t -> p (h t)"), flat[0:MLA_HD, 3 * BANK:5 * BANK],
                                     ACT.Copy).then_inc(q_ready, 1)

            def mla_exp(step):
                for qb in range(2):
                    act.wait_ge(maxed, 2 * step + qb + 1)
                    for hh in range(MLA_GROUP):
                        part = (slice(hh * P, (hh + 1) * P) if qb == 0
                                else slice(MLA_GROUP * P + hh * SEQ, MLA_GROUP * P + (hh + 1) * SEQ))
                        m = qb * MLA_GROUP + hh
                        ins = nc.scalar.activation(prob0[:, part], prob0[:, part], ACT.Exp, bias=nmax[:, m:m + 1],
                                                   accum_out=rsum[:, m:m + 1])
                    ins.then_inc(exped, 1)

            def mla_pT(step):
                act.wait_ge(p_turned, step + 1)
                nc.scalar.activation(probT0[:, :, :].rearrange("p j q -> p (j q)"), flat[:, 0:3 * BANK],
                                     ACT.Copy).then_inc(pt_ready, 1)

            def mla_out(step):
                act.wait_ge(o_summed, step + 1)
                nc.scalar.activation(ot_hi[:, bass.ds(2 * step, 2), :].rearrange("p j t -> p (j t)"), psum[:, 7, :],
                                     ACT.Copy).then_inc(o_hi, 1)

            def bias_copy():
                act.wait_ge(bias_made, 1)
                for g in range(NG + 1):
                    n = 16 if g < NG else RH
                    ins = nc.scalar.activation(brow[0:n, g, :], psum[0:n, BIAS_AT[g], 0:SPAN], ACT.Copy)
                ins.then_inc(brow_out, 1)

            mla_heads(0, 0, 0, lambda: act.wait_ge(ra_ready, 1), bias_copy)
            mla_qT(0)
            ahead(C_MLA + 2)
            act.wait_ge(brow_out, 1)
            for g in range(NG + 1):
                n = 16 if g < NG else RH
                act.dma_start(bias_rows[16 * g:16 * g + n, :], brow[0:n, g, :]).then_inc(rows_stored, 16)
            mla_heads(1, 0, 0, lambda: mla_exp(0))
            mla_pT(0)
            mla_qT(1)
            ahead(C_MLA + 5)
            mla_out(0)
            with act.Fori(0, MLA_STEPS - 2) as i:
                mla_heads(2, 3 * i, i, lambda: mla_exp(i + 1))
                mla_pT(i + 1)
                mla_qT(i + 2)
                ahead(C_MLA + 8, 3 * i, i)
                mla_out(i + 1)
            last = MLA_STEPS - 1
            ahead(C_WO[0])
            mla_exp(last)
            ahead(C_WO[0] + 1)
            mla_pT(last)
            ahead(C_WO[0] + 2)
            mla_out(last)
            ahead(C_WO[0] + 3)
            act.wait_ge(rows_stored, 16 * (NG + 1))
            toeplitz = bass.AP(tensor=bias_rows.tensor, offset=P - 1, ap=[[SPAN, heads_all], [-1, P], [1, 2 * P]])
            act.dma_start(bias_tiles, toeplitz).then_inc(tiles_stored, 16)
            squares_y(("wo", 0))
            turn_hi_rms(T_FFN0)
            load_gain(2, 0)
            ffn(0)
            ple(0, T_PLE0)
            load_gain(3, 1)

            turn_hi_rms(T_DIL)

            def load_dbias(pair, slot):
                of_head = bias_tiles[0:NG * 16, :, :].rearrange("(g r) q k -> r q g k", g=NG)
                for hh in range(2):
                    src = of_head[pair * 2 + hh]
                    act.dma_start(dbias[:, slot, hh, 0:3 * P].rearrange("p (g k) -> p g k", g=NG),
                                  src[:, :, P:]).then_inc(dbias_in[slot], 16)
                    act.dma_start(dbias[:, slot, hh, 3 * P:].rearrange("p (g k) -> p g k", g=NG),
                                  src).then_inc(dbias_in[slot], 16)

            def d_chunk(u, pair0, more, turns):
                ahead(C_DIL + 6 * pair0 + u, 6 * more, turns)

            def d_copy(par, pair0, more):
                act.wait_ge(chunk_used, C_DIL + 6 * pair0 + 6 + 6 * more)
                for tb in range(TB):
                    ins = nc.scalar.activation(dv[:, par, tb].rearrange("p g h d -> p (g h d)"), psum[:, 3 + tb, 0:3 * P],
                                               ACT.Copy, scale=rstd[:, tb:tb + 1])
                ins.then_inc(d_copied, 1)

            def d_exp(pair, hh):
                for qb, part in enumerate((slice(0, 3 * P), slice(3 * P, 9 * P))):
                    act.wait_ge(d_maxed, 4 * pair + 2 * hh + qb + 1)
                    nc.scalar.activation(prob1[:, part], prob1[:, part], ACT.Exp, bias=nmax[:, qb:qb + 1],
                                         accum_out=rsum[:, qb:qb + 1]).then_inc(d_exped, 1)

            def d_pcopy(pair, hh):
                act.wait_ge(d_turned, 2 * pair + hh + 1)
                nc.scalar.activation(probT1[:, hh].rearrange("p j q -> p (j q)"),
                                     flat[:, 5 * BANK:5 * BANK + 9 * P], ACT.Copy).then_inc(d_pt, 1)

            def d_out(pair):
                act.wait_ge(d_summed, pair + 1)
                nc.scalar.activation(ot_hi[:, bass.ds(pair, 1), :].rearrange("p j t -> p (j t)"), psum[:, 2, 0:SEQ],
                                     ACT.Copy).then_inc(d_hi, 1)

            def d_step(i0, par, more, turns):
                pair, nxt = i0 + more, i0 + 1
                load_dbias(pair + 1, 1 - par)
                d_chunk(0, nxt, more, turns)
                d_exp(pair, 0)
                d_chunk(1, nxt, more, turns)
                d_pcopy(pair, 0)
                d_chunk(2, nxt, more, turns)
                d_exp(pair, 1)
                d_chunk(3, nxt, more, turns)
                d_pcopy(pair, 1)
                d_chunk(4, nxt, more, turns)
                d_out(pair)
                d_chunk(5, nxt, more, turns)
                d_copy(1 - par, nxt, more)

            act.wait_ge(tiles_stored, 16)
            load_dbias(0, 0)
            for u in range(6):
                d_chunk(u, 0, 0, 0)
            act.wait_ge(r_ready, 3)
            d_copy(0, 0, 0)
            d_step(0, 0, 0, 0)
            with act.Fori(0, PAIRS // 2 - 1) as i:
                for u in range(2):
                    d_step(1 + u, 1 - u, 2 * i, 4 * i)
            last = PAIRS - 1
            d_exp(last, 0)
            ahead(C_WO[1])
            d_pcopy(last, 0)
            ahead(C_WO[1] + 1)
            d_exp(last, 1)
            d_pcopy(last, 1)
            ahead(C_WO[1] + 2)
            d_out(last)
            squares_y(("wo", 1), lambda: ahead(C_WO[1] + 3))
            turn_hi_rms(T_FFN1)
            load_gain(4, 0)
            ffn(1)
            ple(1, T_PLE1)
            load_gain(5, 1)

            for l in (2, 3):
                n = l - 2
                c = C_MIX[l]
                turn_hi((T_MIX2, T_MIX3)[n], xt_hi)
                act.wait_ge(rows_ready, rows_of((T_MIX2, T_MIX3)[n]) + TB)
                m_src = bias_tiles[NG * 16:, :, :].rearrange("h q k -> q h k")
                act.dma_start(mbias[:, :, near], m_src[:, :, P:2 * P]).then_inc(mbias_in, 16)
                act.dma_start(mbias[:, :, far], m_src).then_inc(mbias_in, 16)
                act.dma_start(dec[:, :, :], decay).then_inc(dec_in, 16)
                for b in range(3):
                    ahead(c + 2 * b)
                    ahead(c + 2 * b + 1)
                    act.wait_ge(chunk_used, c + 2 * b + 2)
                    src = psum[:, 2 * (b % 2):2 * (b % 2) + 2, :]
                    if b < 2:
                        ins = nc.scalar.activation(ret[:, :, b * BANK:(b + 1) * BANK], src, ACT.Copy)
                    else:
                        nc.scalar.activation(ret[:, :, 2 * BANK:3 * RW], src[:, :, 0:3 * RW - 2 * BANK], ACT.Copy)
                        ins = nc.scalar.activation(ret[:, :, 3 * RW:], src[:, :, 3 * RW - 2 * BANK:], ACT.Silu)
                    ins.then_inc(ret_copied, 1)
                for b in range(3):
                    ahead(c + 6 + b)
                    act.wait_ge(chunk_used, c + 7 + b)
                    ins = nc.scalar.activation(mqk[:, b].rearrange("p a t -> p (a t)"), psum[:, 4 + b, :], ACT.Copy)
                ins.then_inc(mqk_copied, 1)
                for b in range(3):
                    ahead(c + 9 + b)
                act.wait_ge(chunk_used, c + 12)
                nc.scalar.activation(mvr[:, :, :, :].rearrange("p b h d -> p b (h d)"), psum[:, 2:4, 0:RW],
                                     ACT.Copy).then_inc(mv_copied, 1)
                act.wait_ge(ret_turned, n + 1)
                nc.scalar.activation(rqk[:, :, :].rearrange("p f t -> p (f t)"), flat[:, 0:RH * SEQ],
                                     ACT.Copy).then_inc(rqk_ready, 1)
                ahead(c + 12)
                act.wait_ge(m_maxed, n + 1)
                for m in range(2 * RH):
                    part = sc2[:, m % RH, near if m < RH else far]
                    ins = nc.scalar.activation(part, part, ACT.Exp, bias=nmax[:, m:m + 1], accum_out=rsum[:, m:m + 1])
                ins.then_inc(m_exped, 1)

                def cv_copy(b, bank):
                    act.wait_ge(chunk_used, c + 13 + b)
                    nc.scalar.activation(cv[:, b].rearrange("p f t -> p (f t)"), psum[:, bank, :],
                                         ACT.Copy).then_inc(cv_copied, 1)

                cv_copy(0, 0)
                ahead(c + 13)
                cv_copy(1, 1)
                ahead(c + 14)
                if n == 1:
                    load_norm(2)
                act.wait_ge(m_turned, n + 1)
                nc.scalar.activation(probT2.rearrange("p j q -> p (j q)"), probs_turned, ACT.Copy).then_inc(m_pt, 1)
                cv_copy(2, 1)
                ahead(C_WO[l])
                act.wait_ge(m_summed, n + 1)
                nc.scalar.activation(ot_hi[:, 3:6, :].rearrange("p j t -> p (j t)"), flat[:, 4 * BANK:4 * BANK + 3 * SEQ],
                                     ACT.Copy).then_inc(m_hi, 1)
                turn_hi((T_RET2, T_RET3)[n], ot_hi)
                for m in range(1, PROJ_N):
                    ahead(C_WO[l] + m)
                turn_hi(T_FFN[l], xt_hi)
                ffn(l)

        @block.vector
        def _(dve):
            v = nc.vector
            steps = [0, None, 0]

            def step(ins):
                steps[0] += 1
                ins.then_inc(dve_step, 1)
                dve.wait_ge(dve_step, steps[0] if steps[1] is None else steps[0] + steps[1] * steps[2])

            @contextmanager
            def loop(n, per):
                begin = steps[0]
                with dve.Fori(0, n) as i:
                    steps[1:] = [i, per]
                    yield i
                assert steps[0] - begin == per, (steps[0] - begin, per)
                steps[0] = begin + per * n
                steps[1:] = [None, 0]

            def rsqrt(n):
                a, y, w = var[:, 0:n], rstd[:, 0:n], newton[:, 0:n]
                step(v.tensor_scalar(w.bitcast(I32), a.bitcast(I32), 1, None, ALU.logical_shift_right))
                step(v.tensor_scalar(y.bitcast(I32), w.bitcast(I32), -1, 0x5F3759DF, ALU.mult, ALU.add))
                for _ in range(3):
                    step(v.tensor_tensor(w, y, y, ALU.mult))
                    step(v.scalar_tensor_tensor(w, w, -0.5, a, ALU.mult, ALU.mult))
                    step(v.scalar_tensor_tensor(y, w, 1.5, y, ALU.add, ALU.mult))

            def rsqrt_of(src, eps):
                col = lambda tile, k: tile[:, k:k + 1]
                rounds = []
                for k in src:
                    rounds.append((col(var, k), col(nhalf, k), col(newton, k), col(rstd, k), src[k]))
                for ops in range(9):
                    for n, (a, ha, w, y, s) in enumerate(rounds):
                        if ops == 0:
                            ins = v.tensor_scalar(a, s[0], s[1], eps, ALU.mult, ALU.add)
                        elif ops == 1:
                            v.tensor_scalar(ha, a, -0.5, None, ALU.mult)
                            ins = v.tensor_scalar(w.bitcast(I32), a.bitcast(I32), 1, None, ALU.logical_shift_right)
                        elif ops == 2:
                            ins = v.tensor_scalar(y.bitcast(I32), w.bitcast(I32), -1, 0x5F3759DF, ALU.mult, ALU.add)
                        elif ops % 2 == 1:
                            ins = v.scalar_tensor_tensor(w, y, y, ha, ALU.mult, ALU.mult)
                        else:
                            ins = v.scalar_tensor_tensor(y, w, 1.5, y, ALU.add, ALU.mult)
                    if ops < 8:
                        step(ins)
                return ins

            squares = [0]

            def sums_ready():
                squares[0] += 1
                dve.wait_ge(squared, squares[0])

            def rms_r():
                sums_ready()
                sums_ready()
                rsqrt_of({k: (stat[:, TB + k:TB + k + 1], 1.0 / D) for k in range(TB)}, RMS_EPS).then_inc(r_ready, 1)

            def r_rows(rb, count, t):
                dve.wait_ge(r_turned, count)
                step(v.tensor_copy(rb[:, :], psum[:, R_AT[t], 0:SEQ]))

            def turn_lo_rest(t):
                for tb in range(1 if t in SPLIT_TURNS else 0, TB):
                    turn_lo_block(t, xt_hi, xt_lo, tb)

            def add_rms_y(y, slot, load, t):
                dve.wait_ge(g_in[slot], 16 * load)
                for tb in range(TB):
                    sums_ready()
                    v.tensor_tensor(t1[:, tb, :], y_rows(y, tb), gbuf[:, slot, :], ALU.mult)
                    if tb == 1 and t in SPLIT_TURNS:
                        turn_lo_block(t, xt_hi, xt_lo, 0)
                    step(rsqrt_of({2 + tb: (stat[:, tb:tb + 1], 1.0 / D)}, RMS_EPS))
                    v.scalar_tensor_tensor(h[:, tb, :], t1[:, tb, :], rstd[:, 2 + tb:3 + tb], h[:, tb, :],
                                           ALU.mult, ALU.add).then_inc(rows_ready, 1)
                turn_lo_rest(t)

            def turn_lo_block(t, hi, lo, tb):
                tok = slice(tb * P, (tb + 1) * P)
                for b, at, kts in turn_parts(t, tb):
                    dve.wait_ge(turned_hi, BANKS_BEFORE[t] + b + 1)
                    tiles = lambda a: a[:, kts.start:kts.stop, tok]
                    wide = lambda a: a[:, 0:len(kts) * P].rearrange("p (k t) -> p k t", t=P)
                    if t in SHIFTED:
                        staged = wide(staging[b % 2][:, :, :].rearrange("p a t -> p (a t)"))
                        step(v.tensor_copy(tiles(hi), staged))
                        ins = v.tensor_tensor(tiles(lo), staged, tiles(hi).bitcast(F32), ALU.subtract)
                    elif t in GAINED:
                        for n, kt in enumerate(kts):
                            ins = v.scalar_tensor_tensor(lo[:, kt, tok], psum[:, at, n * P:(n + 1) * P],
                                                         table_of(gains, GAINED + SHIFTED, t, kt),
                                                         hi[:, kt, tok].bitcast(F32), ALU.mult, ALU.subtract)
                    else:
                        ins = v.tensor_tensor(tiles(lo), wide(psum[:, at, :]), tiles(hi).bitcast(F32), ALU.subtract)
                    ins.then_inc(xt_ready, 1)

            def turn_lo(t, hi, lo):
                for tb in range(TB):
                    turn_lo_block(t, hi, lo, tb)

            def ffn(l):
                def tile(u, i):
                    bank = psum[:, FFN_AT[l] + u % SLOTS, :]
                    j = u if i is None else u + SLOTS * i
                    dve.wait_ge(chunk_used, C_IN[l] + j + 1)
                    if l < 2:
                        v.tensor_tensor(conv[:, u % SLOTS, :], bank[:, 0:SEQ], rb_ffn[:, :], ALU.mult).then_inc(conv_ready, 1)
                    else:
                        cw = [fconv[:, l - 2, j, k:k + 1] if i is None else fconv[:, l - 2, bass.ds(j, 1), k:k + 1].rearrange("p a k -> p (a k)")
                              for k in range(3)]
                        s = conv[:, u % SLOTS, :]
                        step(v.tensor_scalar(s, bank[:, 0:SEQ], cw[2], None, ALU.mult))
                        step(v.scalar_tensor_tensor(s[:, 1:], bank[:, 0:SEQ - 1], cw[1], s[:, 1:], ALU.mult, ALU.add))
                        v.scalar_tensor_tensor(s[:, 2:], bank[:, 0:SEQ - 2], cw[0], s[:, 2:], ALU.mult,
                                               ALU.add).then_inc(conv_ready, 1)
                    dve.wait_ge(gate_ready, l * FT + j + 1)
                    hi = ht_hi[:, j, :] if i is None else ht_hi[:, bass.ds(j, 1), :].rearrange("p a t -> p (a t)")
                    lo = ht_lo[:, j, :] if i is None else ht_lo[:, bass.ds(j, 1), :].rearrange("p a t -> p (a t)")
                    hid = conv[:, u % SLOTS, :]
                    if l < 2:
                        step(v.tensor_tensor(hid, bank[:, SEQ:2 * SEQ], rb_ffn[:, :], ALU.mult))
                        step(v.tensor_tensor(hid, hid, gate[:, u % SLOTS, :], ALU.mult))
                    else:
                        step(v.tensor_tensor(hid, gate[:, u % SLOTS, :], bank[:, SEQ:2 * SEQ], ALU.mult))
                    step(v.tensor_copy(hi, hid))
                    v.tensor_tensor(lo, hid, hi.bitcast(F32), ALU.subtract).then_inc(hidden_ready, 1)

                full = FT // SLOTS
                with loop(full, SLOTS * (3 if l < 2 else 4)) as i:
                    for u in range(SLOTS):
                        tile(u, i)
                for u in range(full * SLOTS, FT):
                    tile(u, None)

            def ple(l):
                for tb in range(TB):
                    dve.wait_ge(sig_ready, TB * l + tb + 1)
                    if tb == 0:
                        dve.wait_ge(y0_ready, YS.index(("proj", l)) + 1)
                    else:
                        dve.wait_ge(chunk_used, C_PROJ[l] + 1)
                    step(v.tensor_tensor(t1[:, tb, :], t1[:, tb, :], flat[:, (4 + 2 * tb) * BANK:(6 + 2 * tb) * BANK], ALU.mult))
                    v.tensor_tensor(h[:, tb, :], h[:, tb, :], t1[:, tb, :], ALU.add).then_inc(rows_ready, 1)

            def layer_norm(y, t=None):
                last = t is None
                for tb in range(TB):
                    if tb == 0:
                        dve.wait_ge(y0_ready, YS.index(y) + 1)
                    else:
                        dve.wait_ge(chunk_used, y_chunk(*y) + 1)
                    step(v.scalar_tensor_tensor(t1[:, tb, :], h[:, tb, :], ALPHA, y_rows(y, tb), ALU.mult, ALU.add))
                    v.bn_stats(bn6[:, tb, 0, :], t1[:, tb, 0:BANK])
                    step(v.bn_stats(bn6[:, tb, 1, :], t1[:, tb, BANK:]))
                    step(v.bn_aggr(mv[:, tb, :], bn6[:, tb, :, :]))
                    if tb == 1 and t in SPLIT_TURNS:
                        turn_lo_block(t, xt_hi, xt_lo, 0)
                    step(rsqrt_of({tb: (mv[:, tb, 1:2], 1.0)}, LN_EPS))
                    ins = v.tensor_scalar(t1[:, tb, :], t1[:, tb, :], mv[:, tb, 0:1], rstd[:, tb:tb + 1],
                                          ALU.subtract, ALU.mult)
                    if last and tb == 0:
                        ins.then_inc(h_rows, 1)
                    elif last:
                        step(ins)
                        norm_rows(tb).then_inc(rows_ready, 1)
                    else:
                        ins.then_inc(rows_ready, 1)
                if not last:
                    turn_lo_rest(t)

            def norm_rows(tb):
                step(v.tensor_tensor(t1[:, tb, :], t1[:, tb, :], gbuf[:, 0, :], ALU.mult))
                return v.tensor_tensor(h[:, tb, :], t1[:, tb, :], gbuf[:, 1, :], ALU.add)

            def norm_loaded(load):
                for slot in range(2):
                    dve.wait_ge(g_in[slot], 16 * load)

            def norm_after_turn(count):
                norm_loaded(count + 2)
                for tb in range(TB):
                    ins = norm_rows(tb)
                ins.then_inc(h_rows, 1)
                dve.wait_ge(h_rows, count)

            def rotate(x1, x2, cos, sin, tmp):
                v.tensor_tensor(tmp[0], x1, cos, ALU.mult)
                v.tensor_tensor(tmp[1], x2, sin, ALU.mult)
                v.tensor_tensor(tmp[2], x2, cos, ALU.mult)
                step(v.tensor_tensor(tmp[3], x1, sin, ALU.mult))
                v.tensor_tensor(x1, tmp[0], tmp[1], ALU.subtract)
                return v.tensor_tensor(x2, tmp[2], tmp[3], ALU.add)

            v.memset(table[:, :], 1.0).then_inc(table_set, 1)
            dve.wait_ge(gains_in, 32)
            turn_lo(T_MLA, xt_hi, xt_lo)
            rms_r()
            dve.wait_ge(const_in, 16 * CONSTS)
            two_pi = 2 * math.pi
            c1 = 6.28125
            c2 = float(np.float32(np.round((two_pi - c1) * 2 ** 20) / 2 ** 20))
            c3 = float(np.float32(two_pi - c1 - c2))
            rounder = 1.5 * 2 ** 23
            step(v.tensor_copy(pos_f[:, :], pos_i[:, :]))
            for tb in range(TB):
                step(v.tensor_scalar(ang[:, 0, tb, :], inv_f[:, :], pos_f[:, tb:tb + 1], None, ALU.mult))
            step(v.tensor_scalar(ang[:, 1], ang[:, 0], 1 / two_pi, rounder, ALU.mult, ALU.add))
            step(v.tensor_scalar(ang[:, 1], ang[:, 1], rounder, None, ALU.subtract))
            for part in (c1, c2, c3):
                step(v.scalar_tensor_tensor(ang[:, 0], ang[:, 1], -part, ang[:, 0], ALU.mult, ALU.add))
            step(v.tensor_scalar(ang[:, 0], ang[:, 0], 3.1415925, -3.1415925, ALU.min, ALU.max))
            step(v.tensor_scalar(ang[:, 2], ang[:, 0], -1.0, None, ALU.mult))
            step(v.tensor_tensor(ang[:, 2], ang[:, 2], ang[:, 0], ALU.max))
            v.tensor_scalar(ang[:, 1], ang[:, 2], -1.0, math.pi / 2, ALU.mult, ALU.add).then_inc(ang_ready, 1)
            dve.wait_ge(p_hi_ready, 1)
            v.tensor_tensor(p_lo[:, :, :, :], p_raw[:, :, :, :], p_hi[:, :, :, :].bitcast(F32),
                            ALU.subtract).then_inc(p_ready, 1)

            turn_lo(T_MLA_C, xt_hi, xt_lo)
            sums_ready()
            sums_ready()
            rsqrt_of({4 + k: (stat[:, k:k + 1], 1.0 / (MLA_Q if k < TB else MLA_KV)) for k in range(2 * TB)},
                     RMS_EPS).then_inc(ra_ready, 1)
            dve.wait_ge(sincos, 1)
            half = ROPE // 2
            step(v.tensor_copy(k_rot[:, :, :], a_rows[:, :, MLA_Q + MLA_KV:]))
            step(rotate(k_rot[:, :, 0:half], k_rot[:, :, half:], cos_p[:, :, :], sin_p[:, :, :],
                        [rtmp[:, k, :, 0, :] for k in range(4)]))
            v.tensor_copy(k_rows[:, :, :, NOPE:], k_rot[:, :, :].unsqueeze(2).to_broadcast([P, TB, MLA_GROUP, ROPE]))
            near4, far4 = slice(0, MLA_GROUP * P), slice(MLA_GROUP * P, MLA_GROUP * CAUSAL_W)

            def mla_rope(at):
                heads = [P, TB, MLA_GROUP, half]
                dve.wait_ge(q_copied, at + 1)
                rotate(q_rows[:, :, :, NOPE:NOPE + half], q_rows[:, :, :, NOPE + half:],
                       cos_p[:, :, :].unsqueeze(2).to_broadcast(heads), sin_p[:, :, :].unsqueeze(2).to_broadcast(heads),
                       [rtmp[:, k] for k in range(4)]).then_inc(roped, 1)

            def mla_kT(at):
                dve.wait_ge(qk_turned, at + 1)
                v.tensor_copy(kT[:, :, :].rearrange("p h t -> p (h t)"), flat[0:MLA_HD, 5 * BANK:7 * BANK]).then_inc(k_ready, 1)

            def mla_values(at):
                dve.wait_ge(heads_copied, at + 1)
                v.tensor_copy(v_rows[:, :, :, :], v_next[:, :, :, :]).then_inc(v_ready, 1)

            def mla_softmax(at):
                dve.wait_ge(scored, at + 1)
                parts = ((near4, psum[:, 0, :], mask[:, 0:P], P), (far4, flat[:, BANK:3 * BANK], mask[:, P:], SEQ))
                of = lambda tile, qb: tile[:, qb * MLA_GROUP:(qb + 1) * MLA_GROUP]
                for qb, (part, src, msk, k) in enumerate(parts):
                    step(v.scalar_tensor_tensor(by_head(prob0[:, part], k), by_head(src, k), MLA_HD ** -0.5,
                                                msk.unsqueeze(1).to_broadcast([P, MLA_GROUP, k]), ALU.mult, ALU.add))
                    v.tensor_reduce(of(nmax, qb), by_head(prob0[:, part], k), AX.X, ALU.max, negate=True).then_inc(maxed, 1)
                for qb, (part, src, msk, k) in enumerate(parts):
                    dve.wait_ge(exped, 2 * at + qb + 1)
                    step(v.reciprocal(of(rinv, qb), of(rsum, qb)))
                    inv = of(rinv, qb).unsqueeze(2).to_broadcast([P, MLA_GROUP, k])
                    ins = v.tensor_tensor(by_head(prob0[:, part], k), by_head(prob0[:, part], k), inv, ALU.mult)
                ins.then_inc(probs_ready, 1)

            def mla_out(at):
                dve.wait_ge(o_hi, at + 1)
                v.tensor_tensor(ot_lo[:, bass.ds(2 * at, 2), :].rearrange("p j t -> p (j t)"), psum[:, 7, :],
                                ot_hi[:, bass.ds(2 * at, 2), :].rearrange("p j t -> p (j t)").bitcast(F32),
                                ALU.subtract).then_inc(ot_ready, 1)

            def mla_step(at):
                mla_softmax(at)
                mla_rope(at + 1)
                mla_kT(at + 1)
                mla_out(at)
                mla_values(at + 1)

            mla_rope(0)
            mla_values(0)
            mla_kT(0)
            mla_step(0)
            with loop(MLA_STEPS - 2, 5) as i:
                mla_step(i + 1)
            mla_softmax(MLA_STEPS - 1)
            mla_out(MLA_STEPS - 1)
            add_rms_y(("wo", 0), 0, 1, T_FFN0)
            rms_r()
            r_rows(rb_ffn, 1, T_FFN0)
            ffn(0)
            add_rms_y(("out", 0), 1, 1, T_PLE0)
            ple(0)

            turn_lo(T_DIL, xt_hi, xt_lo)
            rms_r()
            r_rows(rb_dil, 2, T_DIL)

            def d_qk(u, par, pair):
                dve.wait_ge(chunk_used, C_DIL + 6 * pair + u + 1)
                v.tensor_tensor(dqk[:, par, u], psum[:, u % 2, :].rearrange("p (a t) -> p a t", a=2),
                                rb_dil[:, :].unsqueeze(1).to_broadcast([P, 2, SEQ]), ALU.mult).then_inc(dqk_copied, 1)

            def d_step(pair, par, loads, ahead=True):
                dve.wait_ge(dbias_in[par], 16 * 4 * loads)
                for hh in range(2):
                    bias = dbias[:, par, hh, :]
                    dve.wait_ge(d_scored, 2 * pair + hh + 1)
                    parts = ((slice(0, 3 * P), psum[:, 5, 0:3 * P]),
                             (slice(3 * P, 9 * P), flat[:, 6 * BANK:6 * BANK + 6 * P]))
                    for qb, (part, src) in enumerate(parts):
                        step(v.scalar_tensor_tensor(prob1[:, part], src, HD ** -0.5, bias[:, part], ALU.mult, ALU.add))
                        v.tensor_reduce(nmax[:, qb:qb + 1], prob1[:, part], AX.X, ALU.max, negate=True).then_inc(d_maxed, 1)
                    for qb, (part, src) in enumerate(parts):
                        dve.wait_ge(d_exped, 4 * pair + 2 * hh + qb + 1)
                        step(v.reciprocal(rinv[:, qb:qb + 1], rsum[:, qb:qb + 1]))
                        ins = v.tensor_scalar(prob1[:, part], prob1[:, part], rinv[:, qb:qb + 1], None, ALU.mult)
                    ins.then_inc(d_probs, 1)
                    if ahead:
                        for u in ((0, 1), (2,))[hh]:
                            d_qk(u, 1 - par, pair + 1)
                dve.wait_ge(d_hi, pair + 1)
                sl = bass.ds(pair, 1)
                v.tensor_tensor(ot_lo[:, sl, :].rearrange("p j t -> p (j t)"), psum[:, 2, 0:SEQ],
                                ot_hi[:, sl, :].rearrange("p j t -> p (j t)").bitcast(F32), ALU.subtract).then_inc(d_ready, 1)

            for u in range(NG):
                d_qk(u, 0, 0)
            d_step(0, 0, 1)
            with loop(PAIRS // 2 - 1, 2 * 2 * 4) as i:
                for u in range(2):
                    d_step(1 + u + 2 * i, 1 - u, 1 + u + i)
            d_step(PAIRS - 1, 1, PAIRS // 2, False)
            add_rms_y(("wo", 1), 0, 2, T_FFN1)
            rms_r()
            r_rows(rb_ffn, 3, T_FFN1)
            ffn(1)
            add_rms_y(("out", 1), 1, 2, T_PLE1)
            ple(1)

            for l in (2, 3):
                n = l - 2
                c = C_MIX[l]
                if n == 0:
                    turn_lo(T_MIX2, xt_hi, xt_lo)
                else:
                    norm_after_turn(2)
                dve.wait_ge(ret_copied, 3 * n + 2)
                for part in range(2):
                    qk = ret[:, :, part * RW:(part + 1) * RW].rearrange("p b (h d) -> p b h d", d=HD)
                    shape = [P, TB, RH, HD // 2]
                    size = TB * RH * HD // 2
                    tmp = [t1[:, :, :].rearrange("p b f -> p (b f)")[:, k * size:(k + 1) * size]
                           .rearrange("p (b h d) -> p b h d", b=TB, h=RH) for k in range(4)]
                    ins = rotate(qk[:, :, :, 0:HD // 2], qk[:, :, :, HD // 2:],
                                 rcos[:, :, :].unsqueeze(2).to_broadcast(shape), rsin[:, :, :].unsqueeze(2).to_broadcast(shape), tmp)
                    if part == 0:
                        step(ins)
                ins.then_inc(ret_roped, 1)
                dve.wait_ge(mbias_in, 32 * (n + 1))
                dve.wait_ge(m_scored, n + 1)
                step(v.scalar_tensor_tensor(sc2[:, :, :], logits, HD ** -0.5, mbias[:, :, :], ALU.mult, ALU.add))
                v.tensor_reduce(nmax[:, 0:RH], sc2[:, :, near], AX.X, ALU.max, negate=True)
                v.tensor_reduce(nmax[:, RH:], sc2[:, :, far], AX.X, ALU.max, negate=True).then_inc(m_maxed, 1)
                dve.wait_ge(dec_in, 16 * (n + 1))
                dve.wait_ge(ret_scored, n + 1)
                v.tensor_tensor(dec[:, :, :], logits, dec[:, :, :], ALU.mult).then_inc(ret_decayed, 1)
                dve.wait_ge(m_exped, n + 1)
                step(v.reciprocal(rinv[:, :], rsum[:, :]))
                for part, k, inv in ((near, P, rinv[:, 0:RH]), (far, SEQ, rinv[:, RH:])):
                    ins = v.tensor_tensor(sc2[:, :, part], sc2[:, :, part],
                                          inv.unsqueeze(2).to_broadcast([P, RH, k]), ALU.mult)
                ins.then_inc(m_probs, 1)
                dve.wait_ge(cv_copied, 3 * n + 2)
                prod, acc = cv[:, 0], cv[:, 1]
                step(v.tensor_tensor(prod, cv[:, 0], cv[:, 1], ALU.mult))
                for k, op in ((2, None), (1, 1), (0, 2)):
                    for f in range(2):
                        if op is None:
                            ins = v.tensor_scalar(acc[:, f, :], prod[:, f, :], mconv[:, n, f, k:k + 1], None, ALU.mult)
                        else:
                            ins = v.scalar_tensor_tensor(acc[:, f, op:], prod[:, f, 0:SEQ - op], mconv[:, n, f, k:k + 1],
                                                         acc[:, f, op:], ALU.mult, ALU.add)
                    step(ins)
                dve.wait_ge(ret_summed, n + 1)
                rows = t1[:, :, 0:RW]
                sq = t1[:, :, RW:2 * RW]
                per_head = lambda a: a.rearrange("p b (h d) -> p b h d", d=HD)
                spread = lambda s: s.rearrange("p (b h) -> p b h", b=TB).unsqueeze(3).to_broadcast([P, TB, RH, HD])
                pairs = lambda s: s.rearrange("p (b h) -> p b h", b=TB)
                one = lambda a: a.rearrange("p (h d) -> p h d", d=HD)
                o_rows = [one(psum[:, 2 * tb, 0:RW]) for tb in range(TB)]
                for tb in range(TB):
                    ins = v.tensor_reduce(mean12[:, tb * RH:(tb + 1) * RH], o_rows[tb], AX.X, ALU.add)
                step(ins)
                step(v.tensor_scalar(mean12[:, :], mean12[:, :], 1.0 / HD, None, ALU.mult))
                for tb in range(TB):
                    mean = mean12[:, tb * RH:(tb + 1) * RH].unsqueeze(2).to_broadcast([P, RH, HD])
                    ins = v.tensor_tensor(one(rows[:, tb]), o_rows[tb], mean, ALU.subtract)
                step(ins)
                step(v.tensor_tensor(sq, rows, rows, ALU.mult))
                step(v.tensor_reduce(pairs(var[:, :]), per_head(sq), AX.X, ALU.add))
                step(v.tensor_scalar(var[:, :], var[:, :], 1.0 / HD, LN_EPS, ALU.mult, ALU.add))
                rsqrt(2 * RH)
                step(v.tensor_tensor(per_head(rows), per_head(rows), spread(rstd[:, :]), ALU.mult))
                for tb in range(TB):
                    v.tensor_tensor(rows[:, tb], rows[:, tb], ret[:, tb, 3 * RW:], ALU.mult).then_inc(rows_ready, 1)
                dve.wait_ge(cv_copied, 3 * n + 3)
                step(v.tensor_tensor(acc, acc, cv[:, 2], ALU.mult))
                step(v.tensor_copy(ot_hi[:, 6:8, :], acc))
                v.tensor_tensor(ot_lo[:, 6:8, :], acc, ot_hi[:, 6:8, :].bitcast(F32), ALU.subtract).then_inc(cv_ready, 1)
                dve.wait_ge(m_hi, n + 1)
                v.tensor_tensor(ot_lo[:, 3:6, :].rearrange("p j t -> p (j t)"), flat[:, 4 * BANK:4 * BANK + 3 * SEQ],
                                ot_hi[:, 3:6, :].rearrange("p j t -> p (j t)").bitcast(F32), ALU.subtract).then_inc(m_ready, 1)
                turn_lo((T_RET2, T_RET3)[n], ot_hi, ot_lo)
                layer_norm(("wo", l), T_FFN[l])
                norm_after_turn(1 + 2 * n)
                ffn(l)
                if l == 2:
                    layer_norm(("out", l), T_MIX3)
                else:
                    norm_loaded(6)
                    layer_norm(("out", l))


STAGE_WIDTHS = {name: ws for name, _, ws in STAGES}
HI_WIDTHS = [w for _, n, ws in STAGES for _ in range(n) for w in ws]
for c in range(C_MLA, C_TAIL0):
    if (c - C_MLA) % 3 < 2:
        HI_WIDTHS[c] = W
CONSTS = 7


def bucket_rows():
    d = (2 * P - 1 - np.arange(SPAN)).astype(np.int64)
    rows = np.zeros((BUCKETS + 1, NG + 1, SPAN), np.float32)
    for g in range(NG + 1):
        far = 2048 if g < NG else 128
        if g < NG:
            window, dil = DIL[g]
            valid = (d >= 0) & (d % dil == 0) & (d <= window // dil * dil)
        else:
            valid = d >= 0
        exact = BUCKETS // 2
        n = np.maximum(d, 1).astype(np.float32)
        large = exact + (np.log(n / np.float32(exact)) / np.float32(math.log(far / exact))
                         * np.float32(BUCKETS - exact)).astype(np.int32)
        bucket = np.where(d < exact, np.maximum(d, 0), np.minimum(large, BUCKETS - 1))
        rows[bucket[valid], g, np.nonzero(valid)[0]] = 1.0
        rows[BUCKETS, g, ~valid] = NEG
    return rows


def constants():
    q, k = np.arange(P)[:, None], np.arange(P)[None, :]
    tri = np.where(k <= q, 0.0, NEG).astype(np.float32)
    causal = np.concatenate([tri, np.zeros((P, P), np.float32), tri], axis=1)
    gamma = 1.0 - 2.0 ** (-5.0 - np.arange(RH, dtype=np.float64))
    key, query = np.arange(P)[:, None, None], np.arange(SEQ)[None, None, :]
    far = np.where(query >= key, gamma[None, :, None] ** np.maximum(query - key, 0), 0.0)
    decay = (np.concatenate([far[:, :, 0:P], far], axis=2) * HD ** -0.5).astype(np.float32)
    inv = (np.float32(10000.0) ** (-np.arange(0, HD, 2, dtype=np.float32) / np.float32(HD))).astype(np.float32)
    ang = (np.arange(SEQ, dtype=np.float32)[:, None] * inv[None, :]).astype(np.float32)
    rows = lambda t: np.ascontiguousarray(t.astype(np.float32).reshape(TB, P, HD // 2).transpose(1, 0, 2))
    inv_mla = (np.float32(10000.0) ** (-np.arange(ROPE // 2, dtype=np.float32) / np.float32(ROPE // 2))).astype(np.float32)
    return {
        "causal": causal, "decay": decay, "ret_cos": rows(np.cos(ang)), "ret_sin": rows(np.sin(ang)),
        "inv_freq": np.ascontiguousarray(np.broadcast_to(inv_mla, (P, ROPE // 2))),
        "onehot": bucket_rows(), "identity": np.eye(P, dtype=np.float32),
    }


def tile(w, kts, cols):
    t = w.reshape(-1, P, w.shape[1])[kts.start:kts.stop][:, :, cols]
    return t.transpose(1, 0, 2).reshape(P, -1)


def pad(chunk, width=W):
    full = np.zeros((P, width), chunk.dtype)
    full[:, :chunk.shape[1]] = chunk
    return full


def wide(w):
    return [tile(w, range(k, k + 2), slice(0, D)) for k in range(0, w.shape[0] // P, 2)]


def paired(w, n, left, right, step=P):
    return [tile(w, range(0, KT), np.r_[left + j * step:left + j * step + P, right + j * step:right + j * step + P])
            for j in range(n)]


def by_three(w, cols):
    return [tile(w, r, cols) for r in (range(0, 3), range(3, 6), range(6, 8))]


def pack(a):
    out = {}
    wa = a["mla_w_a"][0]
    out["w_mla_a"] = [[tile(wa, range(0, 4), slice(0, BANK)), tile(wa, range(4, 8), slice(0, BANK)),
                       pad(tile(wa, range(0, KT), slice(BANK, MLA_A)))]]
    uq, ukv = a["mla_w_uq"][0], a["mla_w_ukv"][0].reshape(MLA_KV, 16, NOPE + MLA_V)
    uk = np.ascontiguousarray(ukv[:, :, :NOPE]).reshape(MLA_KV, -1)
    uv = np.ascontiguousarray(ukv[:, :, NOPE:]).reshape(MLA_KV, -1)
    nq, nk = MLA_GROUP * MLA_HD, MLA_GROUP * NOPE
    out["w_mla_heads"] = [[tile(uq, range(0, 3), slice(i * nq, (i + 1) * nq)),
                           tile(uk, range(0, 2), slice(i * nk, (i + 1) * nk)),
                           tile(uv, range(0, 2), slice(i * nk, (i + 1) * nk))] for i in range(MLA_STEPS)]
    threes = lambda chunks: [chunks[i:i + 3] for i in range(0, len(chunks) // 3 * 3, 3)]
    for l, w_o in ((0, a["mla_w_o"][0]), (1, a["dil_w_o"][0])):
        out[f"w_tail{l}"] = threes(wide(w_o) + paired(a["ffn_w_in"][l], FT, 0, D_FF) + wide(a["ffn_w_out"][l])
                                   + wide(a["ple_w_gate"][l]) + wide(a["ple_w_proj"][l]))
    wd = a["dil_w_qkv"][0]
    steps = []
    for i in range(PAIRS):
        at = lambda g, kind: (3 * g + kind) * D + i * P
        vcols = np.concatenate([np.arange(at(g, 2), at(g, 2) + P) for g in range(NG)])
        steps.append([paired(wd, 1, at(g, 0), at(g, 1))[0] for g in range(NG)] + by_three(wd, vcols))
    out["w_dil"] = steps
    for l in (2, 3):
        w = a["w_in_2"][l - 2]
        mq, cb = 4 * RW, 7 * RW
        chunks = [tile(w, range(4 * hf, 4 * hf + 4), slice(b * BANK, (b + 1) * BANK)) for b in range(3) for hf in range(2)]
        chunks += paired(w, 3, mq, mq + RW) + by_three(w, slice(mq + 2 * RW, mq + 3 * RW))
        chunks += [tile(w, range(0, KT), slice(cb + b * 2 * P, cb + (b + 1) * 2 * P)) for b in (1, 2, 0)]
        out[f"w_mix{l}"] = [chunks]
        rest = wide(a["w_out_2"][l - 2])[::-1] + paired(a["w_up_2"][l - 2], FT, 0, D_FF) + wide(a["w_down_2"][l - 2])
        out[f"w_tail{l}"] = threes(rest)
        out[f"w_tail{l}b"] = [rest[len(rest) // 3 * 3:]]
    return {name: np.stack([np.concatenate(it, axis=1) for it in its]) for name, its in out.items()}


def kernel(**inputs):
    import concourse.bacc as bacc
    from concourse.bass_utils import run_bass_kernel_spmd

    a = {name: np.asarray(v) for name, v in inputs.items()}
    feat = lambda g: g.reshape(-1, P).T
    ones = np.ones((P, KT), np.float32)
    norm_g = a["norm_g"]
    c_gain = np.concatenate([feat(a["mla_q_norm"][0]), feat(a["mla_kv_norm"][0]), ones[:, 0:3]], axis=1)
    by_turn = {T_MLA: feat(norm_g[0, 0]), T_MLA_C: c_gain, T_FFN0: feat(norm_g[0, 2]),
               T_DIL: feat(norm_g[1, 0]), T_FFN1: feat(norm_g[1, 2]),
               T_FFN2: feat(a["ln1_g_2"][0]), T_MIX3: feat(a["ln2_g_2"][0]), T_FFN3: feat(a["ln1_g_2"][1])}
    shift = {T_FFN2: feat(a["ln1_b_2"][0]), T_MIX3: feat(a["ln2_b_2"][0]), T_FFN3: feat(a["ln1_b_2"][1])}
    arrays = constants()
    arrays["x"] = a["x"][0]
    arrays["pT"] = np.ascontiguousarray(a["p"][:, 0].transpose(0, 2, 1).reshape(2, 2, P, SEQ).transpose(2, 0, 1, 3))
    arrays["positions"] = np.ascontiguousarray(a["positions"][0].reshape(TB, P).T)
    arrays["gain_fm"] = np.stack([by_turn[t] for t in GAINED + SHIFTED], axis=1)
    arrays["shift_fm"] = np.stack([shift[t] for t in SHIFTED], axis=1)
    arrays["gain_rows"] = np.stack([norm_g[0, 1], norm_g[0, 3], norm_g[1, 1], norm_g[1, 3]] + [
        a[n][l] for l in range(2) for n in ("ln1_g_2", "ln1_b_2", "ln2_g_2", "ln2_b_2")])
    arrays["rel_table"] = a["rel_bias"]
    arrays["rel_table_2"] = a["rel_bias_2"]
    arrays["ffn_conv"] = np.ascontiguousarray(a["ffn_conv_w_2"].reshape(2, 3, FT, P).transpose(3, 0, 2, 1))
    arrays["mix_conv"] = np.ascontiguousarray(a["conv_w_2"].reshape(2, 3, 2, P).transpose(3, 0, 2, 1))
    weights = pack(a)

    nc = bacc.Bacc("TRN2", target_bir_lowering=False, num_devices=1)

    def dram(name, array):
        return nc.dram_tensor(name, list(array.shape), mybir.dt.from_np(array.dtype), kind="ExternalInput").ap()

    aps = {name: dram(name, v) for name, v in arrays.items()}
    streams = {name: dram(name, v) for name, v in weights.items()}
    out = nc.dram_tensor("out", [SEQ, D], F32, kind="ExternalOutput").ap()
    build(nc, weights=streams, out=out, **aps)
    got = run_bass_kernel_spmd(nc, [{**arrays, **weights}], core_ids=[0])
    return got.results[0]["out"].reshape(1, SEQ, D)
```
